# Optimizing a Trainium2 kernel written in Bass

```python
import jax, jax.numpy as jnp
from jax import lax
import numpy as np

D_MODEL = 1024
BATCH = 1
SEQ = 512
DEPTH = 2

GRID_W = 64
CTX_LEN = 256
HEAD_DIM = 64
NA_HEADS = 8
NA_WIN_H = 8
NA_WIN_W = 16
GQA_Q_HEADS = 8
GQA_KV_HEADS = 2
GQA_REP = GQA_Q_HEADS // GQA_KV_HEADS
NA_WIDTH = NA_HEADS * HEAD_DIM
GQA_Q_WIDTH = GQA_Q_HEADS * HEAD_DIM
GQA_KV_WIDTH = GQA_KV_HEADS * HEAD_DIM
IN_SIZES = (NA_WIDTH, NA_WIDTH, NA_WIDTH, GQA_Q_WIDTH, GQA_KV_WIDTH, GQA_KV_WIDTH, D_MODEL, D_MODEL)
IN_COLS = sum(IN_SIZES)
IN_SPLITS = tuple(int(v) for v in np.cumsum(IN_SIZES)[:-1])
D_FF = -(-(8 * D_MODEL) // (3 * 256)) * 256
Q_BLOCK = 128
ROPE_THETA = 10000.0
EPS = 1e-6
SCALE = HEAD_DIM ** -0.5


def rms_norm(x, g):
    xf = x.astype(jnp.float32)
    y = xf * lax.rsqrt(jnp.mean(xf * xf, axis=-1, keepdims=True) + EPS)
    return (y * g.astype(jnp.float32)).astype(x.dtype)

def modulate(h, shift, scale):
    return h * (1 + scale) + shift

def heads(t, n_heads):
    b, n, _ = t.shape
    return t.reshape(b, n, n_heads, HEAD_DIM).transpose(0, 2, 1, 3)

def merge_heads(t):
    b, h, n, d = t.shape
    return t.transpose(0, 2, 1, 3).reshape(b, n, h * d)

def axial_rope_tables(n_tokens):
    t = jnp.arange(n_tokens)
    row = (t // GRID_W).astype(jnp.float32)
    col = (t % GRID_W).astype(jnp.float32)
    half = HEAD_DIM // 2
    inv = ROPE_THETA ** (-jnp.arange(0, half, 2, dtype=jnp.float32) / half)
    ang = jnp.concatenate([row[:, None] * inv, col[:, None] * inv], axis=-1)
    return jnp.cos(ang), jnp.sin(ang)

def apply_rope(x, cos, sin):
    xf = x.astype(jnp.float32).reshape(x.shape[:-1] + (HEAD_DIM // 2, 2))
    x0, x1 = xf[..., 0], xf[..., 1]
    out = jnp.stack([x0 * cos - x1 * sin, x0 * sin + x1 * cos], axis=-1)
    return out.reshape(x.shape).astype(x.dtype)

def na_window_indices(rows):
    kh = min(NA_WIN_H, rows)
    r = jnp.arange(rows)
    col = jnp.arange(GRID_W)
    r_start = jnp.clip(r - kh // 2, 0, rows - kh)
    row_idx = r_start[:, None] + jnp.arange(kh)[None, :]
    c_start = jnp.clip(col - NA_WIN_W // 2, 0, GRID_W - NA_WIN_W)
    in_win = (col[None, :] >= c_start[:, None]) & (col[None, :] < c_start[:, None] + NA_WIN_W)
    dr_idx = row_idx - r[:, None] + (NA_WIN_H - 1)
    dc = col[None, :] - col[:, None]
    dc_idx = jnp.clip(dc, -(NA_WIN_W - 1), NA_WIN_W - 1) + (NA_WIN_W - 1)
    return row_idx, in_win, dr_idx, dc_idx

def na_bias(rpb, in_win, dr_idx, dc_idx):
    b = rpb.astype(jnp.float32)[:, dr_idx[:, None, :, None], dc_idx[None, :, None, :]]
    return jnp.where(in_win[None, None, :, None, :], b, -jnp.inf)

def na_latent(q, k, v, k_ctx, v_ctx, bias, row_idx):
    b, h, s, d = q.shape
    rows = s // GRID_W
    kh = row_idx.shape[1]
    qg = q.reshape(b, h, rows, GRID_W, d)
    kg = k.reshape(b, h, rows, GRID_W, d)[:, :, row_idx]
    vg = v.reshape(b, h, rows, GRID_W, d)[:, :, row_idx]
    s_win = jnp.einsum('bhrwd,bhrjud->bhrwju', qg, kg).astype(jnp.float32) * SCALE + bias[None]
    s_win = s_win.reshape(b, h, rows, GRID_W, kh * GRID_W)
    s_ctx = jnp.einsum('bhrwd,bhld->bhrwl', qg, k_ctx).astype(jnp.float32) * SCALE
    p = jax.nn.softmax(jnp.concatenate([s_win, s_ctx], axis=-1), axis=-1).astype(v.dtype)
    p_win = p[..., :kh * GRID_W].reshape(b, h, rows, GRID_W, kh, GRID_W)
    p_ctx = p[..., kh * GRID_W:]
    o = jnp.einsum('bhrwju,bhrjud->bhrwd', p_win, vg) + jnp.einsum('bhrwl,bhld->bhrwd', p_ctx, v_ctx)
    return o.reshape(b, h, s, d)

def softmax_attn(q, k, v):
    s = jnp.einsum('bgrqd,bgkd->bgrqk', q, k).astype(jnp.float32) * SCALE
    p = jax.nn.softmax(s, axis=-1).astype(v.dtype)
    return jnp.einsum('bgrqk,bgkd->bgrqd', p, v)

def gqa_latent(q, k_all, v_all):
    b, g, r, s, d = q.shape
    nb = s // Q_BLOCK
    qb = q.reshape(b, g, r, nb, Q_BLOCK, d).transpose(3, 0, 1, 2, 4, 5)
    o = lax.map(lambda qblk: softmax_attn(qblk, k_all, v_all), qb)
    return o.transpose(1, 2, 3, 0, 4, 5).reshape(b, g, r, s, d)

def branch_merge(ya, yb, ga, gb, w_pa, w_pb, w_o):
    merged = jax.nn.sigmoid(ga) * (ya @ w_pa) + jax.nn.sigmoid(gb) * (yb @ w_pb)
    return merged @ w_o

def swiglu(h, w_in, w_out):
    a, u = jnp.split(h @ w_in, 2, axis=-1)
    return (jax.nn.silu(a) * u) @ w_out

def first_inputs(seed: int = 0) -> dict:
    key = jax.random.key(seed)
    ks = jax.random.split(key, 18)
    f32 = jnp.float32
    nrm = lambda k, shp, sc: jax.random.normal(k, shp, f32) * sc
    return {
        "x": nrm(ks[0], (BATCH, SEQ, D_MODEL), 1.0),
        "c": nrm(ks[1], (BATCH, D_MODEL), 1.0),
        "ctx": nrm(ks[2], (BATCH, CTX_LEN, D_MODEL), 1.0),
        "c_ctx": nrm(ks[3], (D_MODEL,), 1.0),
        "w_mod": nrm(ks[4], (DEPTH, D_MODEL, 6 * D_MODEL), D_MODEL ** -0.5),
        "b_mod": nrm(ks[5], (DEPTH, 6 * D_MODEL), 0.01),
        "norm1": 1.0 + nrm(ks[6], (DEPTH, D_MODEL), 0.02),
        "w_in": nrm(ks[7], (DEPTH, D_MODEL, IN_COLS), D_MODEL ** -0.5),
        "na_rpb": nrm(ks[8], (DEPTH, NA_HEADS, 2 * NA_WIN_H - 1, 2 * NA_WIN_W - 1), 0.1),
        "q_gain": 1.0 + nrm(ks[9], (DEPTH, HEAD_DIM), 0.02),
        "k_gain": 1.0 + nrm(ks[10], (DEPTH, HEAD_DIM), 0.02),
        "w_pa": nrm(ks[11], (DEPTH, NA_WIDTH, D_MODEL), NA_WIDTH ** -0.5),
        "w_pb": nrm(ks[12], (DEPTH, GQA_Q_WIDTH, D_MODEL), GQA_Q_WIDTH ** -0.5),
        "w_o": nrm(ks[13], (DEPTH, D_MODEL, D_MODEL), D_MODEL ** -0.5),
        "norm2": 1.0 + nrm(ks[14], (DEPTH, D_MODEL), 0.02),
        "w_ffn_in": nrm(ks[15], (DEPTH, D_MODEL, 2 * D_FF), D_MODEL ** -0.5),
        "w_ffn_out": nrm(ks[16], (DEPTH, D_FF, D_MODEL), D_FF ** -0.5),
        "final_norm": 1.0 + nrm(ks[17], (D_MODEL,), 0.02),
    }

def first_block(x, c, ctx, c_ctx, w_mod, b_mod, norm1, w_in, na_rpb, q_gain, k_gain, w_pa, w_pb, w_o,
              norm2, w_ffn_in, w_ffn_out, final_norm):
    b, s, _ = x.shape
    n_ctx = ctx.shape[1]
    rows = s // GRID_W
    cos, sin = axial_rope_tables(s)
    row_idx, in_win, dr_idx, dc_idx = na_window_indices(rows)
    silu_c = jax.nn.silu(c)
    silu_cc = jax.nn.silu(c_ctx)

    for l in range(DEPTH):
        last = l == DEPTH - 1
        mod = silu_c @ w_mod[l] + b_mod[l]
        mod_c = silu_cc @ w_mod[l] + b_mod[l]
        sh1, sc1, g1, sh2, sc2, g2 = jnp.split(mod[:, None, :], 6, axis=-1)
        csh1, csc1, cg1, csh2, csc2, cg2 = jnp.split(mod_c, 6)

        h = modulate(rms_norm(x, norm1[l]), sh1, sc1)
        hc = modulate(rms_norm(ctx, norm1[l]), csh1, csc1)
        na_q, na_k, na_v, gq, gk, gv, ga, gb = jnp.split(h @ w_in[l], IN_SPLITS, axis=-1)
        na_qc, na_kc, na_vc, gqc, gkc, gvc, gac, gbc = jnp.split(hc @ w_in[l], IN_SPLITS, axis=-1)

        qa, ka, va = heads(na_q, NA_HEADS), heads(na_k, NA_HEADS), heads(na_v, NA_HEADS)
        qa_c, ka_c, va_c = heads(na_qc, NA_HEADS), heads(na_kc, NA_HEADS), heads(na_vc, NA_HEADS)
        bias = na_bias(na_rpb[l], in_win, dr_idx, dc_idx)
        ya = merge_heads(na_latent(qa, ka, va, ka_c, va_c, bias, row_idx))

        qb = apply_rope(rms_norm(heads(gq, GQA_Q_HEADS), q_gain[l]), cos, sin)
        kb = apply_rope(rms_norm(heads(gk, GQA_KV_HEADS), k_gain[l]), cos, sin)
        vb = heads(gv, GQA_KV_HEADS)
        qb_c = rms_norm(heads(gqc, GQA_Q_HEADS), q_gain[l])
        kb_c = rms_norm(heads(gkc, GQA_KV_HEADS), k_gain[l])
        vb_c = heads(gvc, GQA_KV_HEADS)
        k_all = jnp.concatenate([kb, kb_c], axis=2)
        v_all = jnp.concatenate([vb, vb_c], axis=2)
        ob = gqa_latent(qb.reshape(b, GQA_KV_HEADS, GQA_REP, s, HEAD_DIM), k_all, v_all)
        yb = merge_heads(ob.reshape(b, GQA_Q_HEADS, s, HEAD_DIM))

        x = x + g1 * branch_merge(ya, yb, ga, gb, w_pa[l], w_pb[l], w_o[l])

        if not last:
            ya_c = merge_heads(softmax_attn(qa_c[:, :, None], ka_c, va_c)[:, :, 0])
            ob_c = softmax_attn(qb_c.reshape(b, GQA_KV_HEADS, GQA_REP, n_ctx, HEAD_DIM), kb_c, vb_c)
            yb_c = merge_heads(ob_c.reshape(b, GQA_Q_HEADS, n_ctx, HEAD_DIM))
            ctx = ctx + cg1 * branch_merge(ya_c, yb_c, gac, gbc, w_pa[l], w_pb[l], w_o[l])

        h2 = modulate(rms_norm(x, norm2[l]), sh2, sc2)
        x = x + g2 * swiglu(h2, w_ffn_in[l], w_ffn_out[l])
        if not last:
            hc2 = modulate(rms_norm(ctx, norm2[l]), csh2, csc2)
            ctx = ctx + cg2 * swiglu(hc2, w_ffn_in[l], w_ffn_out[l])

    return rms_norm(x, final_norm)


DEPTH_2 = 1

CHUNK = 64
PLE_DIM = 256
D_MIX = D_MODEL
D_CONV = D_MIX // 2
D_LRU = D_MIX - D_CONV
CONV_HEADS = 8
LRU_HEADS = 8
LRU_HEAD_DIM = D_LRU // LRU_HEADS
CONV_WIDTH = 31
LRU_CONV_WIDTH = 4
LRU_C = 8.0
N_GROUPS = 4
EXPERTS_PER_GROUP = 8
N_EXPERTS = N_GROUPS * EXPERTS_PER_GROUP
TOP_K = 2
D_EXPERT = D_MODEL // 2
ROUTE_BLOCK = 128


def _rmsnorm(x, g):
    xf = x.astype(jnp.float32)
    y = xf * lax.rsqrt(jnp.mean(xf * xf, axis=-1, keepdims=True) + EPS)
    return (y * g.astype(jnp.float32)).astype(x.dtype)

def _layernorm(x, g, b):
    xf = x.astype(jnp.float32)
    mu = jnp.mean(xf, axis=-1, keepdims=True)
    var = jnp.mean(jnp.square(xf - mu), axis=-1, keepdims=True)
    y = (xf - mu) * lax.rsqrt(var + EPS)
    return (y * g.astype(jnp.float32) + b.astype(jnp.float32)).astype(x.dtype)

def _causal_depthwise_conv(x, w, b):
    width = w.shape[0]
    y = lax.conv_general_dilated(
        x, w[:, None, :], window_strides=(1,), padding=((width - 1, 0),),
        dimension_numbers=('NWC', 'WIO', 'NWC'), feature_group_count=x.shape[-1])
    return y + b

def _conformer_conv(v, g, w_dw, b_dw, ln_g, ln_b):
    u = v * jax.nn.sigmoid(g)
    u = _causal_depthwise_conv(u, w_dw, b_dw)
    return jax.nn.silu(_layernorm(u, ln_g, ln_b))

def _rglru(x, w_r, b_r, w_i, b_i, lam):
    B, S, C = x.shape
    xh = x.reshape(B, S, LRU_HEADS, LRU_HEAD_DIM)
    r = jax.nn.sigmoid(jnp.einsum('bshi,hij->bshj', xh, w_r).reshape(B, S, C) + b_r)
    i_g = jax.nn.sigmoid(jnp.einsum('bshi,hij->bshj', xh, w_i).reshape(B, S, C) + b_i)
    log_a = -LRU_C * r.astype(jnp.float32) * jax.nn.softplus(-lam.astype(jnp.float32))
    a = jnp.exp(log_a)
    u = jnp.sqrt(-jnp.expm1(2.0 * log_a)) * (i_g * x).astype(jnp.float32)
    nc = S // CHUNK
    a_c = a.reshape(B, nc, CHUNK, C)
    u_c = u.reshape(B, nc, CHUNK, C)

    def combine(left, right):
        a_l, h_l = left
        a_r, h_r = right
        return a_l * a_r, a_r * h_l + h_r

    a_cum, h_loc = lax.associative_scan(combine, (a_c, u_c), axis=2)

    def step(h_prev, xs):
        ac, hl = xs
        h = hl + ac * h_prev[:, None, :]
        return h[:, -1, :], h

    _, h = lax.scan(step, jnp.zeros((B, C), jnp.float32),
                    (jnp.moveaxis(a_cum, 1, 0), jnp.moveaxis(h_loc, 1, 0)))
    return jnp.moveaxis(h, 0, 1).reshape(B, S, C).astype(x.dtype)

def _hier_route(h, w_group, b_group, w_expert, b_expert):
    T = h.shape[0]
    g_logits = (h @ w_group).astype(jnp.float32) + b_group.astype(jnp.float32)
    g_prob, g_idx = lax.top_k(jax.nn.softmax(g_logits, axis=-1), 1)
    e_logits = ((h @ w_expert).astype(jnp.float32) + b_expert.astype(jnp.float32))
    e_logits = e_logits.reshape(T, N_GROUPS, EXPERTS_PER_GROUP)
    e_sel = jnp.take_along_axis(e_logits, g_idx[:, :, None], axis=1)[:, 0]
    e_prob, e_loc = lax.top_k(jax.nn.softmax(e_sel, axis=-1), TOP_K)
    e_prob = e_prob / jnp.sum(e_prob, axis=-1, keepdims=True)
    gate = g_prob * e_prob
    expert_id = g_idx * EXPERTS_PER_GROUP + e_loc
    return expert_id, gate

def _routed_experts(h, expert_id, gate, w1, w3, w2):
    T, D = h.shape
    A = T * TOP_K
    flat_e = expert_id.reshape(A)
    flat_tok = jnp.repeat(jnp.arange(T, dtype=jnp.int32), TOP_K, total_repeat_length=A)
    flat_gate = gate.reshape(A)
    order = jnp.argsort(flat_e)
    se, st, sg = flat_e[order], flat_tok[order], flat_gate[order]
    counts = jnp.zeros((N_EXPERTS,), jnp.int32).at[flat_e].add(1)
    padded = (counts + ROUTE_BLOCK - 1) // ROUTE_BLOCK * ROUTE_BLOCK
    start = jnp.cumsum(counts) - counts
    pad_end = jnp.cumsum(padded)
    pad_start = pad_end - padded
    dest = pad_start[se] + (jnp.arange(A, dtype=jnp.int32) - start[se])
    n_blocks = -(-A // ROUTE_BLOCK) + N_EXPERTS
    P = n_blocks * ROUTE_BLOCK
    buf_tok = jnp.zeros((P,), jnp.int32).at[dest].set(st)
    buf_gate = jnp.zeros((P,), jnp.float32).at[dest].set(sg)
    block_start = jnp.arange(n_blocks, dtype=jnp.int32) * ROUTE_BLOCK
    block_e = jnp.minimum(jnp.searchsorted(pad_end, block_start, side='right'), N_EXPERTS - 1)

    def expert_block(args):
        tok, e, g = args
        xb = h[tok]
        y = (jax.nn.silu(xb @ w1[e]) * (xb @ w3[e])) @ w2[e]
        return (y * g[:, None]).astype(h.dtype)

    y = lax.map(expert_block, (buf_tok.reshape(n_blocks, ROUTE_BLOCK), block_e,
                               buf_gate.reshape(n_blocks, ROUTE_BLOCK)))
    return jnp.zeros_like(h).at[buf_tok].add(y.reshape(P, D))

def second_inputs(seed: int = 0) -> dict:
    key = jax.random.key(seed)
    ks = jax.random.split(key, 32)
    f32 = jnp.float32
    L = DEPTH_2

    def nrm(k, shape, scale):
        return jax.random.normal(k, shape, f32) * scale

    def gain(k, shape):
        return 1.0 + 0.05 * jax.random.normal(k, shape, f32)

    u = jax.random.uniform(ks[14], (L, D_LRU), f32, 0.9, 0.999)
    s = u ** (1.0 / LRU_C)
    lru_lambda = jnp.log(s) - jnp.log1p(-s)
    return {
        'x': nrm(ks[0], (BATCH, SEQ, D_MODEL), 1.0),
        'p': nrm(ks[1], (L, BATCH, SEQ, PLE_DIM), 1.0),
        'g_mix': gain(ks[2], (L, D_MODEL)),
        'w_in': nrm(ks[3], (L, D_MODEL, 2 * D_CONV + 2 * D_LRU), D_MODEL ** -0.5),
        'conv_dw_w': nrm(ks[4], (L, CONV_WIDTH, D_CONV), CONV_WIDTH ** -0.5),
        'conv_dw_b': nrm(ks[5], (L, D_CONV), 0.02),
        'conv_ln_g': gain(ks[6], (L, D_CONV)),
        'conv_ln_b': nrm(ks[7], (L, D_CONV), 0.02),
        'lru_conv_w': nrm(ks[8], (L, LRU_CONV_WIDTH, D_LRU), LRU_CONV_WIDTH ** -0.5),
        'lru_conv_b': nrm(ks[9], (L, D_LRU), 0.02),
        'lru_w_r': nrm(ks[10], (L, LRU_HEADS, LRU_HEAD_DIM, LRU_HEAD_DIM), LRU_HEAD_DIM ** -0.5),
        'lru_b_r': nrm(ks[11], (L, D_LRU), 0.02),
        'lru_w_i': nrm(ks[12], (L, LRU_HEADS, LRU_HEAD_DIM, LRU_HEAD_DIM), LRU_HEAD_DIM ** -0.5),
        'lru_b_i': nrm(ks[13], (L, D_LRU), 0.02),
        'lru_lambda': lru_lambda,
        'w_out': nrm(ks[15], (L, D_MIX, D_MODEL), D_MIX ** -0.5),
        'g_ffn': gain(ks[16], (L, D_MODEL)),
        'w_group': nrm(ks[17], (L, D_MODEL, N_GROUPS), D_MODEL ** -0.5),
        'b_group': nrm(ks[18], (L, N_GROUPS), 0.01),
        'w_expert': nrm(ks[19], (L, D_MODEL, N_EXPERTS), D_MODEL ** -0.5),
        'b_expert': nrm(ks[20], (L, N_EXPERTS), 0.01),
        'w1': nrm(ks[21], (L, N_EXPERTS, D_MODEL, D_EXPERT), D_MODEL ** -0.5),
        'w3': nrm(ks[22], (L, N_EXPERTS, D_MODEL, D_EXPERT), D_MODEL ** -0.5),
        'w2': nrm(ks[23], (L, N_EXPERTS, D_EXPERT, D_MODEL), D_EXPERT ** -0.5),
        'g_ple': gain(ks[24], (L, D_MODEL)),
        'w_ple': nrm(ks[25], (L, PLE_DIM, D_MODEL), PLE_DIM ** -0.5),
        'g_ple_proj': gain(ks[26], (L, D_MODEL)),
        'w_ple_gate': nrm(ks[27], (L, D_MODEL, D_MODEL), D_MODEL ** -0.5),
        'g_final': gain(ks[28], (D_MODEL,)),
    }

def second_block(x, p, g_mix, w_in, conv_dw_w, conv_dw_b, conv_ln_g, conv_ln_b,
              lru_conv_w, lru_conv_b, lru_w_r, lru_b_r, lru_w_i, lru_b_i, lru_lambda,
              w_out, g_ffn, w_group, b_group, w_expert, b_expert, w1, w3, w2,
              g_ple, w_ple, g_ple_proj, w_ple_gate, g_final):
    B, S, D = x.shape
    for i in range(DEPTH_2):
        h = _rmsnorm(x, g_mix[i])
        z = h @ w_in[i]
        conv_v, conv_g, lru_x, lru_g = jnp.split(
            z, [D_CONV, 2 * D_CONV, 2 * D_CONV + D_LRU], axis=-1)
        y_conv = _conformer_conv(conv_v, conv_g, conv_dw_w[i], conv_dw_b[i],
                                 conv_ln_g[i], conv_ln_b[i])
        xr = _causal_depthwise_conv(lru_x, lru_conv_w[i], lru_conv_b[i])
        y_lru = _rglru(xr, lru_w_r[i], lru_b_r[i], lru_w_i[i], lru_b_i[i],
                       lru_lambda[i]) * jax.nn.gelu(lru_g)
        x = x + jnp.concatenate([y_conv, y_lru], axis=-1) @ w_out[i]
        hf = _rmsnorm(x, g_ffn[i]).reshape(B * S, D)
        eid, gate = _hier_route(hf, w_group[i], b_group[i], w_expert[i], b_expert[i])
        x = x + _routed_experts(hf, eid, gate, w1[i], w3[i], w2[i]).reshape(B, S, D)
        e = _rmsnorm(p[i] @ w_ple[i], g_ple_proj[i])
        pg = jax.nn.sigmoid(_rmsnorm(x, g_ple[i]) @ w_ple_gate[i])
        x = x + pg * e
    return _rmsnorm(x, g_final)


def setup_inputs(seed=0):
    out = dict(first_inputs(seed))
    for name, value in second_inputs(seed + 1).items():
        if name != "x":
            out[name + "_2"] = value
    return out


def reference(
    x, c, ctx, c_ctx, w_mod, b_mod, norm1, w_in, na_rpb, q_gain, k_gain, w_pa, w_pb, w_o, norm2,
    w_ffn_in, w_ffn_out, final_norm, p_2, g_mix_2, w_in_2, conv_dw_w_2, conv_dw_b_2,
    conv_ln_g_2, conv_ln_b_2, lru_conv_w_2, lru_conv_b_2, lru_w_r_2, lru_b_r_2, lru_w_i_2,
    lru_b_i_2, lru_lambda_2, w_out_2, g_ffn_2, w_group_2, b_group_2, w_expert_2, b_expert_2,
    w1_2, w3_2, w2_2, g_ple_2, w_ple_2, g_ple_proj_2, w_ple_gate_2, g_final_2,
):
    x = first_block(
        x, c, ctx, c_ctx, w_mod, b_mod, norm1, w_in, na_rpb, q_gain, k_gain, w_pa, w_pb, w_o,
        norm2, w_ffn_in, w_ffn_out, final_norm,
    )
    return second_block(
        x, p_2, g_mix_2, w_in_2, conv_dw_w_2, conv_dw_b_2, conv_ln_g_2, conv_ln_b_2,
        lru_conv_w_2, lru_conv_b_2, lru_w_r_2, lru_b_r_2, lru_w_i_2, lru_b_i_2, lru_lambda_2,
        w_out_2, g_ffn_2, w_group_2, b_group_2, w_expert_2, b_expert_2, w1_2, w3_2, w2_2,
        g_ple_2, w_ple_2, g_ple_proj_2, w_ple_gate_2, g_final_2,
    )


_drawn_inputs = setup_inputs


def setup_inputs(seed=0):
    import zlib

    import numpy as np

    out = dict(_drawn_inputs(seed))
    spreads = {}
    factors = {'norm1': 4.526,
     'na_rpb': 4.149,
     'q_gain': 8.0,
     'k_gain': 8.0,
     'conv_dw_b_2': 2.967,
     'conv_ln_b_2': 3.854,
     'lru_b_r_2': 8.0,
     'lru_b_i_2': 13.361,
     'b_group_2': 4.986,
     'b_expert_2': 5.378,
     'g_ple_2': 7.754,
     'g_ple_proj_2': 2.884}
    for name, (base, spread) in spreads.items():
        noise = np.random.default_rng([zlib.crc32(name.encode()), seed]).standard_normal(out[name].shape)
        drawn = base * np.exp(spread * noise) if base else spread * noise
        out[name] = __import__('jax').numpy.asarray(drawn.astype(out[name].dtype))
    for name, factor in factors.items():
        out[name] = (out[name] * factor).astype(out[name].dtype)
    return out
```

```python
import concourse.bass as bass
from concourse import mybir
from contextlib import ExitStack
import numpy as np

P = 128
D = 1024
KD = D // P
NL, NC = 512, 256
T = NL + NC
LAYERS = 2
FF = 2816
KF = FF // P
HD = 64
GRID = 64
EPS = 1e-6
QSCALE = HD ** -0.5

RING = 4
SLOT = KD * 256
FFQ = [(0, 6), (6, 12), (12, 18), (18, 22)]


def layer_slots(l):
    first = [("mod_head", 8)] if l == 0 else []
    return first + [("gq", 2), ("gkv", 1), ("nak", 2), ("naq", 2), ("nav", 2),
                    ("mod_rest", 24 if l == 0 else 16),
                    ("merge", 16), ("w_o", 4), ("ffn_in", KF), ("ffn_out", 16)]


SLOT0 = {}
_n = 0
for _l in range(LAYERS):
    for _name, _count in layer_slots(_l):
        SLOT0[_l, _name] = _n
        _n += _count
BLOCK1_SLOTS = _n
for _name, _count in [("w_in2", 8), ("w_out2", 4)]:
    SLOT0[2, _name] = _n
    _n += _count
N_STREAM = _n

EVACUATES = ""
for _l in range(LAYERS):
    for _name, _count in layer_slots(_l):
        EVACUATES += {"mod_head": "--", "mod_rest": "--", "gq": "AA", "gkv": "AA", "nak": "AA", "naq": "AA",
                      "nav": "AA", "merge": "AAVVAAVV", "w_o": "VV", "ffn_in": "AV",
                      "ffn_out": "------VV"}[_name] * (_count // (4 if _name in ("merge", "ffn_out") else 1))
EVACUATES += "AV" * 4 + "AA" * 4 + "VV" * 4


def evacuated(who, s):
    return EVACUATES[:s + 1].count(who)


def previous_user(s):
    for q in range(s - 2, -1, -2):
        if EVACUATES[q] != "-":
            return EVACUATES[q], evacuated(EVACUATES[q], q)
    return None


VEC = {}
_v = 0


def _vec(name, n):
    global _v
    VEC[name] = _v
    _v += n


_vec("c2", 16)
for _l in range(LAYERS):
    for _name, _count in [("norm1", 8), ("norm2", 8), ("b_mod", 48), ("q_gain", 1), ("k_gain", 1)]:
        _vec(f"{_name}{_l}", _count)
_vec("final_norm", 8)
for _name, _count in [("g_mix", 8), ("conv_w", 124), ("conv_b", 4), ("ln_g", 4), ("ln_b", 4), ("lru_w", 16),
                      ("lru_b", 4), ("b_r", 4), ("b_i", 4), ("lam", 4), ("g_ffn", 8), ("g_ple", 8),
                      ("g_proj", 8), ("g_final", 8)]:
    _vec(_name, _count)
NV = _v

CST = {"ident": 0, "ones": 128, "blk": 256, "rot": 384, "cos": 512, "sin": 1024, "namask": 1536, "iota": 1600,
       "tri": 1664, "one": 1792, "eidx": 1920, "fold": 1956}
NCST = 1956 + 2


def attention_units(l):
    return [(na, t, qb, half) for na in (True, False) for t in range(4)
            for qb in range(6 if l == 0 else 4) for half in range(2)]


TAPS, LTAPS = 31, 4
PE_CONV = (2, 3)
NG4, NE = 4, 32
CAP = 64
PAIRS = NE // 2
NR = NG4 + NE


def build(nc, stream, vecs, consts, xT, ctxT, rpb, experts, router, router_b, lru_w, w_ple, pT, w_gate, out):
    fp32 = mybir.dt.float32
    ALU = mybir.AluOpType
    ACT = mybir.ActivationFunctionType
    AX = mybir.AxisListType
    ds = bass.ds

    es = ExitStack()
    with es:
        def sb(name, shape):
            return es.enter_context(nc.sbuf_tensor(name, shape, fp32))

        def sem(name):
            return es.enter_context(nc.semaphore(name))

        rows = nc.dram_tensor("bias_rows", (LAYERS * 120, GRID, 128), fp32, kind="Internal").ap()
        rows_in = sem("bias_rows_copied")
        ring = sb("ring", [P, RING, SLOT])
        X = sb("X", [P, KD, T])
        H = sb("H", [P, KD, T])
        UW = sb("UW", [P, 28160])
        U, W = UW[:, 0:19968], UW[:, 19968:28160]
        gate = sb("gate", [P, 4, NE])
        pos = sb("pos", [P, 4, NE])
        total_i = nc.sbuf_tensor("total_i", [P, 1], mybir.dt.int32)
        total_i = es.enter_context(total_i)
        lam8 = sb("lam8", [P, 8, 4])
        vec = sb("vec", [P, NV])
        cst = sb("cst", [P, NCST])
        sc2 = sb("sc2", [P, KD, 32])
        mrow = sb("mod_rows", [P, 256])
        mod = sb("mod", [P, LAYERS * 48, 2])
        amod = sb("amod", [P, LAYERS * 2, KD, 2])
        inv = sb("inverse_sums", [P, 2, P])
        small = sb("small", [P, 4, 8])
        qg8 = sb("qg8", [P, LAYERS])
        epsc = sb("epsc", [P, 1])

        def view(t, at, *shape):
            n = int(np.prod(shape))
            ap = t[:, at:at + n]
            return ap.rearrange("p (a b) -> p a b", b=shape[-1]) if len(shape) == 2 else ap

        KNA, QNA, QG = (view(U, i * 3072, 4, T) for i in range(3))
        KG = view(U, 9216, 1, T)
        V = view(U, 9984, 6, 640)
        Y = view(U, 13824, 8, T)
        M = view(U, 0, 8, T)
        G = view(U, 0, KF, T)
        PB = view(W, 0, 3, T)
        PT = view(W, 3 * T, 3, T)
        BIAS = view(W, 4608, 4, 14 * GRID)
        RAW, SQ, RS, NG, CG = (view(W, i * 1536, 2, T) for i in range(5))

        ps = [es.enter_context(nc.psum_tensor(f"ps{i}", [P, 1024], fp32)) for i in range(4)]

        ident = cst[:, 0:128]
        onesm = cst[:, CST["ones"]:CST["ones"] + P]
        ones1 = cst[:, CST["one"]:CST["one"] + P]
        tri = cst[:, CST["tri"]:CST["tri"] + P]
        blk = cst[:, CST["blk"]:CST["blk"] + P]
        rot = cst[:, CST["rot"]:CST["rot"] + P]
        cosT = cst[:, CST["cos"]:CST["cos"] + NL]
        sinT = cst[:, CST["sin"]:CST["sin"] + NL]
        fold = cst[:, CST["fold"]:CST["fold"] + 2]
        namask = cst[:, CST["namask"]:CST["namask"] + GRID]

        def vcol(name, i=0, n=1):
            return vec[:, VEC[name] + i:VEC[name] + i + n]

        loaded = [sem(f"slot{r}_loaded") for r in range(RING)]
        steps = sem("steps_done")
        evac = {"A": sem("scalar_evacuated"), "V": sem("vector_evacuated")}
        inputs = sem("inputs_loaded")
        x_loaded = sem("x_loaded")
        silu_done = sem("silu_done")
        mod_ready = sem("mod_ready")
        x_upd = sem("x_updated")
        squared = sem("squared")
        summed = sem("squares_summed")
        sum_spread = sem("sum_spread")
        rooted = sem("rms_rooted")
        rstd_ok = sem("rstd_ready")
        normed = sem("x_times_rstd")
        h_ready = sem("h_ready")
        g_sq = sem("head_squares")
        g_ms = sem("head_mean_square")
        g_rt = sem("head_rooted")
        g_rr = sem("head_rstd")
        g_n = sem("head_normed")
        g_rot = sem("head_rotated")
        g_cos = sem("head_cos")
        g_sin = sem("head_sin")
        g_q = sem("head_roped")
        bias_in = [sem(f"bias_in{i}") for i in range(4)]
        bias_ok = sem("bias_ready")
        s_sc, s_m1, s_m2 = sem("scores_done"), sem("window_max"), sem("context_max")
        s_mx = sem("max_ready")
        s_exp, s_tr, s_pta, s_ptb = sem("exp_done"), sem("turned"), sem("turned_kept_a"), sem("turned_kept_b")
        s_pv, s_ri, s_dg, s_y = sem("pv_done"), sem("rowsum_inverse"), sem("inverse_diagonal"), sem("y_kept")
        mod_kept, mod_turned, sc_zero = sem("mod_rows_kept"), sem("mod_turned"), sem("c_zeroed")
        merged = sem("merged_ready")
        mod_sum = sem("mod_summed")
        small_q = sem("query_gain_ready")
        small_ok = sem("small_ready")
        xo = sem("x_out")

        UC = view(UW, 0, 4, TAPS - 1 + NL)
        XL = view(UW, 2176, 4, LTAPS - 1 + NL)
        GL = view(UW, 4240, 4, NL)
        CV = view(UW, 6288, 4, NL)
        XR = view(UW, 8336, 4, NL)
        LA = view(UW, 10384, 4, NL)
        LU = view(UW, 12432, 4, NL)
        LH = view(UW, 14480, 4, NL)
        TH = view(UW, 16528, 4, NL)
        WB = UW[:, 23040:24064].rearrange("p (g t n) -> p g t n", g=2, t=4)
        DG = UW[:, 21504:23040].rearrange("p (i n) -> p i n", n=P)
        NDG = 12
        MR = UW[:, 0:12 * SLOT].rearrange("p (q n) -> p q n", n=SLOT)
        scr = ring[:, :, :].rearrange("p r n -> p (r n)")
        XG = view(scr, 0, KD, 2 * CAP)
        SEL, SELG, SELT, GH = (scr[:, 1024 + 512 * i:1536 + 512 * i] for i in range(4))
        GT = view(scr, 3072, 4, 2 * CAP)
        YS = scr[:, 4096:5120]
        WP = view(scr, 5120, 2, D)
        PTT = view(scr, 7168, 2, NL)
        SGM = UW[:, 27648:28160]
        EB = view(UW, 8192, KD, NL)
        EQ = view(UW, 14336, KD, NL)
        PG = view(UW, 12288, 2, NL)
        RE = UW[:, 13312:13824]
        WR = sb("wr", [P, KD, NR])
        rb = sb("rb", [P, NR])

        def htok(c, k):
            if c < 3:
                at = 19968 + 4608 + c * D + k * P
                return UW[:, at:at + P]
            return H[:, k // 2, NL + (k % 2) * P:NL + (k % 2 + 1) * P]

        def htok_half(c, q):
            if c < 3:
                at = 19968 + 4608 + c * D + q * 4 * P
                return UW[:, at:at + 4 * P].rearrange("p (a b) -> p a b", a=2)
            return H[:, 2 * q:2 * q + 2, NL:NL + 2 * P]

        zeroed = sem("pads_zeroed")
        wb_in, wb_zero = sem("lru_weights_in"), sem("lru_weights_zeroed")
        chain = sem("vector_chain")
        lam_e, lam_a = sem("lambda_exp"), sem("lambda_abs")
        h2 = sem("plain_h_ready")
        conv_t = sem("conv_taps")
        conv_p, conv_k = sem("conv_products"), sem("conv_kept")
        diag, lconv = sem("diagonals"), sem("short_conv_ready")
        gpe, gact = sem("lru_gate_products"), sem("lru_gates_ready")
        lth, lexp, lm2, lsq = sem("lru_tanh"), sem("lru_decay"), sem("lru_square"), sem("lru_root")
        ylru, lnm, lnc, lns = sem("lru_branch_ready"), sem("ln_mean"), sem("ln_centred"), sem("ln_squares")
        lnv, lnr, lnn, yconv = sem("ln_variance"), sem("ln_rooted"), sem("ln_normed"), sem("conv_branch_ready")
        r_in, rl, re1, re2 = sem("router_in"), sem("route_logits"), sem("route_exp_in"), sem("route_exp")
        r_mask, r_pos, r_ok = sem("route_mask"), sem("route_positions"), sem("route_ready")
        ht, htk_a, htk_v = sem("tokens_turned"), sem("tokens_kept_a"), sem("tokens_kept_v")
        m_load = [sem(f"expert_slot{q}_loaded") for q in range(12)]
        m_steps = sem("expert_slots_used")
        m_sel, m_selt, m_seltk = sem("selection_ready"), sem("selection_turned"), sem("selection_kept")
        m_xg, m_xga, m_xgv = sem("tokens_gathered"), sem("gathered_kept_a"), sem("gathered_kept_v")
        m_act, m_g, m_gt, m_gk = sem("expert_silu"), sem("expert_hidden"), sem("hidden_turned"), sem("hidden_kept")
        m_ysa, m_ysv = sem("expert_out_kept_a"), sem("expert_out_kept_v")
        m_sc, m_add = sem("scattered"), sem("added_to_x")
        p_in, e_pe, e_k, e_sq, e_ms = sem("ple_in"), sem("e_products"), sem("e_kept"), sem("e_squares"), sem("e_mean")
        e_rt, e_ok = sem("e_rooted"), sem("e_ready")
        pg_pe, pg_a, pg_in = sem("ple_gate_product"), sem("ple_gate"), sem("ple_gate_loaded")
        m_eq, m_dec, r_lam = sem("places_found"), sem("places_lowered"), sem("lambda_ready")

        def rtile(at, a, b):
            return scr[:, at:at + a * b].rearrange("p (a b) -> p a b", b=b)

        rexp = [scr[:, 848:864], scr[:, 904:908]]

        block = es.enter_context(nc.Block())

        def pieces(nt):
            return [(a, min(a + 512, nt)) for a in range(0, nt, 512)]

        U0 = [0, len(attention_units(0))]

        def updating_step(n, m):
            if n % 2:
                return 2 * SLOT0[n // 2, "w_o"] + m
            return 2 * SLOT0[n // 2 - 1, "ffn_out"] + 8 * (m // 2) + 6 + m % 2


        @block.sync
        def _(sp):
            def load(n, k, n4=None):
                r = n % RING
                at = n if n4 is None else n4 * 4 + r
                if n >= RING:
                    sp.wait_ge(steps, 2 * at - 6)
                sp.dma_start(ring[:, r, 0:k * 256],
                             stream[ds(at, 1), :, 0:k * 256].rearrange("a p n -> p (a n)"))\
                  .then_inc(loaded[r], 16)

            def load_phase(n0, count, widths):
                n = n0
                for j in range(min(count, 4) if count < 8 else 4):
                    load(n + j, widths[j % len(widths)])
                left = count - 4
                if left >= 4:
                    rounds = left // 4
                    with sp.Fori(1, 1 + rounds) as i:
                        for j in range(4):
                            m = n0 + j
                            load_at(m, widths[j % len(widths)], i)
                    left -= 4 * rounds
                if left > 0:
                    for j in range(left):
                        m = n0 + count - left + j
                        load(m, widths[(count - left + j) % len(widths)])

            def load_at(m, k, i):
                r = m % RING
                sp.wait_ge(steps, 8 * i + (2 * m - 6))
                sp.dma_start(ring[:, r, 0:k * 256],
                             stream[ds(4 * i + m, 1), :, 0:k * 256].rearrange("a p n -> p (a n)"))\
                  .then_inc(loaded[r], 16)

            for l in range(LAYERS):
                for name, count in layer_slots(l):
                    load_phase(SLOT0[l, name], count,
                               {"merge": [8, 4], "ffn_out": [b - a for a, b in FFQ]}.get(name, [8]))
            load_phase(SLOT0[2, "w_in2"], 8, [KD])
            load_phase(SLOT0[2, "w_out2"], 4, [KD])
            sp.wait_ge(steps, 2 * N_STREAM)
            for q in range(12):
                sp.dma_start(MR[:, q, :], experts[0, q]).then_inc(m_load[q], 16)
            sp.dma_start(scr[:, 5120:7168], w_ple).then_inc(p_in, 16)
            sp.dma_start(scr[:, 7168:8192], pT).then_inc(p_in, 16)
            sp.wait_ge(r_ok, 1)
            total = sp.value_load(total_i[0:1, 0:1], min_val=PAIRS, max_val=PAIRS * (NL // CAP))
            with sp.Fori(1, total) as i:
                j = i % PAIRS
                for q in range(12):
                    sp.wait_ge(m_steps, 12 * i + (q // 2 * 2 - 10))
                    sp.dma_start(MR[:, q, :], experts[ds(j, 1), q].rearrange("a p n -> p (a n)")).then_inc(m_load[q], 16)
            sp.wait_ge(m_steps, 12 * total)
            for q in range(4):
                sp.dma_start(MR[:, q, :], w_gate[q]).then_inc(pg_in, 16)
            for k in range(KD):
                sp.wait_ge(x_upd, 17 + k)
                sp.dma_start(out[k * P:(k + 1) * P, :], X[:, k, 0:NL]).then_inc(xo, 16)
            sp.wait_ge(xo, 16 * KD)

        @block.tensor
        def _(pe):
            def wait_slot(n, extra=0):
                pe.wait_ge(loaded[n % RING], 16 * (n // RING + 1) + extra)

            def wait_half(s, extra=0):
                u = previous_user(s)
                if u:
                    pe.wait_ge(evac[u[0]], u[1] + extra)

            def wide(s, k0, k1, rhs, nt, start=True, stop=True, signal=True):
                r, half = (s // 2) % RING, s % 2
                w = ring[:, r, :].rearrange("p (k n) -> p k n", n=256)
                for k in range(k0, k1):
                    for a, b in pieces(nt):
                        last = nc.tensor.matmul(ps[half][:, a:b], w[:, k - k0, half * P:(half + 1) * P],
                                                rhs(k, a, b), start=start and k == k0, stop=stop and k == k1 - 1)
                last.then_inc(steps, 1)

            def tokens_first(s):
                r, half = (s // 2) % RING, s % 2
                w = ring[:, r, :].rearrange("p (k n) -> p k n", n=256)
                for c in range(6):
                    for k in range(KD):
                        last = nc.tensor.matmul(ps[half][:, c * P:(c + 1) * P], H[:, k, c * P:(c + 1) * P],
                                                w[:, k, half * P:(half + 1) * P], start=k == 0, stop=k == KD - 1)
                last.then_inc(steps, 1)

            kept = []

            def mod_turn():
                tile, l = kept[-1]
                pe.wait_ge(mod_kept, len(kept))
                for half in range(2):
                    c = 768 + 96 * l + 2 * (tile + half)
                    last = nc.tensor.matmul(ps[3][:, c:c + 2], mrow[:, half * P:(half + 1) * P], fold, start=True, stop=True)
                last.then_inc(mod_turned, 1)

            def mod_slot(n, tile, l, first=False):
                if not first:
                    mod_turn()
                wait_slot(n)
                w = ring[:, n % RING, :].rearrange("p (k n) -> p k n", n=256)
                for k in range(KD):
                    g = 32 * (k % 4)
                    last = nc.tensor.matmul(ps[3][g:g + 32, 512:768], sc2[:, k, :], w[:, k, :], start=k < 4, stop=k >= 4)
                last.then_inc(steps, 2)
                kept.append((tile, l))

            def spread_sum(n, nt):
                pe.wait_ge(summed, 8 * n + 8)
                for a, b in pieces(nt):
                    last = nc.tensor.matmul(ps[2][:, a:b], onesm, NG[:, 0, a:b], start=True, stop=True)
                last.then_inc(sum_spread, 1)

            pe.wait_ge(inputs, 32)
            pe.wait_ge(silu_done, 1)
            for n in range(8):
                mod_slot(n, 2 * n, 0, n == 0)
            mod_turn()

            h_of = lambda k, a, b: H[:, k, a:b]
            for l in range(LAYERS):
                spread_sum(2 * l, T)
                ntq = T if l == 0 else NL
                hbase = 16 * l

                def plain(s, nt, wait_h=False):
                    if s % 2 == 0:
                        wait_slot(s // 2)
                    wait_half(s)
                    if wait_h:
                        r = (s // 2) % RING
                        w = ring[:, r, :].rearrange("p (k n) -> p k n", n=256)
                        for k in range(KD):
                            pe.wait_ge(h_ready, hbase + k + 1)
                            for a, b in pieces(nt):
                                last = nc.tensor.matmul(ps[s % 2][:, a:b], w[:, k, (s % 2) * P:(s % 2 + 1) * P],
                                                        H[:, k, a:b], start=k == 0, stop=k == KD - 1)
                        last.then_inc(steps, 1)
                    else:
                        wide(s, 0, KD, h_of, nt)

                def head_stat(t):
                    nt = ntq if t < 4 else T
                    g = 5 * l + t
                    pe.wait_ge(g_sq, g + 1)
                    if g:
                        pe.wait_ge(g_rt, g)
                    for a, b in pieces(nt):
                        last = nc.tensor.matmul(ps[2][:, a:b], blk, SQ[:, t % 2, a:b], start=True, stop=True)
                    last.then_inc(g_ms, 1)

                def head_rot(t):
                    g = 5 * l + t
                    pe.wait_ge(g_n, g + 1)
                    if g:
                        pe.wait_ge(g_sin, g)
                    nc.tensor.matmul(ps[3][:, 0:NL], rot, NG[:, t % 2, 0:NL], start=True, stop=True).then_inc(g_rot, 1)

                s = 2 * SLOT0[l, "gq"]
                for j in range(4):
                    plain(s + j, ntq, wait_h=(j == 0))
                    if j >= 1:
                        head_stat(j - 1)
                    if j >= 2:
                        head_rot(j - 2)
                plain(s + 4, T)
                head_stat(3)
                head_rot(2)
                wait_half(s + 5)
                tokens_first(s + 5)
                head_stat(4)
                head_rot(3)
                s = 2 * SLOT0[l, "nak"]
                for j in range(4):
                    plain(s + j, T)
                    if j == 0:
                        head_rot(4)
                for j in range(4):
                    plain(s + 4 + j, ntq)
                for j in range(4):
                    if j % 2 == 0:
                        wait_slot((s + 8 + j) // 2)
                    wait_half(s + 8 + j)
                    tokens_first(s + 8 + j)

                units = attention_units(l)
                NU = len(units)
                u0 = U0[l]
                slot = SLOT0[l, "mod_rest"]
                mods = [(0, 16 + 2 * j) for j in range(16)] + [(1, 2 * j) for j in range(8)] if l == 0 else \
                       [(1, 16 + 2 * j) for j in range(16)]
                per_pair = NU // 8
                pe.wait_ge(evac["A"], evacuated("A", 2 * SLOT0[l, "mod_rest"] - 1))
                pe.wait_ge(g_q, 5 * (l + 1))
                for i in range(NU + 4):
                    if i < NU:
                        na, t, qb, half = units[i]
                        lo = half * HD
                        Q, K = (QNA[:, t, :], KNA[:, t, :]) if na else (QG[:, t, :], KG[:, 0, :])
                        if i >= 2:
                            pe.wait_ge(s_exp, u0 + i - 1)
                        q = Q[lo:lo + HD, qb * P:(qb + 1) * P]
                        for a, b in ((0, 512), (512, 768)):
                            if qb >= 4 and a == 0:
                                continue
                            last = nc.tensor.matmul(ps[i % 2][:, a:b], q, K[lo:lo + HD, a:b], start=True, stop=True)
                        last.then_inc(s_sc, 1)
                        if i % (per_pair // (3 if l == 0 else 2)) == 0:
                            lm, tile = mods[slot - SLOT0[l, "mod_rest"]]
                            mod_slot(slot, tile, lm, i == 0)
                            slot += 1
                    if 2 <= i < NU + 2:
                        u = u0 + i - 2
                        c0 = 0 if units[i - 2][2] < 4 else 4
                        pe.wait_ge(s_dg, u + 1)
                        if i > 2:
                            pe.wait_ge(s_pta, u)
                        for c in range(c0, 4):
                            last = nc.tensor.matmul(ps[2][:, c * P:(c + 1) * P], PB[:, u % 3, c * P:(c + 1) * P],
                                                    inv[:, u % 2, :], start=True, stop=True)
                        if c0 == 0:
                            last.then_inc(s_tr, 1)
                        if i > 2:
                            pe.wait_ge(s_ptb, u)
                        for c in range(4, 6):
                            last = nc.tensor.matmul(ps[2][:, c * P:(c + 1) * P], PB[:, u % 3, c * P:(c + 1) * P],
                                                    inv[:, u % 2, :], start=True, stop=True)
                        last.then_inc(s_tr, 1 if c0 == 0 else 2)
                    if i >= 4 and i % 2 == 0:
                        na, t, qb, _ = units[i - 4]
                        u = u0 + i - 4
                        w = u // 2
                        c0 = 0 if qb < 4 else 4
                        pe.wait_ge(s_pta, u + 2)
                        pe.wait_ge(s_ptb, u + 2)
                        if i >= 8:
                            pe.wait_ge(s_y, w - 1)
                        for c in range(c0, 6):
                            for half in range(2):
                                h = (2 * t + half) * HD if na else 512 + half * HD
                                last = nc.tensor.matmul(ps[3][half * HD:(half + 1) * HD, P * (w % 2):P * (w % 2) + P],
                                                        V[:, c, h:h + HD], PT[:, (u + half) % 3, c * P:(c + 1) * P],
                                                        start=c == c0, stop=c == 5)
                        last.then_inc(s_pv, 1)
                mod_turn()

                nt = ntq
                s0 = 2 * SLOT0[l, "merge"]
                pe.wait_ge(s_y, (u0 + NU) // 2)

                def merge_round(i):
                    for j in range(4):
                        for half in range(2):
                            s = s0 + 2 * j + half
                            n = s // 2
                            if half == 0:
                                pe.wait_ge(loaded[n % RING], 16 * i + 16 * (n // RING + 1))
                            if j == 0 and isinstance(i, int) and i == 0:
                                wait_half(s)
                            else:
                                sq = s + 8
                                who, count = previous_user(sq)
                                per = 4
                                pe.wait_ge(evac[who], per * i + (count - per))
                            if j % 2 == 0:
                                wide(s, 0, KD, h_of, nt)
                            else:
                                wide(s, 0, 4, lambda k, a, b: Y[:, (0 if j == 1 else 4) + k, a:b], nt)

                merge_round(0)
                with pe.Fori(1, 4) as i:
                    merge_round(i)

                s0 = 2 * SLOT0[l, "w_o"]
                pe.wait_ge(merged, 8 * (l + 1))
                for j in range(8):
                    if j % 2 == 0:
                        wait_slot((s0 + j) // 2)
                    wait_half(s0 + j)
                    wide(s0 + j, 0, KD, lambda k, a, b: M[:, k, a:b], nt)

                spread_sum(2 * l + 1, nt)
                s0 = 2 * SLOT0[l, "ffn_in"]
                hb = hbase + 8

                def ffn_in_slots(count, first, i=0):
                    for j in range(count):
                        for half in range(2):
                            s = s0 + 2 * (first + j) + half
                            n = s // 2
                            if half == 0:
                                pe.wait_ge(loaded[n % RING], 16 * i + 16 * (n // RING + 1))
                            u = previous_user(s)
                            pe.wait_ge(evac[u[0]], 4 * i + u[1])
                            w = ring[:, n % RING, :].rearrange("p (k n) -> p k n", n=256)
                            for k in range(KD):
                                if first == 0 and j == 0 and half == 0:
                                    pe.wait_ge(h_ready, hb + k + 1)
                                for a, b in pieces(nt):
                                    last = nc.tensor.matmul(ps[half][:, a:b], w[:, k, half * P:(half + 1) * P],
                                                            H[:, k, a:b], start=k == 0, stop=k == KD - 1)
                            last.then_inc(steps, 1)

                ffn_in_slots(2, 0)
                with pe.Fori(0, 5) as i:
                    ffn_in_slots(4, 2, i)

                s0 = 2 * SLOT0[l, "ffn_out"]
                pe.wait_ge(evac["V"], evacuated("V", s0 - 1))

                def ffn_out_round(i):
                    for q, (ka, kb) in enumerate(FFQ):
                        for half in range(2):
                            s = s0 + 2 * q + half
                            n = s // 2
                            if half == 0:
                                pe.wait_ge(loaded[n % RING], 16 * i + 16 * (n // RING + 1))
                            if q == 0:
                                if isinstance(i, int):
                                    wait_half(s)
                                else:
                                    who, count = previous_user(s + 8)
                                    pe.wait_ge(evac[who], 2 * i + (count - 2))
                            wide(s, ka, kb, lambda k, a, b: G[:, k, a:b], nt, start=q == 0, stop=q == 3)

                ffn_out_round(0)
                with pe.Fori(1, 4) as i:
                    ffn_out_round(i)
            spread_sum(4, NL)
            spread_sum(5, NL)

            s0 = 2 * SLOT0[2, "w_in2"]
            for j in range(16):
                s = s0 + j
                if j % 2 == 0:
                    wait_slot(s // 2)
                wait_half(s)
                w = ring[:, (s // 2) % RING, :].rearrange("p (k n) -> p k n", n=256)
                for k in range(KD):
                    if j == 0:
                        pe.wait_ge(h2, k + 1)
                    last = nc.tensor.matmul(ps[s % 2][:, 0:NL], w[:, k, (s % 2) * P:(s % 2 + 1) * P], H[:, k, 0:NL],
                                            start=k == 0, stop=k == KD - 1)
                last.then_inc(steps, 1)
            pe.wait_ge(wb_in, 16 * 16)
            for j in range(8):
                t, g = j // 2, j % 2
                if g == 0:
                    pe.wait_ge(lconv, t + 1)
                if j >= 4:
                    pe.wait_ge(gact, j - 3)
                bank = ps[2 + (j % 4) // 2][:, 512 * (j % 2):512 * (j % 2) + 512]
                nc.tensor.matmul(bank, WB[:, g, t, :], XR[:, t, :], start=True, stop=True).then_inc(gpe, 1)
            pe.wait_ge(evac["A"], evacuated("A", s0 + 15))
            for n, t in enumerate(PE_CONV):
                pe.wait_ge(evac["V"], evacuated("V", s0 + 2 * t + 1))
                for d in range(TAPS):
                    c = n * TAPS + d
                    pe.wait_ge(diag, c + 1)
                    nc.tensor.matmul(ps[n][:, 0:NL], DG[:, c % NDG, :], UC[:, t, d:d + NL], start=d == 0,
                                     stop=d == TAPS - 1).then_inc(conv_p, 1)
            pe.wait_ge(gact, 8)
            pe.wait_ge(conv_k, 4)
            for t in range(4):
                last = nc.tensor.matmul(ps[2][:, 0:NL], onesm, CV[:, t, :], start=t == 0, stop=t == 3)
            last.then_inc(lnm, 1)
            for t in range(4):
                pe.wait_ge(lns, t + 1)
                last = nc.tensor.matmul(ps[3][:, 0:NL], onesm, TH[:, t, :], start=t == 0, stop=t == 3)
            last.then_inc(lnv, 1)
            s0 = 2 * SLOT0[2, "w_out2"]
            pe.wait_ge(ylru, 4)
            for j in range(8):
                s = s0 + j
                if j % 2 == 0:
                    wait_slot(s // 2)
                if j >= 2:
                    wait_half(s)
                w = ring[:, (s // 2) % RING, :].rearrange("p (k n) -> p k n", n=256)
                for n, k in enumerate((4, 5, 6, 7, 0, 1, 2, 3)):
                    if j == 0 and k < 4:
                        pe.wait_ge(yconv, k + 1)
                    rhs = CV[:, k, :] if k < 4 else LH[:, k - 4, :]
                    last = nc.tensor.matmul(ps[s % 2][:, 0:NL], w[:, k, (s % 2) * P:(s % 2 + 1) * P], rhs,
                                            start=n == 0, stop=n == KD - 1)
                last.then_inc(steps, 1)
            spread_sum(6, NL)
            pe.wait_ge(r_in, 32)
            pe.wait_ge(lnr, 1)
            pe.wait_ge(h2, 16)
            for c in range(4):
                for k in range(KD):
                    last = nc.tensor.matmul(ps[3][:, c * 64:c * 64 + NR], H[:, k, c * P:(c + 1) * P], WR[:, k, :],
                                            start=k == 0, stop=k == KD - 1)
            last.then_inc(rl, 1)
            pe.wait_ge(rooted, 7)
            for c in range(3):
                if c < 2:
                    wait_half(2 * N_STREAM + c)
                for k in range(KD):
                    last = nc.tensor.transpose(ps[c][:, k * P:(k + 1) * P], H[:, k, c * P:(c + 1) * P], ident)
                last.then_inc(ht, 1)
            pe.wait_ge(htk_a, 1)
            pe.wait_ge(htk_v, 1)
            for k in range(KD):
                last = nc.tensor.transpose(ps[0][:, k * P:(k + 1) * P], H[:, k, 3 * P:4 * P], ident)
            last.then_inc(ht, 1)
            pe.wait_ge(r_mask, 1)
            for c in range(4):
                for b in range(c + 1):
                    nc.tensor.matmul(ps[3][:, c * 32:(c + 1) * 32], tri if b == c else ones1, SEL[:, b * 32:(b + 1) * 32],
                                     start=b == 0, stop=b == c)
            for b in range(4):
                last = nc.tensor.matmul(ps[3][:, 128:160], ones1, SEL[:, b * 32:(b + 1) * 32], start=b == 0, stop=b == 3)
            last.then_inc(r_pos, 1)

            pe.wait_ge(htk_a, 4)
            pe.wait_ge(htk_v, 4)
            pe.wait_ge(r_ok, 1)
            total = pe.value_load(total_i[0:1, 0:1], min_val=PAIRS, max_val=PAIRS * (NL // CAP))
            with pe.Fori(0, total) as i:
                pe.wait_ge(m_sel, i + 1)
                for c in range(4):
                    last = nc.tensor.transpose(ps[3][:, c * P:(c + 1) * P], SELG[:, c * P:(c + 1) * P], ident)
                last.then_inc(m_selt, 1)
                pe.wait_ge(m_add, 8 * i + 1)
                for k in range(KD):
                    for c in range(4):
                        last = nc.tensor.matmul(ps[0][:, k * P:(k + 1) * P], htok(c, k), SEL[:, c * P:(c + 1) * P],
                                                start=c == 0, stop=c == 3)
                last.then_inc(m_xg, 1)
                pe.wait_ge(m_xga, i + 1)
                pe.wait_ge(m_xgv, i + 1)
                for w13 in range(2):
                    for kk in range(2):
                        q = 4 * w13 + 2 * kk
                        pe.wait_ge(m_load[q], 16 * i + 16)
                        pe.wait_ge(m_load[q + 1], 16 * i + 16)
                        for k in range(4):
                            for x in range(2):
                                w = MR[:, q + x, k * 512:(k + 1) * 512]
                                last = nc.tensor.matmul(ps[1][CAP * x:CAP * x + CAP, 512 * w13:512 * w13 + 512],
                                                        XG[:, 4 * kk + k, x * CAP:(x + 1) * CAP], w,
                                                        start=kk == 0 and k == 0, stop=kk == 1 and k == 3)
                        last.then_inc(m_steps, 2)
                pe.wait_ge(m_g, i + 1)
                for k in range(4):
                    last = nc.tensor.transpose(ps[3][:, 512 + k * P:640 + k * P], GH[:, k * P:(k + 1) * P], ident)
                last.then_inc(m_gt, 1)
                pe.wait_ge(m_gk, i + 1)
                for kk in range(2):
                    q = 8 + 2 * kk
                    pe.wait_ge(m_load[q], 16 * i + 16)
                    pe.wait_ge(m_load[q + 1], 16 * i + 16)
                    for k in range(2):
                        for n in range(2):
                            for x in range(2):
                                w = MR[:, q + x, k * D + 512 * n:k * D + 512 * n + 512]
                                last = nc.tensor.matmul(ps[2][CAP * x:CAP * x + CAP, 512 * n:512 * n + 512],
                                                        GT[:, 2 * kk + k, x * CAP:(x + 1) * CAP], w,
                                                        start=kk == 0 and k == 0, stop=kk == 1 and k == 1)
                    last.then_inc(m_steps, 2)
                pe.wait_ge(m_seltk, i + 1)
                for m in range(KD):
                    pe.wait_ge((m_ysa, m_ysv)[m // 4], i + 1)
                    if m >= 2:
                        pe.wait_ge(m_add, 8 * i + m)
                    nc.tensor.matmul(ps[0][:, 512 * (m % 2):512 * (m % 2) + 512], YS[:, m * P:(m + 1) * P], SELT,
                                     start=True, stop=True).then_inc(m_sc, 1)

            pe.wait_ge(p_in, 32)
            pe.wait_ge(m_add, 8 * total + 1)
            for m in range(KD):
                if m >= 2:
                    pe.wait_ge(e_sq, m - 1)
                for k in range(2):
                    last = nc.tensor.matmul(ps[m % 2][:, 0:NL], WP[:, k, m * P:(m + 1) * P], PTT[:, k, :],
                                            start=k == 0, stop=k == 1)
                last.then_inc(e_pe, 1)
            spread_sum(7, NL)
            for m in range(KD):
                pe.wait_ge(e_sq, m + 1)
                last = nc.tensor.matmul(ps[3][:, 0:NL], onesm, EQ[:, m, :], start=m == 0, stop=m == KD - 1)
            last.then_inc(e_ms, 1)
            for m in range(KD):
                if m % 2 == 0:
                    pe.wait_ge(pg_in, 64)
                if m >= 2:
                    pe.wait_ge(pg_a, m - 1)
                w = MR[:, m // 2, :].rearrange("p (k n) -> p k n", n=256)
                for k in range(KD):
                    if m == 0:
                        pe.wait_ge(h2, 17 + k)
                    last = nc.tensor.matmul(ps[m % 2][:, 0:NL], w[:, k, (m % 2) * P:(m % 2 + 1) * P], H[:, k, 0:NL],
                                            start=k == 0, stop=k == KD - 1)
                last.then_inc(pg_pe, 1)
            spread_sum(8, NL)

        @block.scalar
        def _(act):
            act.dma_start(vec[:, :], vecs).then_inc(inputs, 16)
            act.dma_start(cst[:, :], consts).then_inc(inputs, 16)
            for k in range(KD):
                act.dma_start(X[:, k, 0:NL], xT[k * P:(k + 1) * P, :]).then_inc(x_loaded, 16)
                act.dma_start(X[:, k, NL:T], ctxT[k * P:(k + 1) * P, :]).then_inc(x_loaded, 16)
            act.wait_ge(inputs, 32)
            act.wait_ge(sc_zero, 1)
            act.activation(sc2[:, :, 0:2], vcol("c2", 0, 16).rearrange("p (k n) -> p k n", n=2), ACT.Silu)\
               .then_inc(silu_done, 1)

            def keep_mod(n):
                act.wait_ge(steps, 2 * n + 2)
                act.activation(mrow[:, :], ps[3][:, 512:768], ACT.Copy).then_inc(mod_kept, 1)


            def squares(n, nt):
                for m in range(KD):
                    if n == 0:
                        act.wait_ge(x_loaded, 32 * (m + 1) if m == KD - 1 else 256)
                    elif n in (5, 8):
                        act.wait_ge(x_upd, (1 if n == 5 else 9) + m)
                    elif n == 6:
                        act.wait_ge(evac["V"], evacuated("V", 2 * SLOT0[2, "w_out2"] + m))
                    elif n != 7:
                        act.wait_ge(evac["V"], evacuated("V", updating_step(n, m)))
                    if 8 * n + m >= 2:
                        act.wait_ge(summed, 8 * n + m - 1)
                    act.activation(CG[:, m % 2, 0:nt], X[:, m, 0:nt], ACT.Square).then_inc(squared, 1)

            def root(n, nt):
                act.wait_ge(sum_spread, n + 1)
                act.activation(NG[:, 1, 0:nt], ps[2][:, 0:nt], ACT.Sqrt, bias=epsc[:, 0:1]).then_inc(rooted, 1)

            def shift_scale(l, which, nt):
                n = 2 * l + which
                for k in range(KD):
                    act.wait_ge(normed, 8 * n + k + 1)
                    if k == 0:
                        act.wait_ge(mod_ready, 2 * l + which + 1)
                    for kind, (a, b) in enumerate(((0, NL), (NL, nt))):
                        if a == b:
                            continue
                        last = act.activation(H[:, k, a:b], H[:, k, a:b], ACT.Identity,
                                              scale=amod[:, 2 * l + which, k, kind:kind + 1],
                                              bias=mod[:, 48 * l + 24 * which + k, kind:kind + 1])
                    last.then_inc(h_ready, 1)

            act.wait_ge(small_ok, 1)
            squares(0, T)
            for l in range(LAYERS):
                ntq = T if l == 0 else NL
                root(2 * l, T)
                shift_scale(l, 0, T)

                def step_done(s):
                    act.wait_ge(steps, s + 1)

                def keep_head(t):
                    s = 2 * SLOT0[l, "gq"] + t
                    g = 5 * l + t
                    nt = ntq if t < 4 else T
                    step_done(s)
                    if g >= 2:
                        act.wait_ge(g_n, g - 1)
                    act.activation(RAW[:, t % 2, 0:nt], ps[s % 2][:, 0:nt], ACT.Copy).then_inc(evac["A"], 1)
                    act.wait_ge(evac["A"], evacuated("A", s))
                    if g >= 2:
                        act.wait_ge(g_ms, g - 1)
                    act.activation(SQ[:, t % 2, 0:nt], RAW[:, t % 2, 0:nt], ACT.Square).then_inc(g_sq, 1)

                def root_head(t):
                    g = 5 * l + t
                    nt = ntq if t < 4 else T
                    act.wait_ge(g_ms, g + 1)
                    if g >= 2:
                        act.wait_ge(g_n, g - 1)
                    act.activation(RS[:, t % 2, 0:nt], ps[2][:, 0:nt], ACT.Sqrt, bias=epsc[:, 0:1]).then_inc(g_rt, 1)

                for t in range(5):
                    keep_head(t)
                    if t:
                        root_head(t - 1)
                s = 2 * SLOT0[l, "gkv"] + 1
                step_done(s)
                act.activation(V[:, :, 512:640], ps[s % 2][:, 0:T].rearrange("p (c n) -> p c n", n=P), ACT.Copy)\
                   .then_inc(evac["A"], 1)
                root_head(4)
                s = 2 * SLOT0[l, "nak"]
                for j in range(4):
                    step_done(s + j)
                    act.activation(KNA[:, j, :], ps[(s + j) % 2][:, 0:T], ACT.Copy).then_inc(evac["A"], 1)
                s = 2 * SLOT0[l, "naq"]
                for j in range(4):
                    step_done(s + j)
                    act.activation(QNA[:, j, 0:ntq], ps[(s + j) % 2][:, 0:ntq], ACT.Copy, scale=QSCALE)\
                       .then_inc(evac["A"], 1)
                s = 2 * SLOT0[l, "nav"]
                for j in range(4):
                    step_done(s + j)
                    act.activation(V[:, :, j * P:(j + 1) * P], ps[(s + j) % 2][:, 0:T].rearrange("p (c n) -> p c n", n=P),
                                   ACT.Copy).then_inc(evac["A"], 1)

                units = attention_units(l)
                NU = len(units)
                u0 = U0[l]
                act.wait_ge(g_q, 5 * (l + 1))
                slot = SLOT0[l, "mod_rest"]
                per_pair = NU // 8
                for i in range(NU + 4):
                    if 2 <= i < NU + 2:
                        u = u0 + i - 2
                        if i >= 5:
                            act.wait_ge(s_pv, (u - 3) // 2 + 1)
                        if units[i - 2][2] < 4:
                            act.wait_ge(s_tr, 2 * u + 1)
                            act.activation(PT[:, u % 3, 0:512], ps[2][:, 0:512], ACT.Copy).then_inc(s_pta, 1)
                        else:
                            act.wait_ge(s_tr, 2 * u + 2)
                            act.activation(small[:, 3, 7:8], epsc[:, 0:1], ACT.Copy).then_inc(s_pta, 1)
                    if i < NU:
                        u = u0 + i
                        c0 = 0 if units[i][2] < 4 else 512
                        act.wait_ge(s_mx, u + 1)
                        if i >= 3:
                            act.wait_ge(s_tr, 2 * (u - 3) + 2)
                        act.activation(PB[:, u % 3, c0:T], ps[i % 2][:, c0:T], ACT.Exp, bias=small[:, 0, u % 8:u % 8 + 1],
                                       accum_out=small[:, 1, u % 8:u % 8 + 1]).then_inc(s_exp, 1)
                        if i % (per_pair // (3 if l == 0 else 2)) == 0:
                            keep_mod(slot)
                            slot += 1
                    if i >= 4 and i % 2 == 0:
                        na, t, qb, _h = units[i - 4]
                        w = (u0 + i - 4) // 2
                        act.wait_ge(s_pv, w + 1)
                        act.activation(Y[:, (0 if na else 4) + t, qb * P:(qb + 1) * P],
                                       ps[3][:, P * (w % 2):P * (w % 2) + P], ACT.Copy).then_inc(s_y, 1)

                s0 = 2 * SLOT0[l, "merge"]
                nt = ntq

                def gates(i):
                    for j in (0, 2):
                        for half in range(2):
                            s = s0 + 2 * j + half
                            act.wait_ge(steps, 8 * i + (s + 1))
                            if j:
                                act.wait_ge(evac["V"], 4 * i + evacuated("V", s - 2))
                            elif not isinstance(i, int):
                                act.wait_ge(evac["V"], 4 * i + (evacuated("V", s + 6) - 4))
                            act.activation(RAW[:, half, 0:nt], ps[half][:, 0:nt], ACT.Sigmoid).then_inc(evac["A"], 1)

                gates(0)
                with act.Fori(1, 4) as i:
                    gates(i)

                squares(2 * l + 1, nt)
                root(2 * l + 1, nt)
                shift_scale(l, 1, nt)

                s0 = 2 * SLOT0[l, "ffn_in"]

                def silus(count, first, i=0):
                    for j in range(first, first + count):
                        s = s0 + 2 * j
                        act.wait_ge(steps, 8 * i + (s + 1))
                        if j >= 2:
                            act.wait_ge(evac["V"], 4 * i + evacuated("V", s - 3))
                        act.activation(RAW[:, j % 2, 0:nt], ps[0][:, 0:nt], ACT.Silu).then_inc(evac["A"], 1)

                silus(2, 0)
                with act.Fori(0, 5) as i:
                    silus(4, 2, i)
                if l == 0:
                    squares(2, T)
            squares(4, NL)
            root(4, NL)
            squares(5, NL)
            root(5, NL)
            act.wait_ge(lam_a, 1)
            act.activation(lam8[:, 1, :], lam8[:, 0, :], ACT.Exp).then_inc(lam_e, 1)
            s0 = 2 * SLOT0[2, "w_in2"]
            for t in range(4):
                s = s0 + 2 * t
                act.wait_ge(steps, s + 1)
                if t >= 2:
                    act.wait_ge(evac["V"], evacuated("V", s - 3))
                act.activation(RAW[:, t % 2, 0:NL], ps[0][:, 0:NL], ACT.Sigmoid).then_inc(evac["A"], 1)
            for t in range(4):
                s = s0 + 8 + t
                act.wait_ge(steps, s + 1)
                act.activation(XL[:, t, LTAPS - 1:LTAPS - 1 + NL], ps[s % 2][:, 0:NL], ACT.Copy).then_inc(evac["A"], 1)
            for t in range(4):
                s = s0 + 12 + t
                act.wait_ge(steps, s + 1)
                act.activation(GL[:, t, :], ps[s % 2][:, 0:NL], ACT.Gelu_apprx_tanh).then_inc(evac["A"], 1)
            for j in range(8):
                t, g = j // 2, j % 2
                act.wait_ge(gpe, j + 1)
                act.activation((LA, LU)[g][:, t, :], ps[2 + (j % 4) // 2][:, 512 * (j % 2):512 * (j % 2) + 512],
                               ACT.Sigmoid, bias=vcol(("b_r", "b_i")[g], t)).then_inc(gact, 1)
            act.wait_ge(r_lam, 1)
            for t in range(4):
                act.wait_ge(gact, 2 * t + 1)
                act.activation(TH[:, t, :], LA[:, t, :], ACT.Tanh, scale=lam8[:, 6, t:t + 1]).then_inc(lth, 1)
            for t in range(4):
                act.wait_ge(lth, t + 1)
                act.activation(LA[:, t, :], LA[:, t, :], ACT.Exp, scale=lam8[:, 7, t:t + 1]).then_inc(lexp, 1)
            for n, t in enumerate(PE_CONV):
                act.wait_ge(conv_p, TAPS * (n + 1))
                act.activation(CV[:, t, :], ps[n][:, 0:NL], ACT.Identity, bias=vcol("conv_b", t)).then_inc(conv_k, 1)
            for t in range(4):
                act.wait_ge(lm2, t + 1)
                act.activation(TH[:, t, :], TH[:, t, :], ACT.Sqrt).then_inc(lsq, 1)
            for t in range(4):
                act.wait_ge(lnc, t + 1)
                act.wait_ge(ylru, t + 1)
                act.activation(TH[:, t, :], CV[:, t, :], ACT.Square).then_inc(lns, 1)
            act.wait_ge(lnv, 1)
            act.activation(RAW[:, 0, 0:NL], ps[3][:, 0:NL], ACT.Sqrt, bias=epsc[:, 0:1], scale=2.0).then_inc(lnr, 1)
            for t in range(4):
                act.wait_ge(lnn, t + 1)
                act.activation(CV[:, t, :], CV[:, t, :], ACT.Silu, scale=vcol("ln_g", t), bias=vcol("ln_b", t))\
                   .then_inc(yconv, 1)
            squares(6, NL)
            root(6, NL)

            for c in range(4):
                if c == 3:
                    for n in range(2):
                        act.wait_ge(re1, n + 1)
                        act.activation(rexp[n], rexp[n], ACT.Exp).then_inc(re2, 1)
                act.wait_ge(ht, c + 1)
                act.activation(htok_half(c, 0), ps[c % 3][:, 0:512].rearrange("p (a b) -> p a b", a=2), ACT.Copy)\
                   .then_inc(htk_a, 1)

            act.wait_ge(r_ok, 1)
            total = act.value_load(total_i[0:1, 0:1], min_val=PAIRS, max_val=PAIRS * (NL // CAP))
            with act.Fori(0, total) as i:
                act.wait_ge(m_selt, i + 1)
                act.activation(SELT, ps[3][:, 0:512], ACT.Copy).then_inc(m_seltk, 1)
                act.wait_ge(m_xg, i + 1)
                act.activation(scr[:, 0:512], ps[0][:, 0:512], ACT.Copy).then_inc(m_xga, 1)
                act.wait_ge(m_steps, 12 * i + 4)
                act.activation(SGM, ps[1][:, 0:512], ACT.Silu).then_inc(m_act, 1)
                act.wait_ge(m_gt, i + 1)
                act.activation(scr[:, 3072:3584], ps[3][:, 512:1024], ACT.Copy).then_inc(m_gk, 1)
                act.wait_ge(m_steps, 12 * i + 12)
                act.activation(YS[:, 0:512], ps[2][:, 0:512], ACT.Copy).then_inc(m_ysa, 1)

            act.wait_ge(m_add, 8 * total + 1)
            squares(7, NL)
            for m in range(KD):
                act.wait_ge(e_pe, m + 1)
                act.activation(EB[:, m, :], ps[m % 2][:, 0:NL], ACT.Copy).then_inc(e_k, 1)
                act.activation(EQ[:, m, :], ps[m % 2][:, 0:NL], ACT.Square).then_inc(e_sq, 1)
            root(7, NL)
            act.wait_ge(e_ms, 1)
            act.activation(RE, ps[3][:, 0:NL], ACT.Sqrt, bias=epsc[:, 0:1]).then_inc(e_rt, 1)
            for m in range(KD):
                act.wait_ge(pg_pe, m + 1)
                if m >= 2:
                    act.wait_ge(x_upd, 8 + m - 1)
                act.activation(PG[:, m % 2, :], ps[m % 2][:, 0:NL], ACT.Sigmoid).then_inc(pg_a, 1)
            squares(8, NL)
            root(8, NL)

        @block.gpsimd
        def _(pool):
            def sum_squares(n, nt):
                for m in range(KD):
                    pool.wait_ge(squared, 8 * n + m + 1)
                    if m == 0:
                        nc.gpsimd.tensor_copy(NG[:, 0, 0:nt], CG[:, 0, 0:nt]).then_inc(summed, 1)
                    else:
                        pool.wait_ge(summed, 8 * n + m)
                        nc.gpsimd.tensor_tensor(NG[:, 0, 0:nt], NG[:, 0, 0:nt], CG[:, m % 2, 0:nt], ALU.add)\
                            .then_inc(summed, 1)

            nc.gpsimd.memset(sc2[:, :, :], 0.0).then_inc(sc_zero, 1)
            nc.gpsimd.memset(epsc[:, :], EPS).then_inc(small_ok, 1)
            for l in range(LAYERS):
                src = bass.AP(rpb.tensor, l * 120 * 128, [[128, 120], [0, GRID], [1, 128]])
                dst = bass.AP(rows.tensor, l * 120 * GRID * 128, [[GRID * 128, 120], [128, GRID], [1, 128]])
                pool.dma_start(dst, src).then_inc(rows_in, 16)
            sum_squares(0, T)
            for l in range(LAYERS):
                ntq = T if l == 0 else NL
                for t in range(5):
                    g = 5 * l + t
                    pool.wait_ge(g_n, g + 1)
                    if g >= 2:
                        pool.wait_ge(g_q, g - 1)
                    if t == 4 or l == 0:
                        dst = QG[:, t, NL:T] if t < 4 else KG[:, 0, NL:T]
                        nc.gpsimd.tensor_copy(dst, NG[:, t % 2, NL:T])
                    nc.gpsimd.tensor_tensor(CG[:, t % 2, 0:NL], NG[:, t % 2, 0:NL], cosT, ALU.mult).then_inc(g_cos, 1)
                pool.wait_ge(rows_in, 16 * LAYERS)
                units = attention_units(l)
                per_head = len(units) // 8
                pool.wait_ge(g_q, 5 * (l + 1))
                for h in range(8):
                    b = h % 4
                    if h >= 4:
                        pool.wait_ge(s_mx, U0[l] + per_head * (h // 2 - 1))
                    for half in range(2):
                        src = bass.AP(rows.tensor, ((l * 8 + h) * 15 + 1 - half) * GRID * 128 + 63,
                                      [[127, GRID], [GRID * 128, 14], [1, GRID]])
                        pool.dma_start(BIAS[half * GRID:(half + 1) * GRID, b, :].rearrange("p (i u) -> p i u", u=GRID),
                                       src).then_inc(bias_in[b], 16)
                    pool.wait_ge(bias_in[b], 32 * (2 * l + h // 4 + 1))
                    t3 = BIAS[:, b, :].rearrange("p (i u) -> p i u", u=GRID)
                    nc.gpsimd.tensor_tensor(t3, t3, namask[:, None, :].to_broadcast([P, 14, GRID]), ALU.add)\
                        .then_inc(bias_ok, 1)
                sum_squares(2 * l + 1, ntq)
                if l == 0:
                    sum_squares(2, T)
                if l == 1:
                    pool.wait_ge(s_y, (U0[1] + len(attention_units(1))) // 2)
                    pool.wait_ge(sum_spread, 4)
                    nc.gpsimd.memset(WB, 0.0).then_inc(wb_zero, 1)
                    pool.wait_ge(wb_zero, 1)
                    for g in range(2):
                        for h in range(8):
                            lo = (h % 2) * HD
                            pool.dma_start(WB[lo:lo + HD, g, h // 2, lo:lo + HD], lru_w[g, h]).then_inc(wb_in, 16)
                    pool.dma_start(WR[:, :, :].rearrange("p k n -> p (k n)"), router).then_inc(r_in, 16)
                    pool.dma_start(rb[:, :], router_b).then_inc(r_in, 16)
            sum_squares(4, NL)
            pool.wait_ge(sum_spread, 5)
            nc.gpsimd.memset(UC[:, :, 0:TAPS - 1], 0.0).then_inc(zeroed, 1)
            nc.gpsimd.memset(XL[:, :, 0:LTAPS - 1], 0.0).then_inc(zeroed, 1)
            sum_squares(5, NL)
            for c in range(TAPS * len(PE_CONV)):
                t, d = PE_CONV[c // TAPS], c % TAPS
                if c >= NDG:
                    pool.wait_ge(conv_p, c - NDG + 1)
                nc.gpsimd.tensor_scalar(DG[:, c % NDG, :], ident, vcol("conv_w", 4 * d + t), None, ALU.mult)\
                    .then_inc(diag, 1)
            for n in (6, 7, 8):
                sum_squares(n, NL)

        @block.vector
        def _(dve):
            def rstd(n, nt):
                dve.wait_ge(rooted, n + 1)
                nc.vector.reciprocal(NG[:, 1, 0:nt], NG[:, 1, 0:nt]).then_inc(rstd_ok, 1)
                dve.wait_ge(rstd_ok, n + 1)

            def times_rstd(n, nt):
                rstd(n, nt)
                for k in range(KD):
                    nc.vector.tensor_tensor(H[:, k, 0:nt], X[:, k, 0:nt], NG[:, 1, 0:nt], ALU.mult).then_inc(normed, 1)

            modc = [0]

            def mod_add(l, m0, m1, last=True):
                for kind in range(2):
                    nc.vector.tensor_tensor(mod[:, 48 * l + m0:48 * l + m1, kind],
                                            ps[3][:, 768 + 96 * l + 2 * m0 + kind:768 + 96 * l + 2 * m1:2],
                                            vcol(f"b_mod{l}", m0, m1 - m0), ALU.add).then_inc(mod_sum, 1)
                modc[0] += 2
                dve.wait_ge(mod_sum, modc[0])

            def mod_gain(l, which):
                for kind in range(2):
                    a = 48 * l + 24 * which + 8
                    ins = nc.vector.scalar_tensor_tensor(out=amod[:, 2 * l + which, :, kind], in0=mod[:, a:a + 8, kind],
                                                         scalar=1.0, in1=vcol(f"norm{which + 1}{l}", 0, 8),
                                                         op0=ALU.add, op1=ALU.mult)
                    ins.then_inc(mod_ready, 1) if kind else None

            dve.wait_ge(inputs, 32)
            for l in range(LAYERS):
                nc.vector.tensor_scalar(qg8[:, l:l + 1], vcol(f"q_gain{l}"), QSCALE, None, ALU.mult).then_inc(small_q, 1)
            for n in range(8):
                dve.wait_ge(steps, 2 * n + 2)
                nc.vector.tensor_copy(mrow[:, :], ps[3][:, 512:768]).then_inc(mod_kept, 1)
            dve.wait_ge(mod_turned, 8)
            mod_add(0, 0, 16)
            mod_gain(0, 0)
            for l in range(LAYERS):
                ntq = T if l == 0 else NL
                times_rstd(2 * l, T)
                dve.wait_ge(small_q, LAYERS)

                def norm_head(t):
                    g = 5 * l + t
                    nt = ntq if t < 4 else T
                    dve.wait_ge(g_rt, g + 1)
                    nc.vector.reciprocal(RS[:, t % 2, 0:nt], RS[:, t % 2, 0:nt]).then_inc(g_rr, 1)
                    dve.wait_ge(g_rr, g + 1)
                    if g >= 2:
                        dve.wait_ge(g_cos, g - 1)
                        dve.wait_ge(g_rot, g - 1)
                    gain = qg8[:, l:l + 1] if t < 4 else vcol(f"k_gain{l}")
                    nc.vector.scalar_tensor_tensor(out=NG[:, t % 2, 0:nt], in0=RAW[:, t % 2, 0:nt], scalar=gain,
                                                   in1=RS[:, t % 2, 0:nt], op0=ALU.mult, op1=ALU.mult).then_inc(g_n, 1)

                def rope_head(t):
                    g = 5 * l + t
                    dve.wait_ge(g_rot, g + 1)
                    dst = QG[:, t, 0:NL] if t < 4 else KG[:, 0, 0:NL]
                    nc.vector.tensor_tensor(dst, ps[3][:, 0:NL], sinT, ALU.mult).then_inc(g_sin, 1)
                    dve.wait_ge(g_sin, g + 1)
                    dve.wait_ge(g_cos, g + 1)
                    nc.vector.tensor_tensor(dst, dst, CG[:, t % 2, 0:NL], ALU.add).then_inc(g_q, 1)

                norm_head(0)
                for t in range(1, 5):
                    norm_head(t)
                    rope_head(t - 1)
                rope_head(4)

                units = attention_units(l)
                NU = len(units)
                u0 = U0[l]
                bias_units = [i for i, (na, _, qb, _) in enumerate(units) if na and qb < 4]
                for i in range(NU + 4):
                    if i < NU:
                        na, t, qb, half = units[i]
                        u = u0 + i
                        c = u % 8
                        dve.wait_ge(s_sc, u + 1)
                        if na and qb < 4:
                            h = 2 * t + half
                            dve.wait_ge(bias_ok, 8 * l + h + 1)
                            at = (6 - 2 * qb) * GRID
                            nc.vector.tensor_tensor(ps[i % 2][:, 0:512], ps[i % 2][:, 0:512],
                                                    BIAS[:, h % 4, at:at + 512], ALU.add).then_inc(s_m1, 1)
                            dve.wait_ge(s_m1, 32 * l + bias_units.index(i) + 1)
                        c0 = 0 if qb < 4 else 512
                        nc.vector.tensor_reduce(small[:, 0, c:c + 1], ps[i % 2][:, c0:T], AX.X, ALU.max, negate=True)\
                            .then_inc(s_mx, 1)
                    if 1 <= i < NU + 1:
                        u = u0 + i - 1
                        c = u % 8
                        dve.wait_ge(s_exp, u + 1)
                        nc.vector.reciprocal(small[:, 2, c:c + 1], small[:, 1, c:c + 1]).then_inc(s_ri, 1)
                        dve.wait_ge(s_ri, u + 1)
                        if i >= 3:
                            dve.wait_ge(s_tr, 2 * (u - 2) + 2)
                        nc.vector.tensor_scalar(inv[:, u % 2, :], ident, small[:, 2, c:c + 1], None, ALU.mult)\
                            .then_inc(s_dg, 1)
                    if 2 <= i < NU + 2:
                        u = u0 + i - 2
                        dve.wait_ge(s_tr, 2 * u + 2)
                        if i >= 5:
                            dve.wait_ge(s_pv, (u - 3) // 2 + 1)
                        nc.vector.tensor_copy(PT[:, u % 3, 512:T], ps[2][:, 512:T]).then_inc(s_ptb, 1)

                dve.wait_ge(mod_turned, 32 if l == 0 else 48)
                mod_add(l, 16, 48)
                mod_gain(l, 1)
                if l == 0:
                    mod_add(1, 0, 16)
                    mod_gain(1, 0)

                s0 = 2 * SLOT0[l, "merge"]
                nt = ntq

                def products(i):
                    for j in (1, 3):
                        for half in range(2):
                            s = s0 + 2 * j + half
                            dve.wait_ge(steps, 8 * i + (s + 1))
                            dve.wait_ge(evac["A"], 4 * i + evacuated("A", s))
                            if isinstance(i, int):
                                dst = (M[:, 2 * i + half, 0:nt] if j == 1 else SQ[:, half, 0:nt])
                            else:
                                dst = (M[:, ds(2 * i + half, 1), 0:nt] if j == 1 else SQ[:, half:half + 1, 0:nt])
                            src, gate = ps[half][:, 0:nt], RAW[:, half, 0:nt]
                            if j == 3 and not isinstance(i, int):
                                dst = SQ[:, half, 0:nt]
                            if j == 1 and not isinstance(i, int):
                                src, gate = ps[half][:, None, 0:nt], RAW[:, half:half + 1, 0:nt]
                            nc.vector.tensor_tensor(dst, src, gate, ALU.mult).then_inc(evac["V"], 1)
                            if j == 3:
                                dve.wait_ge(evac["V"], 4 * i + evacuated("V", s))
                                if isinstance(i, int):
                                    d = M[:, 2 * i + half, 0:nt]
                                    o = SQ[:, half, 0:nt]
                                else:
                                    d = M[:, ds(2 * i + half, 1), 0:nt]
                                    o = SQ[:, half:half + 1, 0:nt]
                                nc.vector.tensor_tensor(d, d, o, ALU.add).then_inc(merged, 1)

                products(0)
                with dve.Fori(1, 4) as i:
                    products(i)

                def update(s, g0, m):
                    dve.wait_ge(steps, s + 1)
                    for kind, (a, b) in enumerate(((0, NL), (NL, nt))):
                        if a == b:
                            continue
                        gate = mod[:, 48 * l + g0 + m, kind:kind + 1]
                        last = nc.vector.scalar_tensor_tensor(out=X[:, m, a:b], in0=ps[s % 2][:, a:b], scalar=gate,
                                                              in1=X[:, m, a:b], op0=ALU.mult, op1=ALU.add)
                    last.then_inc(evac["V"], 1)

                for m in range(8):
                    update(2 * SLOT0[l, "w_o"] + m, 16, m)
                times_rstd(2 * l + 1, nt)

                s0 = 2 * SLOT0[l, "ffn_in"]

                def hidden(count, first, i=0):
                    for j in range(first, first + count):
                        s = s0 + 2 * j + 1
                        dve.wait_ge(steps, 8 * i + (s + 1))
                        dve.wait_ge(evac["A"], 4 * i + evacuated("A", s))
                        if isinstance(i, int):
                            dst, src, g = G[:, j, 0:nt], ps[1][:, 0:nt], RAW[:, j % 2, 0:nt]
                        else:
                            dst, src, g = G[:, ds(4 * i + j, 1), 0:nt], ps[1][:, None, 0:nt], RAW[:, j % 2:j % 2 + 1, 0:nt]
                        nc.vector.tensor_tensor(dst, src, g, ALU.mult).then_inc(evac["V"], 1)

                hidden(2, 0)
                with dve.Fori(0, 5) as i:
                    hidden(4, 2, i)
                s0 = 2 * SLOT0[l, "ffn_out"]
                for j in range(4):
                    for half in range(2):
                        update(s0 + 8 * j + 6 + half, 40, 2 * j + half)
            rstd(4, NL)
            for k in range(KD):
                nc.vector.scalar_tensor_tensor(out=X[:, k, 0:NL], in0=X[:, k, 0:NL], scalar=vcol("final_norm", k),
                                               in1=NG[:, 1, 0:NL], op0=ALU.mult, op1=ALU.mult).then_inc(x_upd, 1)

            links = [0]

            def link(ins):
                links[0] += 1
                ins.then_inc(chain, 1)
                dve.wait_ge(chain, links[0])

            def plain_norm(n, name):
                rstd(n, NL)
                for k in range(KD):
                    nc.vector.scalar_tensor_tensor(out=H[:, k, 0:NL], in0=X[:, k, 0:NL], scalar=vcol(name, k),
                                                   in1=NG[:, 1, 0:NL], op0=ALU.mult, op1=ALU.mult).then_inc(h2, 1)

            lam = vcol("lam", 0, 4)
            L = lambda i: lam8[:, i, :]
            nc.vector.scalar_tensor_tensor(out=L(0), in0=lam, scalar=-1.0, in1=lam, op0=ALU.mult, op1=ALU.min)\
                .then_inc(lam_a, 1)
            plain_norm(5, "g_mix")
            dve.wait_ge(lam_e, 1)
            link(nc.vector.tensor_scalar(L(2), L(1), 2.0, None, ALU.add))
            link(nc.vector.reciprocal(L(3), L(2)))
            link(nc.vector.tensor_tensor(L(2), L(1), L(3), ALU.mult))
            link(nc.vector.tensor_tensor(L(3), L(2), L(2), ALU.mult))
            link(nc.vector.tensor_scalar(L(4), L(3), 1.0 / 17, None, ALU.mult))
            for odd in range(15, 1, -2):
                link(nc.vector.scalar_tensor_tensor(out=L(4), in0=L(4), scalar=1.0 / odd, in1=L(3), op0=ALU.add, op1=ALU.mult))
            link(nc.vector.scalar_tensor_tensor(out=L(4), in0=L(4), scalar=1.0, in1=L(2), op0=ALU.add, op1=ALU.mult))
            link(nc.vector.tensor_scalar(L(5), lam, -1.0, 0.0, ALU.mult, ALU.max))
            link(nc.vector.scalar_tensor_tensor(out=L(5), in0=L(4), scalar=2.0, in1=L(5), op0=ALU.mult, op1=ALU.add))
            link(nc.vector.tensor_scalar(L(6), L(5), 8.0, None, ALU.mult))
            nc.vector.tensor_scalar(L(7), L(5), -8.0, None, ALU.mult).then_inc(r_lam, 1)

            s0 = 2 * SLOT0[2, "w_in2"]
            dve.wait_ge(zeroed, 2)
            for t in range(4):
                s = s0 + 2 * t + 1
                dve.wait_ge(steps, s + 1)
                dve.wait_ge(evac["A"], evacuated("A", s))
                nc.vector.tensor_tensor(UC[:, t, TAPS - 1:TAPS - 1 + NL], ps[1][:, 0:NL], RAW[:, t % 2, 0:NL], ALU.mult)\
                    .then_inc(evac["V"], 1)
            dve.wait_ge(evac["V"], evacuated("V", s0 + 7))
            mine = [t for t in range(4) if t not in PE_CONV]
            for d in range(TAPS):
                for n, t in enumerate(mine):
                    src, w = UC[:, t, d:d + NL], vcol("conv_w", 4 * d + t)
                    if d == 0:
                        ins = nc.vector.tensor_scalar(CV[:, t, :], src, w, vcol("conv_b", t), ALU.mult, ALU.add)
                    else:
                        dve.wait_ge(conv_t, len(mine) * (d - 1) + n + 1)
                        ins = nc.vector.scalar_tensor_tensor(out=CV[:, t, :], in0=src, scalar=w, in1=CV[:, t, :],
                                                             op0=ALU.mult, op1=ALU.add)
                    ins.then_inc(conv_t, 1) if d < TAPS - 1 else ins.then_inc(conv_k, 1)
                if d == 19:
                    dve.wait_ge(evac["A"], evacuated("A", s0 + 11))
                    for t in range(4):
                        link(nc.vector.tensor_scalar(XR[:, t, :], XL[:, t, 0:NL], vcol("lru_w", t), vcol("lru_b", t),
                                                     ALU.mult, ALU.add))
                        for e in range(1, LTAPS):
                            ins = nc.vector.scalar_tensor_tensor(out=XR[:, t, :], in0=XL[:, t, e:e + NL],
                                                                 scalar=vcol("lru_w", 4 * e + t), in1=XR[:, t, :],
                                                                 op0=ALU.mult, op1=ALU.add)
                            link(ins) if e < LTAPS - 1 else ins.then_inc(lconv, 1)
            dve.wait_ge(lconv, 4)
            dve.wait_ge(gact, 8)
            for t in range(4):
                dve.wait_ge(lexp, t + 1)
                link(nc.vector.tensor_tensor(LH[:, t, :], LA[:, t, :], LA[:, t, :], ALU.mult))
                nc.vector.scalar_tensor_tensor(out=TH[:, t, :], in0=LH[:, t, :], scalar=1.0, in1=TH[:, t, :],
                                               op0=ALU.add, op1=ALU.mult).then_inc(lm2, 1)
                link(nc.vector.tensor_tensor(LU[:, t, :], LU[:, t, :], XR[:, t, :], ALU.mult))
            for t in range(4):
                dve.wait_ge(lsq, t + 1)
                link(nc.vector.tensor_tensor(LU[:, t, :], LU[:, t, :], TH[:, t, :], ALU.mult))
                link(nc.vector.tensor_tensor_scan(LH[:, t, :], LA[:, t, :], LU[:, t, :], 0.0, ALU.mult, ALU.add))
                nc.vector.tensor_tensor(LH[:, t, :], LH[:, t, :], GL[:, t, :], ALU.mult).then_inc(ylru, 1)
            dve.wait_ge(lnm, 1)
            for t in range(4):
                nc.vector.scalar_tensor_tensor(out=CV[:, t, :], in0=ps[2][:, 0:NL], scalar=-2.0, in1=CV[:, t, :],
                                               op0=ALU.mult, op1=ALU.add).then_inc(lnc, 1)
            dve.wait_ge(lnr, 1)
            link(nc.vector.reciprocal(RAW[:, 0, 0:NL], RAW[:, 0, 0:NL]))
            for t in range(4):
                dve.wait_ge(lns, t + 1)
                nc.vector.tensor_tensor(CV[:, t, :], CV[:, t, :], RAW[:, 0, 0:NL], ALU.mult).then_inc(lnn, 1)
            for m in range(KD):
                s = 2 * SLOT0[2, "w_out2"] + m
                dve.wait_ge(steps, s + 1)
                nc.vector.tensor_tensor(X[:, m, 0:NL], ps[s % 2][:, 0:NL], X[:, m, 0:NL], ALU.add).then_inc(evac["V"], 1)
            plain_norm(6, "g_ffn")

            def r3(ap, n):
                return ap.rearrange("p (c n) -> p c n", n=n)

            def over(ap, n):
                return ap[:, :, None].to_broadcast([P, ap.shape[1], n])

            eidx = cst[:, CST["eidx"]:CST["eidx"] + NE]
            LG, EM, EQU = rtile(0, 4, NR), rtile(144, 4, NE), rtile(272, 4, NE)
            CAND, OH1, OH2 = rtile(400, 4, NE), rtile(528, 4, NE), rtile(656, 4, NE)
            g4 = rtile(784, 4, NG4)
            GEQ, GCAND, GHOT, GSH = (rtile(800 + 16 * i, 4, NG4) for i in range(4))
            col4 = [scr[:, 880 + 4 * i:884 + 4 * i] for i in range(8)]
            gmax, gbest, gsum, m1, b1, m2, dif, den = col4

            def hottest(hot, vals, eq, cand, top, best, n):
                link(nc.vector.tensor_reduce(top, vals, AX.X, ALU.max))
                link(nc.vector.tensor_tensor(eq, vals, over(top, n), ALU.is_equal))
                idx = eidx[:, 0:n][:, None, :].to_broadcast([P, 4, n])
                link(nc.vector.scalar_tensor_tensor(out=cand, in0=eq, scalar=100.0, in1=idx, op0=ALU.mult,
                                                    op1=ALU.subtract))
                link(nc.vector.tensor_reduce(best, cand, AX.X, ALU.max))
                link(nc.vector.tensor_tensor(hot, cand, over(best, n), ALU.is_equal))

            dve.wait_ge(rl, 1)
            dve.wait_ge(r_in, 32)
            link(nc.vector.tensor_tensor(LG, r3(ps[3][:, 0:256], 64)[:, :, 0:NR],
                                         rb[:, None, :].to_broadcast([P, 4, NR]), ALU.add))
            link(nc.vector.tensor_copy(g4, LG[:, :, 0:NG4]))
            hottest(GHOT, g4, GEQ, GCAND, gmax, gbest, NG4)
            nc.vector.tensor_tensor(GSH, g4, over(gmax, NG4), ALU.subtract).then_inc(re1, 1)
            link(nc.vector.tensor_scalar(GEQ, GHOT, 1e30, -1e30, ALU.mult, ALU.add))
            for g in range(NG4):
                link(nc.vector.tensor_tensor(EM[:, :, 8 * g:8 * g + 8], LG[:, :, NG4 + 8 * g:NG4 + 8 * g + 8],
                                             GEQ[:, :, g:g + 1].to_broadcast([P, 4, 8]), ALU.add))
            hottest(OH1, EM, EQU, CAND, m1, b1, NE)
            link(nc.vector.scalar_tensor_tensor(out=EM, in0=OH1, scalar=-3e30, in1=EM, op0=ALU.mult, op1=ALU.add))
            hottest(OH2, EM, EQU, CAND, m2, b1, NE)
            mask = r3(SEL[:, 0:128], NE)
            nc.vector.tensor_tensor(mask, OH1, OH2, ALU.add).then_inc(r_mask, 1)
            nc.vector.tensor_tensor(dif, m2, m1, ALU.subtract).then_inc(re1, 1)
            for c in range(4):
                dve.wait_ge(ht, c + 1)
                nc.vector.tensor_copy(htok_half(c, 1), ps[c % 3][:, 512:1024].rearrange("p (a b) -> p a b", a=2))\
                    .then_inc(htk_v, 1)

            dve.wait_ge(re2, 2)
            link(nc.vector.tensor_reduce(gsum, GSH, AX.X, ALU.add))
            link(nc.vector.tensor_scalar(den, dif, 1.0, None, ALU.add))
            link(nc.vector.tensor_tensor(gsum, gsum, den, ALU.mult))
            link(nc.vector.reciprocal(m1, gsum))
            link(nc.vector.tensor_tensor(m2, m1, dif, ALU.mult))
            link(nc.vector.tensor_tensor(OH1, OH1, over(m1, NE), ALU.mult))
            link(nc.vector.tensor_tensor(OH2, OH2, over(m2, NE), ALU.mult))
            link(nc.vector.tensor_tensor(gate[:, :, :], OH1, OH2, ALU.add))
            dve.wait_ge(r_pos, 1)
            link(nc.vector.scalar_tensor_tensor(out=pos[:, :, :], in0=r3(ps[3][:, 0:128], NE), scalar=1.0, in1=mask,
                                                op0=ALU.add, op1=ALU.mult))
            link(nc.vector.tensor_scalar(pos[:, :, :], pos[:, :, :], -1.0, None, ALU.add))
            cnt = scr[:, 912:944]
            link(nc.vector.tensor_copy(cnt, ps[3][:, 128:160]))
            link(nc.vector.tensor_reduce(gmax[:, 0:1], cnt, AX.X, ALU.max))
            passes = scr[:, 944:952]
            link(nc.vector.tensor_scalar(passes, cst[:, CST["iota"]:CST["iota"] + 8], float(CAP), None, ALU.mult))
            link(nc.vector.tensor_tensor(passes, passes, gmax[:, 0:1].to_broadcast([P, 8]), ALU.is_lt))
            link(nc.vector.tensor_reduce(gmax[:, 1:2], passes, AX.X, ALU.add))
            link(nc.vector.tensor_scalar(gmax[:, 2:3], gmax[:, 1:2], float(PAIRS), None, ALU.mult))
            nc.vector.tensor_copy(total_i[:, :], gmax[:, 2:3]).then_inc(r_ok, 1)

            dve.wait_ge(r_ok, 1)
            total = dve.value_load(total_i[0:1, 0:1], min_val=PAIRS, max_val=PAIRS * (NL // CAP))
            iota = cst[:, CST["iota"]:CST["iota"] + CAP]
            sel4 = SEL.rearrange("p (c x n) -> p c x n", c=4, x=2)
            selg4 = SELG.rearrange("p (c x n) -> p c x n", c=4, x=2)
            shape4 = [P, 4, 2, CAP]

            def select(j, first=False):
                two = pos[:, :, ds(2 * j, 2)] if not first else pos[:, :, 0:2]
                wts = gate[:, :, ds(2 * j, 2)] if not first else gate[:, :, 0:2]
                nc.vector.tensor_tensor(sel4, iota[:, None, None, :].to_broadcast(shape4),
                                        two[:, :, :, None].to_broadcast(shape4), ALU.is_equal).then_inc(m_eq, 1)
                return two, wts

            two, wts = select(0, True)
            dve.wait_ge(m_eq, 1)
            nc.vector.tensor_tensor(selg4, sel4, wts[:, :, :, None].to_broadcast(shape4), ALU.mult).then_inc(m_sel, 1)
            nc.vector.tensor_scalar(two, two, -float(CAP), None, ALU.add).then_inc(m_add, 1)
            with dve.Fori(0, total) as i:
                dve.wait_ge(m_xg, i + 1)
                nc.vector.tensor_copy(scr[:, 512:1024], ps[0][:, 512:1024]).then_inc(m_xgv, 1)
                dve.wait_ge(m_selt, i + 1)
                two, wts = select((i + 1) % PAIRS)
                dve.wait_ge(m_eq, i + 2)
                nc.vector.tensor_tensor(selg4, sel4, wts[:, :, :, None].to_broadcast(shape4), ALU.mult).then_inc(m_sel, 1)
                nc.vector.tensor_scalar(two, two, -float(CAP), None, ALU.add).then_inc(m_dec, 1)
                dve.wait_ge(m_act, i + 1)
                dve.wait_ge(m_steps, 12 * i + 8)
                nc.vector.tensor_tensor(GH, ps[1][:, 512:1024], SGM, ALU.mult).then_inc(m_g, 1)
                dve.wait_ge(m_steps, 12 * i + 12)
                nc.vector.tensor_copy(YS[:, 512:1024], ps[2][:, 512:1024]).then_inc(m_ysv, 1)
                for m in range(KD):
                    dve.wait_ge(m_sc, 8 * i + (m + 1))
                    nc.vector.tensor_tensor(X[:, m, 0:NL], ps[0][:, 512 * (m % 2):512 * (m % 2) + 512], X[:, m, 0:NL],
                                            ALU.add).then_inc(m_add, 1)

            dve.wait_ge(m_add, 8 * total + 1)
            plain_norm(7, "g_ple")
            dve.wait_ge(e_rt, 1)
            link(nc.vector.reciprocal(RE, RE))
            dve.wait_ge(e_k, 8)
            for m in range(KD):
                nc.vector.scalar_tensor_tensor(out=EB[:, m, :], in0=EB[:, m, :], scalar=vcol("g_proj", m), in1=RE,
                                               op0=ALU.mult, op1=ALU.mult).then_inc(e_ok, 1)
            for m in range(KD):
                dve.wait_ge(pg_a, m + 1)
                dve.wait_ge(e_ok, m + 1)
                link(nc.vector.tensor_tensor(PG[:, m % 2, :], PG[:, m % 2, :], EB[:, m, :], ALU.mult))
                nc.vector.tensor_tensor(X[:, m, 0:NL], X[:, m, 0:NL], PG[:, m % 2, :], ALU.add).then_inc(x_upd, 1)
            rstd(8, NL)
            for k in range(KD):
                nc.vector.scalar_tensor_tensor(out=X[:, k, 0:NL], in0=X[:, k, 0:NL], scalar=vcol("g_final", k),
                                               in1=NG[:, 1, 0:NL], op0=ALU.mult, op1=ALU.mult).then_inc(x_upd, 1)


def slots(w):
    k, n = w.shape
    return w.reshape(k // P, P, n // 256, 256).transpose(2, 1, 0, 3).reshape(n // 256, P, -1)


def lay_out(x):
    f = np.float32
    z = np.zeros((N_STREAM, P, SLOT), f)

    def put(l, name, blocks):
        n = SLOT0[l, name]
        for b in blocks:
            z[n:n + b.shape[0], :, :b.shape[2]] = b
            n += b.shape[0]

    for l in range(LAYERS):
        wm, w = x["w_mod"][l], x["w_in"][l]
        if l == 0:
            put(0, "mod_head", [slots(wm[:, :2048])])
            put(0, "mod_rest", [slots(wm[:, 2048:]), slots(x["w_mod"][1][:, :2048])])
        else:
            put(1, "mod_rest", [slots(wm[:, 2048:])])
        naq, nak, nav, gq, gk, gv, ga, gb = np.split(w, np.cumsum([512, 512, 512, 512, 128, 128, 1024]), axis=1)
        order = [h for t in range(4) for h in (t, t + 4)]
        gq = gq.reshape(D, 8, HD)[:, order].reshape(D, 512)
        put(l, "gq", [slots(gq)])
        put(l, "gkv", [slots(np.concatenate([gk, gv], axis=1))])
        put(l, "nak", [slots(nak)])
        put(l, "naq", [slots(naq)])
        put(l, "nav", [slots(nav)])
        ga, gb, pa = slots(ga), slots(gb), slots(x["w_pa"][l])
        pb = slots(x["w_pb"][l].reshape(8, HD, D)[order].reshape(512, D))
        put(l, "merge", [b[j:j + 1] for j in range(4) for b in (ga, pa, gb, pb)])
        put(l, "w_o", [slots(x["w_o"][l])])
        wf = x["w_ffn_in"][l].reshape(D, 2, KF, P).transpose(0, 2, 1, 3).reshape(D, KF * 256)
        put(l, "ffn_in", [slots(wf)])
        wo = x["w_ffn_out"][l]
        put(l, "ffn_out", [slots(wo[a * P:b * P, 256 * j:256 * j + 256]) for j in range(4) for a, b in FFQ])

    v = np.zeros((P, NV), f)

    def col(name, a):
        a = np.asarray(a).reshape(-1, P).T
        v[:, VEC[name]:VEC[name] + a.shape[1]] = a

    v[:, VEC["c2"]:VEC["c2"] + 16:2] = x["c"].reshape(KD, P).T
    v[:, VEC["c2"] + 1:VEC["c2"] + 16:2] = x["c_ctx"].reshape(KD, P).T
    for l in range(LAYERS):
        for name in ("norm1", "norm2", "b_mod"):
            col(f"{name}{l}", x[name][l])
        for name in ("q_gain", "k_gain"):
            col(f"{name}{l}", np.tile(x[name][l], 2))
    col("final_norm", x["final_norm"])

    for name, src in (("g_mix", "g_mix"), ("conv_b", "conv_dw_b"), ("ln_g", "conv_ln_g"), ("ln_b", "conv_ln_b"),
                      ("conv_w", "conv_dw_w"), ("lru_w", "lru_conv_w"), ("lru_b", "lru_conv_b"), ("b_r", "lru_b_r"),
                      ("b_i", "lru_b_i"), ("lam", "lru_lambda"), ("g_ffn", "g_ffn"), ("g_ple", "g_ple"),
                      ("g_proj", "g_ple_proj")):
        col(name, x[src + "_2"][0])
    col("g_final", x["g_final_2"])

    w = x["w_in_2"][0].reshape(D, 4, 4, P)
    put(2, "w_in2", [slots(np.stack([w[:, 1], w[:, 0]], axis=2).reshape(D, D)), slots(w[:, 2:].reshape(D, D))])
    put(2, "w_out2", [slots(x["w_out_2"][0])])

    def chunks(w, rows, per):
        w = w.reshape(PAIRS, 2, rows // P // per, per, P, -1).transpose(0, 2, 1, 4, 3, 5)
        return w.reshape(PAIRS, -1, P, SLOT)

    experts = np.concatenate([chunks(x["w1_2"][0], D, 4), chunks(x["w3_2"][0], D, 4), chunks(x["w2_2"][0], D // 2, 2)],
                             axis=1)
    router = np.concatenate([x["w_group_2"][0], x["w_expert_2"][0]], axis=1)
    router = router.reshape(KD, P, NR).transpose(1, 0, 2).reshape(P, KD * NR)
    router_b = np.concatenate([x["b_group_2"][0], x["b_expert_2"][0]])[None].repeat(P, axis=0)

    def by_rows(a):
        return a.reshape(-1, P, a.shape[-1]).transpose(1, 0, 2).reshape(P, -1)

    pad = np.zeros((LAYERS, 8, 15, 128), f)
    pad[..., 48:79] = x["na_rpb"]
    return {"stream": z, "vecs": v, "consts": constants(), "xT": np.ascontiguousarray(x["x"][0].T),
            "ctxT": np.ascontiguousarray(x["ctx"][0].T), "rpb": pad, "experts": experts,
            "router": router, "router_b": router_b, "lru_w": np.concatenate([x["lru_w_r_2"], x["lru_w_i_2"]]),
            "w_ple": by_rows(x["w_ple_2"][0]), "pT": by_rows(x["p_2"][0, 0].T), "w_gate": slots(x["w_ple_gate_2"][0])}


def constants():
    f = np.float32
    c = np.zeros((P, NCST), f)
    i = np.arange(P)
    c[:, 0:128] = np.eye(P)
    c[:, 128:256] = 1.0 / D
    c[:, 256:384] = (i[:, None] // HD == i[None, :] // HD) / HD
    c[i[1::2], 384 + i[0::2]] = -1
    c[i[0::2], 384 + i[1::2]] = 1
    t = np.arange(NL)
    half = HD // 2
    inv = (f(10000.0) ** (-np.arange(0, half, 2, dtype=f) / f(half))).astype(f)
    ang = np.concatenate([(t // GRID).astype(f)[:, None] * inv, (t % GRID).astype(f)[:, None] * inv], axis=1)
    pair = (i % HD) // 2
    c[:, CST["cos"]:CST["cos"] + NL] = np.cos(ang).T[pair]
    c[:, CST["sin"]:CST["sin"] + NL] = np.sin(ang).T[pair]
    w = i % GRID
    u = np.arange(GRID)
    start = np.clip(w - 8, 0, GRID - 16)[:, None]
    c[:, CST["namask"]:CST["namask"] + GRID] = np.where((u >= start) & (u < start + 16), 0, -1e30)
    c[:, CST["iota"]:CST["iota"] + HD] = u
    c[:, CST["one"]:CST["one"] + P] = 1
    c[:, CST["eidx"]:CST["eidx"] + NR] = np.arange(NR)
    for j in range(2):
        c[j::32, CST["fold"] + j] = 1
    c[:, CST["tri"]:CST["tri"] + P] = i[:, None] < i[None, :]
    return c


def kernel(**inputs):
    import concourse.bacc as bacc
    from concourse.bass_utils import run_bass_kernel_spmd

    nc = bacc.Bacc("TRN2", target_bir_lowering=False, num_devices=1)
    arrays = lay_out({k: np.asarray(a) for k, a in inputs.items()})
    fp32 = mybir.dt.float32
    aps = {n: nc.dram_tensor(n, a.shape, fp32, kind="ExternalInput").ap() for n, a in arrays.items()}
    outT = nc.dram_tensor("outT", (D, NL), fp32, kind="ExternalOutput").ap()
    build(nc, out=outT, **aps)
    r = run_bass_kernel_spmd(nc, [arrays], core_ids=[0])
    return np.ascontiguousarray(r.results[0]["outT"].T)[None]
```

```python
import concourse.bass as bass
from concourse import mybir
from contextlib import ExitStack
import numpy as np

P = 128
D = 1024
KD = D // P
NL, NC = 512, 256
T = NL + NC
LAYERS = 2
FF = 2816
KF = FF // P
HD = 64
GRID = 64
EPS = 1e-6
QSCALE = HD ** -0.5

RING = 2
SLOT = KD * 256
KH = KF // 2
FFQ = (6, KH - 6)


def layer_slots(l):
    first = [("mod_head", 8)] if l == 0 else []
    return first + [("gq", 2), ("gkv", 1), ("nak", 2), ("naq", 2), ("nav", 2),
                    ("mod_rest", 24 if l == 0 else 16),
                    ("merge", 16), ("w_o", 4), ("ffn_in0", KH), ("ffn_out0", 8), ("ffn_in1", KH), ("ffn_out1", 8)]


WIDTHS = {"merge": (8, 4), "ffn_out0": FFQ, "ffn_out1": FFQ}
EVACUATION = {"mod_head": "-", "mod_rest": "-", "merge": "AAVVAAVV", "w_o": "V", "ffn_in0": "AV", "ffn_in1": "AV",
              "ffn_out0": "--VV", "ffn_out1": "--VV", "w_in2": "AVAVAVAVAAAAAAAA", "w_out2": "V"}
DIRECT = ("mod_head", "mod_rest")

SLOT0 = {}
CHUNKS = []
EVACUATES = ""
SPLIT = []
for _l in range(LAYERS + 1):
    for _name, _count in layer_slots(_l) if _l < LAYERS else [("w_in2", 8), ("w_out2", 4)]:
        SLOT0[_l, _name] = len(CHUNKS)
        _widths, _who = WIDTHS.get(_name, (KD,)), EVACUATION.get(_name, "A")
        CHUNKS += [_widths[_i % len(_widths)] for _i in range(_count)]
        EVACUATES += "".join(_who[_i % len(_who)] for _i in range(2 * _count))
        SPLIT += [_name not in DIRECT] * (2 * _count)
N_STREAM = len(CHUNKS)


def evacuated(who, s):
    return EVACUATES[:s + 1].count(who)


def previous_user(s):
    for q in range(s - 2, -1, -2):
        if EVACUATES[q] != "-":
            return EVACUATES[q], evacuated(EVACUATES[q], q)
    return None


def splits(s):
    return sum(SPLIT[:s + 1])


def is_split(s):
    return s < len(SPLIT) and SPLIT[s]


VEC = {}
_v = 0


def _vec(name, n):
    global _v
    VEC[name] = _v
    _v += n


_vec("c2", 16)
for _l in range(LAYERS):
    for _name, _count in [("norm1", 8), ("norm2", 8), ("b_mod", 48), ("q_gain", 1), ("k_gain", 1)]:
        _vec(f"{_name}{_l}", _count)
_vec("final_norm", 8)
for _name, _count in [("g_mix", 8), ("conv_w", 124), ("conv_b", 4), ("ln_g", 4), ("ln_b", 4), ("lru_w", 16),
                      ("lru_b", 4), ("b_r", 4), ("b_i", 4), ("lam", 4), ("g_ffn", 8), ("g_ple", 8),
                      ("g_proj", 8), ("g_final", 8)]:
    _vec(_name, _count)
NV = _v

CST = {"ident": 0, "ones": 128, "blk": 256, "rot": 384, "cos": 512, "sin": 1024, "namask": 1536, "iota": 1600,
       "tri": 1664, "one": 1792, "eidx": 1920, "fold": 1956}
NCST = 1956 + 2


def attention_units(l):
    return [(na, t, qb, half) for na in (True, False) for t in range(4)
            for qb in range(6 if l == 0 else 4) for half in range(2)]


TAPS, LTAPS = 31, 4
SHORT_AT, RECURRENCE_AT = 12, 27
PE_CONV = (3,)
NG4, NE = 4, 32
CAP = 64
PAIRS = NE // 2
NR = NG4 + NE


def build(nc, stream, vecs, consts, xT, ctxT, rpb, experts, router, router_b, lru_w, w_ple, pT, w_gate, out):
    fp32 = mybir.dt.float32
    f32r = mybir.dt.float32r
    ALU = mybir.AluOpType
    ACT = mybir.ActivationFunctionType
    AX = mybir.AxisListType
    ds = bass.ds

    es = ExitStack()
    with es:
        def sb(name, shape):
            return es.enter_context(nc.sbuf_tensor(name, shape, fp32))

        def sem(name):
            return es.enter_context(nc.semaphore(name))

        rows = nc.dram_tensor("bias_rows", (LAYERS * 120, GRID, 128), fp32, kind="Internal").ap()
        rows_in = sem("bias_rows_copied")
        X = sb("X", [P, KD, T])

        def at(name, first, size, dtype=fp32):
            with ExitStack() as place:
                if first:
                    place.enter_context(nc.sbuf_tensor(f"below_{name}", [P, first], fp32))
                return place.enter_context(nc.sbuf_tensor(name, [P, size], dtype))

        B0 = 16384
        ring = at("ring", 0, RING * SLOT).rearrange("p (r n) -> p r n", n=SLOT)
        h_parts = at("h_parts", 4096, 2 * KD * T, f32r)
        B = at("first_block", B0, 26112)
        BR = at("half_slots", B0 + 22016, 4 * D, f32r)
        y_parts = at("y_parts", B0 + 9216, 2 * KD * T, f32r)
        kn_low, kg_low = at("na_k_lower", B0, 4 * T, f32r), at("gqa_k_lower", B0 + 9216, T, f32r)
        g_parts = at("hidden_parts", B0 + 4608, 2 * KH * T, f32r)
        scr = at("scratch", 0, 8192)
        h_plain = at("h_plain", 8192, KD * T)
        UW = at("second_block", 14336, 28160)
        half_slots2 = at("half_slots2", 4096, 4 * D, f32r)
        h2_parts = at("h2_parts", 14336 + 10384, 2 * KD * NL, f32r)
        mix_up, mix_low = at("mixed_upper", 14336, KD * NL, f32r), at("mixed_lower", 14336 + 8336, KD * NL, f32r)
        m_parts = at("expert_parts", 8192, KD * T, f32r)
        es.enter_context(nc.sbuf_tensor("common_memory", [P, 42496], fp32))
        gate = sb("gate", [P, 4, NE])
        pos = sb("pos", [P, 4, NE])
        total_i = nc.sbuf_tensor("total_i", [P, 1], mybir.dt.int32)
        total_i = es.enter_context(total_i)
        lam8 = sb("lam8", [P, 8, 4])
        vec = sb("vec", [P, NV])
        cst = sb("cst", [P, NCST])
        sc2 = sb("sc2", [P, KD, 32])
        mrow = sb("mod_rows", [P, 256])
        mod = sb("mod", [P, LAYERS * 48, 2])
        amod = sb("amod", [P, LAYERS * 2, KD, 2])
        inv = sb("inverse_sums", [P, 2, P])
        small = sb("small", [P, 4, 8])
        qg8 = sb("qg8", [P, LAYERS])
        epsc = sb("epsc", [P, 1])
        q_parts = es.enter_context(nc.sbuf_tensor("q_parts", [P, 4, P], f32r))
        rms = sb("rms", [P, 6])

        def view(t, at, *shape):
            n = int(np.prod(shape))
            ap = t[:, at:at + n]
            return ap.rearrange("p (a b) -> p a b", b=shape[-1]) if len(shape) == 2 else ap

        HS = [view(h_parts, i * KD * T, KD, T) for i in range(2)]
        SR = [view(BR, i * 2 * D, 2, D) for i in range(2)]
        KU = view(BR, 0, 5, T)
        KL = [view(kn_low, 0, 4, T)[:, t, :] for t in range(4)] + [kg_low[:, :]]
        KNA, Y = view(B, 0, 4, T), view(B, 3072, 8, T)
        QNA, QG = view(B, 3072, 4, T), view(B, 6144, 4, T)
        KG = view(B, 9216, 1, T)
        V = view(B, 9984, 6, 640)
        RAWH, SQH, NGH, CGH = (view(B, 13824 + i * 1536, 2, T) for i in range(4))
        PB = view(B, 13824, 3, T)
        PT = view(B, 13824 + 3 * T, 3, T)
        BIAS = view(B, 13824 + 6 * T, 4, 14 * GRID)
        YS2 = [view(y_parts, i * KD * T, KD, T) for i in range(2)]
        M = Y
        MS2 = YS2
        RAW, SQ, CG = view(B, 0, 2, T), view(B, 1536, 2, T), view(B, 3072, 2, T)
        NG = SQ
        TM = view(B, 4608, 4, T)
        GS = [view(g_parts, i * KH * T, KH, T) for i in range(2)]
        RAW2, NG2, CG2 = view(UW, 19968, 2, T), view(UW, 24576, 2, T), view(UW, 26112, 2, T)
        H = view(h_plain, 0, KD, T)
        SR2 = [view(half_slots2, i * 2 * D, 2, D) for i in range(2)]
        H2 = [view(h2_parts, i * KD * NL, KD, NL) for i in range(2)]
        MIX = [view(mix_up, 0, KD, NL), view(mix_low, 0, KD, NL)]

        ps = [es.enter_context(nc.psum_tensor(f"ps{i}", [P, 1024], fp32)) for i in range(4)]

        ident = cst[:, 0:128]
        onesm = cst[:, CST["ones"]:CST["ones"] + P]
        ones1 = cst[:, CST["one"]:CST["one"] + P]
        tri = cst[:, CST["tri"]:CST["tri"] + P]
        blk = cst[:, CST["blk"]:CST["blk"] + P]
        rot = cst[:, CST["rot"]:CST["rot"] + P]
        cosT = cst[:, CST["cos"]:CST["cos"] + NL]
        sinT = cst[:, CST["sin"]:CST["sin"] + NL]
        fold = cst[:, CST["fold"]:CST["fold"] + 2]
        namask = cst[:, CST["namask"]:CST["namask"] + GRID]

        def vcol(name, i=0, n=1):
            return vec[:, VEC[name] + i:VEC[name] + i + n]

        loaded = [sem(f"slot{r}_loaded") for r in range(RING)]
        steps = sem("steps_done")
        evac = {"A": sem("scalar_evacuated"), "V": sem("vector_evacuated")}
        inputs = sem("inputs_loaded")
        x_loaded = sem("x_loaded")
        silu_done = sem("silu_done")
        mod_ready = sem("mod_ready")
        x_upd = sem("x_updated")
        squared = sem("squared")
        summed = sem("squares_summed")
        ms_ready = sem("mean_square_ready")
        spread = sem("rstd_spread")
        rooted = sem("rms_rooted")
        rstd_ok = sem("rstd_ready")
        normed = sem("x_times_rstd")
        hi_done = sem("upper_parts_ready")
        lo_done = sem("both_parts_ready")
        h_sum = sem("h_odd_tiles")
        h_hi, h_lov, h_lop = sem("h_upper"), sem("h_lower_even"), sem("h_lower_odd")
        y_hi, y_lo = sem("y_or_m_upper"), sem("y_or_m_lower")
        gs_hi, gs_lo = sem("hidden_upper"), sem("hidden_lower")
        k_hi, k_lo, q_hi, q_lo = sem("keys_upper"), sem("keys_lower"), sem("queries_upper"), sem("queries_lower")
        p_hi, p_lov, p_lop = sem("plain_h_upper"), sem("plain_h_lower_even"), sem("plain_h_lower_odd")
        mix_hi, mix_lo = sem("mixed_upper_ready"), sem("mixed_lower_ready")
        v_t, v_k = sem("v_turned"), sem("v_kept")
        g_sq = sem("head_squares")
        g_ms = sem("head_mean_square")
        g_rt = sem("head_rooted")
        g_rr = sem("head_rstd")
        g_n = sem("head_normed")
        g_rot = sem("head_rotated")
        g_cos = sem("head_cos")
        g_sin = sem("head_sin")
        g_q = sem("head_roped")
        bias_in = [sem(f"bias_in{i}") for i in range(4)]
        bias_ok = sem("bias_ready")
        s_sc, s_m1 = sem("scores_done"), sem("bias_added")
        s_mx = sem("max_ready")
        s_exp, s_tr, s_pta, s_ptb = sem("exp_done"), sem("turned"), sem("turned_kept_a"), sem("turned_kept_b")
        s_pv, s_ri, s_dg, s_y = sem("pv_done"), sem("rowsum_inverse"), sem("inverse_diagonal"), sem("y_kept")
        mod_kept, mod_turned, sc_zero = sem("mod_rows_kept"), sem("mod_turned"), sem("c_zeroed")
        merged = sem("merged_ready")
        mod_sum = sem("mod_summed")
        small_q = sem("query_gain_ready")
        small_ok = sem("small_ready")
        xo = sem("x_out")

        UC = view(UW, 0, 4, TAPS - 1 + NL)
        XL = view(UW, 2176, 4, LTAPS - 1 + NL)
        GL = view(UW, 4240, 4, NL)
        CV = view(UW, 6288, 4, NL)
        XR = view(UW, 8336, 4, NL)
        LA = view(UW, 10384, 4, NL)
        LU = view(UW, 12432, 4, NL)
        LH = view(UW, 14480, 4, NL)
        TH = view(UW, 16528, 4, NL)
        WB = UW[:, 23040:24064].rearrange("p (g t n) -> p g t n", g=2, t=4)
        DG = UW[:, 21504:23040].rearrange("p (i n) -> p i n", n=P)
        NDG = 12
        MR = UW[:, 0:12 * SLOT].rearrange("p (q n) -> p q n", n=SLOT)
        XG = view(scr, 0, KD, 2 * CAP)
        SEL, SELG, SELT, GH = (scr[:, 1024 + 512 * i:1536 + 512 * i] for i in range(4))
        GT = view(scr, 3072, 4, 2 * CAP)
        mp = m_parts.rearrange("p (a b) -> p a b", b=T)
        PICK = mp[:, 0, 0:NL]
        YP = [mp[:, 2 + 2 * i:4 + 2 * i, 0:NL] for i in range(2)]
        WP = view(scr, 5120, 2, D)
        PTT = view(scr, 7168, 2, NL)
        SGM = UW[:, 27648:28160]
        EB = view(UW, 8192, KD, NL)
        EQ = view(UW, 14336, KD, NL)
        PG = view(UW, 12288, 2, NL)
        RE = UW[:, 13312:13824]
        wslot = sb("wslot", [P, 1])
        WR = sb("wr", [P, KD, NR])
        rb = sb("rb", [P, NR])

        def htok(c, k):
            if c < 3:
                at = 19968 + 4608 + c * D + k * P
                return UW[:, at:at + P]
            return H[:, k // 2, NL + (k % 2) * P:NL + (k % 2 + 1) * P]

        def htok_half(c, q):
            if c < 3:
                at = 19968 + 4608 + c * D + q * 4 * P
                return UW[:, at:at + 4 * P].rearrange("p (a b) -> p a b", a=2)
            return H[:, 2 * q:2 * q + 2, NL:NL + 2 * P]

        zeroed = sem("pads_zeroed")
        wb_in, wb_zero = sem("lru_weights_in"), sem("lru_weights_zeroed")
        chain = sem("vector_chain")
        lam_e, lam_a = sem("lambda_exp"), sem("lambda_abs")
        h2 = sem("plain_h_ready")
        conv_t = sem("conv_taps")
        conv_p, conv_k = sem("conv_products"), sem("conv_kept")
        diag, lconv = sem("diagonals"), sem("short_conv_ready")
        gpe, gact = sem("lru_gate_products"), sem("lru_gates_ready")
        lth, lexp, lm2, lsq = sem("lru_tanh"), sem("lru_decay"), sem("lru_square"), sem("lru_root")
        ylru, lnm, lnc, lns = sem("lru_branch_ready"), sem("ln_mean"), sem("ln_centred"), sem("ln_squares")
        lnv, lnr, lnn, yconv = sem("ln_variance"), sem("ln_rooted"), sem("ln_normed"), sem("conv_branch_ready")
        r_in, rl, re1, re2 = sem("router_in"), sem("route_logits"), sem("route_exp_in"), sem("route_exp")
        r_mask, r_pos, r_ok = sem("route_mask"), sem("route_positions"), sem("route_ready")
        ht, htk_a, htk_v = sem("tokens_turned"), sem("tokens_kept_a"), sem("tokens_kept_v")
        m_load = [sem(f"expert_slot{q}_loaded") for q in range(12)]
        m_steps = sem("expert_slots_used")
        m_sel, m_selt = sem("selection_ready"), sem("selection_turned")
        m_w, m_pick = sem("slot_weights_ready"), sem("picks_ready")
        m_xg, m_xga, m_xgv = sem("tokens_gathered"), sem("gathered_kept_a"), sem("gathered_kept_v")
        m_act, m_g, m_gt, m_gk = sem("expert_silu"), sem("expert_hidden"), sem("hidden_turned"), sem("hidden_kept")
        m_ysa, m_ysv = sem("expert_out_kept_a"), sem("expert_out_kept_v")
        m_sc, m_add = sem("scattered"), sem("added_to_x")
        p_in, e_pe, e_k, e_sq, e_ms = sem("ple_in"), sem("e_products"), sem("e_kept"), sem("e_squares"), sem("e_mean")
        e_rt, e_ok = sem("e_rooted"), sem("e_ready")
        pg_pe, pg_a, pg_in = sem("ple_gate_product"), sem("ple_gate"), sem("ple_gate_loaded")
        m_eq, m_dec, r_lam = sem("places_found"), sem("places_lowered"), sem("lambda_ready")

        def rtile(at, a, b):
            return scr[:, at:at + a * b].rearrange("p (a b) -> p a b", b=b)

        rexp = [scr[:, 848:864], scr[:, 904:908]]

        block = es.enter_context(nc.Block())

        def pieces(nt):
            return [(a, min(a + 512, nt)) for a in range(0, nt, 512)]

        NGS = {n: NG if n < 5 else NG2 for n in range(9)}
        CGS = {n: CG if n < 5 else CG2 for n in range(9)}
        U0 = [0, len(attention_units(0))]

        def updating_step(n, m):
            if n % 2:
                return 2 * SLOT0[n // 2, "w_o"] + m
            return 2 * SLOT0[n // 2 - 1, "ffn_out1"] + 4 * (m // 2) + 2 + m % 2

        def raw_half(s):
            n = s // 2
            w = ring[:, n % RING, 0:CHUNKS[n] * 256].rearrange("p (k n) -> p k n", n=256)
            return w[:, :, (s % 2) * P:(s % 2 + 1) * P]

        def part(x, s):
            place = (SR, SR2)[s >= 2 * SLOT0[2, "w_in2"]]
            return place[x][:, s % 2, 0:CHUNKS[s // 2] * P].rearrange("p (k n) -> p k n", n=P)

        def ev(who, s, per=0, i=0):
            if isinstance(i, int):
                return evacuated(who, s + per * i)
            return (evacuated(who, s + per) - evacuated(who, s)) * i + evacuated(who, s)


        @block.sync
        def _(sp):
            def load(n, i=0):
                m = n - RING
                if m >= 0 and SPLIT[2 * m]:
                    sp.wait_ge(lo_done, 8 * i + splits(2 * m + 1))
                elif m >= 0:
                    sp.wait_ge(steps, 8 * i + (2 * m + 2))
                k = CHUNKS[n]
                sp.dma_start(ring[:, n % RING, 0:k * 256],
                             stream[ds(4 * i + n, 1), :, 0:k * 256].rearrange("a p n -> p (a n)"))\
                  .then_inc(loaded[n % RING], 16)

            def load_phase(n0, count):
                for n in range(n0, n0 + min(count, 4)):
                    load(n)
                rounds = count // 4 - 1
                if rounds > 0:
                    with sp.Fori(1, 1 + rounds) as i:
                        for n in range(n0, n0 + 4):
                            load_at(n, i)
                for n in range(n0 + 4 + 4 * max(rounds, 0), n0 + count):
                    load(n)

            def load_at(n, i):
                m = n + 4 - RING
                if SPLIT[2 * m]:
                    sp.wait_ge(lo_done, 8 * i + (splits(2 * m + 1) - 8))
                else:
                    sp.wait_ge(steps, 8 * i + (2 * m - 6))
                k = CHUNKS[n]
                sp.dma_start(ring[:, n % RING, 0:k * 256],
                             stream[ds(4 * i + n, 1), :, 0:k * 256].rearrange("a p n -> p (a n)"))\
                  .then_inc(loaded[n % RING], 16)

            for l in range(LAYERS):
                for name, count in layer_slots(l):
                    load_phase(SLOT0[l, name], count)
            load_phase(SLOT0[2, "w_in2"], 8)
            load_phase(SLOT0[2, "w_out2"], 4)
            sp.wait_ge(steps, 2 * N_STREAM)
            for q in range(12):
                sp.dma_start(MR[:, q, :], experts[0, q]).then_inc(m_load[q], 16)
            sp.dma_start(scr[:, 5120:7168], w_ple).then_inc(p_in, 16)
            sp.dma_start(scr[:, 7168:8192], pT).then_inc(p_in, 16)
            sp.wait_ge(r_ok, 1)
            total = sp.value_load(total_i[0:1, 0:1], min_val=PAIRS, max_val=PAIRS * (NL // CAP))
            with sp.Fori(1, total) as i:
                j = i % PAIRS
                for q in range(12):
                    sp.wait_ge(m_steps, 12 * i + (q // 2 * 2 - 10))
                    sp.dma_start(MR[:, q, :], experts[ds(j, 1), q].rearrange("a p n -> p (a n)")).then_inc(m_load[q], 16)
            sp.wait_ge(m_steps, 12 * total)
            for q in range(4):
                sp.dma_start(MR[:, q, :], w_gate[q]).then_inc(pg_in, 16)
            for k in range(KD):
                sp.wait_ge(x_upd, 17 + k)
                sp.dma_start(out[k * P:(k + 1) * P, :], X[:, k, 0:NL]).then_inc(xo, 16)
            sp.wait_ge(xo, 16 * KD)

        @block.tensor
        def _(pe):
            def wait_slot(n, extra=0):
                pe.wait_ge(loaded[n % RING], 16 * (n // RING + 1) + extra)

            def wait_half(s, extra=0):
                u = previous_user(s)
                if u:
                    pe.wait_ge(evac[u[0]], u[1] + extra)

            def half_free(s, per=0, i=0):
                if isinstance(i, int):
                    wait_half(s + per * i)
                else:
                    who, count = previous_user(s + per)
                    inc = evacuated(who, s + per) - evacuated(who, s)
                    pe.wait_ge(evac[who], inc * i + (count - inc))

            def product(s, parts, nt, per=0, i=0, tile=0, start=True, stop=True, ready=None):
                pe.wait_ge(lo_done, per * i + splits(s))
                last_k = CHUNKS[s // 2] - 1
                for k in range(last_k + 1):
                    if ready:
                        ready(k)
                    for a, b in pieces(nt):
                        for n, (x, y) in enumerate(((0, 0), (0, 1), (1, 0))):
                            last = nc.tensor.matmul(ps[s % 2][:, a:b], part(x, s)[:, k, :], parts[y][:, tile + k, a:b],
                                                    start=start and k == 0 and n == 0,
                                                    stop=stop and k == last_k and n == 2)
                last.then_inc(steps, 1)

            def h_tile(n):
                return lambda k: pe.wait_ge((h_lov, h_lop)[k % 2], 4 * n + k // 2 + 1)

            kept = []

            def mod_turn():
                tile, l = kept[-1]
                pe.wait_ge(mod_kept, len(kept))
                for half in range(2):
                    c = 768 + 96 * l + 2 * (tile + half)
                    last = nc.tensor.matmul(ps[3][:, c:c + 2], mrow[:, half * P:(half + 1) * P], fold, start=True, stop=True)
                last.then_inc(mod_turned, 1)

            def mod_slot(n, tile, l, first=False):
                if not first:
                    mod_turn()
                wait_slot(n)
                w = ring[:, n % RING, :].rearrange("p (k n) -> p k n", n=256)
                for k in range(KD):
                    g = 32 * (k % 4)
                    last = nc.tensor.matmul(ps[3][g:g + 32, 512:768], sc2[:, k, :], w[:, k, :], start=k < 4, stop=k >= 4)
                last.then_inc(steps, 2)
                kept.append((tile, l))

            def spread_sum(n, nt):
                pe.wait_ge(summed, 7 * n + 7)
                pe.wait_ge(squared, 8 * n + 8)
                for c in range(nt // P):
                    nc.tensor.matmul(ps[2][:, c:c + 1], NGS[n][:, 0, c * P:(c + 1) * P], onesm[:, 0:1], start=True, stop=False)
                    last = nc.tensor.matmul(ps[2][:, c:c + 1], CGS[n][:, 1, c * P:(c + 1) * P], onesm[:, 0:1], start=False,
                                            stop=True)
                last.then_inc(ms_ready, 1)
                pe.wait_ge(rstd_ok, 2 * n + 2)
                for a, b in pieces(nt):
                    last = nc.tensor.matmul(ps[2][:, a:b], ones1, NGS[n][:, 1, a:b], start=True, stop=True)
                last.then_inc(spread, 1)

            pe.wait_ge(inputs, 32)
            pe.wait_ge(silu_done, 1)
            for n in range(8):
                mod_slot(n, 2 * n, 0, n == 0)
            mod_turn()

            for l in range(LAYERS):
                spread_sum(2 * l, T)
                ntq = T if l == 0 else NL

                def head_stat(t):
                    nt = ntq if t < 4 else T
                    g = 5 * l + t
                    pe.wait_ge(g_sq, g + 1)
                    if g:
                        pe.wait_ge(g_rt, g)
                    for a, b in pieces(nt):
                        last = nc.tensor.matmul(ps[2][:, a:b], blk, SQH[:, t % 2, a:b], start=True, stop=True)
                    last.then_inc(g_ms, 1)

                def head_rot(t):
                    g = 5 * l + t
                    pe.wait_ge(g_n, g + 1)
                    if g:
                        pe.wait_ge(g_sin, g)
                    nc.tensor.matmul(ps[3][:, 0:NL], rot, NGH[:, t % 2, 0:NL], start=True, stop=True).then_inc(g_rot, 1)

                def turn_v(j, s):
                    v = 5 * l + j
                    pe.wait_ge(evac["A"], evacuated("A", s))
                    if j == 0:
                        pe.wait_ge(g_rt, 5 * (l + 1))
                    if v:
                        pe.wait_ge(v_k, v)
                    for c in range(6):
                        last = nc.tensor.transpose(ps[2][:, c * P:(c + 1) * P], RAWH[:, (j + 1) % 2, c * P:(c + 1) * P],
                                                   ident)
                    last.then_inc(v_t, 1)

                s0 = 2 * SLOT0[l, "gq"]
                gv = s0 + 5
                nav = 2 * SLOT0[l, "nav"]
                for j in range(18):
                    s = s0 + j
                    wait_half(s)
                    product(s, HS, ntq if j < 4 or 10 <= j < 14 else T, ready=h_tile(2 * l) if j == 0 else None)
                    if 1 <= j <= 5:
                        head_stat(j - 1)
                    if 2 <= j <= 6:
                        head_rot(j - 2)
                    if j == 7:
                        turn_v(0, gv)
                    if s > nav:
                        turn_v(s - nav, s - 1)
                turn_v(4, nav + 3)

                units = attention_units(l)
                NU = len(units)
                u0 = U0[l]
                slot = SLOT0[l, "mod_rest"]
                mods = [(0, 16 + 2 * j) for j in range(16)] + [(1, 2 * j) for j in range(8)] if l == 0 else \
                       [(1, 16 + 2 * j) for j in range(16)]
                per_pair = NU // 8
                pe.wait_ge(evac["A"], evacuated("A", 2 * SLOT0[l, "mod_rest"] - 1))
                pe.wait_ge(g_q, 5 * (l + 1))
                pe.wait_ge(v_k, 5 * (l + 1))
                for i in range(NU + 4):
                    if i < NU:
                        na, t, qb, half = units[i]
                        lo = half * HD
                        kt = t if na else 4
                        w = (u0 + i) // 2
                        if i >= 2:
                            pe.wait_ge(s_exp, u0 + i - 1)
                        pe.wait_ge(q_lo, w + 1)
                        pe.wait_ge(k_lo, 5 * l + kt + 1)
                        for a, b in ((0, 512), (512, 768)):
                            if qb >= 4 and a == 0:
                                continue
                            for n, (x, y) in enumerate(((0, 0), (0, 1), (1, 0))):
                                k = (KL[kt] if y else KU[:, kt, :])[lo:lo + HD, a:b]
                                last = nc.tensor.matmul(ps[i % 2][:, a:b], q_parts[lo:lo + HD, 2 * x + w % 2, :], k,
                                                        start=n == 0, stop=n == 2)
                        last.then_inc(s_sc, 1)
                        if i % (per_pair // (3 if l == 0 else 2)) == 0:
                            lm, tile = mods[slot - SLOT0[l, "mod_rest"]]
                            mod_slot(slot, tile, lm, i == 0)
                            slot += 1
                    if 2 <= i < NU + 2:
                        u = u0 + i - 2
                        c0 = 0 if units[i - 2][2] < 4 else 4
                        pe.wait_ge(s_dg, u + 1)
                        if i > 2:
                            pe.wait_ge(s_pta, u)
                        for c in range(c0, 4):
                            last = nc.tensor.matmul(ps[2][:, c * P:(c + 1) * P], PB[:, u % 3, c * P:(c + 1) * P],
                                                    inv[:, u % 2, :], start=True, stop=True)
                        if c0 == 0:
                            last.then_inc(s_tr, 1)
                        if i > 2:
                            pe.wait_ge(s_ptb, u)
                        for c in range(4, 6):
                            last = nc.tensor.matmul(ps[2][:, c * P:(c + 1) * P], PB[:, u % 3, c * P:(c + 1) * P],
                                                    inv[:, u % 2, :], start=True, stop=True)
                        last.then_inc(s_tr, 1 if c0 == 0 else 2)
                    if i >= 4 and i % 2 == 0:
                        na, t, qb, _ = units[i - 4]
                        u = u0 + i - 4
                        w = u // 2
                        c0 = 0 if qb < 4 else 4
                        pe.wait_ge(s_pta, u + 2)
                        pe.wait_ge(s_ptb, u + 2)
                        if i >= 8:
                            pe.wait_ge(s_y, w - 1)
                        for c in range(c0, 6):
                            for half in range(2):
                                h = (2 * t + half) * HD if na else 512 + half * HD
                                last = nc.tensor.matmul(ps[3][half * HD:(half + 1) * HD, P * (w % 2):P * (w % 2) + P],
                                                        V[:, c, h:h + HD], PT[:, (u + half) % 3, c * P:(c + 1) * P],
                                                        start=c == c0, stop=c == 5)
                        last.then_inc(s_pv, 1)
                mod_turn()

                nt = ntq
                s0 = 2 * SLOT0[l, "merge"]

                def merge_round(i):
                    for j in range(4):
                        for half in range(2):
                            s = s0 + 2 * j + half
                            half_free(s, 8, i)
                            if j % 2 == 0:
                                product(s, HS, nt, 8, i)
                            else:
                                tile = 0 if j == 1 else 4
                                first = isinstance(i, int) and half == 0
                                product(s, YS2, nt, 8, i, tile,
                                        ready=(lambda k: pe.wait_ge(y_lo, 16 * l + tile + k + 1)) if first else None)

                merge_round(0)
                with pe.Fori(1, 4) as i:
                    merge_round(i)

                s0 = 2 * SLOT0[l, "w_o"]
                for j in range(8):
                    wait_half(s0 + j)
                    product(s0 + j, MS2, nt, ready=(lambda k: pe.wait_ge(y_lo, 16 * l + 9 + k)) if j == 0 else None)

                spread_sum(2 * l + 1, nt)
                for hf in range(2):
                    s0 = 2 * SLOT0[l, f"ffn_in{hf}"]

                    def ffn_in_slots(j0, j1, i=0):
                        for j in range(2 * j0, 2 * j1):
                            half_free(s0 + j, 4, i)
                            product(s0 + j, HS, nt, 4, i, ready=h_tile(2 * l + 1) if hf == 0 and j == 0 else None)

                    ffn_in_slots(0, 3)
                    with pe.Fori(0, (KH - 3) // 2) as i:
                        ffn_in_slots(3, 5, i)

                    s0 = 2 * SLOT0[l, f"ffn_out{hf}"]
                    done = (2 * l + hf) * KH

                    def ffn_out_round(i):
                        for j in range(4):
                            if j < 2:
                                half_free(s0 + j, 4, i)
                            first = isinstance(i, int) and j in (0, 2)
                            product(s0 + j, GS, nt, 4, i, FFQ[0] * (j // 2), start=j < 2, stop=j >= 2,
                                    ready=(lambda k: pe.wait_ge(gs_lo, done + FFQ[0] * (j // 2) + k + 1)) if first else None)

                    ffn_out_round(0)
                    with pe.Fori(1, 4) as i:
                        ffn_out_round(i)
            spread_sum(4, NL)
            spread_sum(5, NL)

            s0 = 2 * SLOT0[2, "w_in2"]
            for j in range(16):
                s = s0 + j
                wait_half(s)
                product(s, H2, NL, ready=(lambda k: pe.wait_ge((p_lov, p_lop)[k % 2], k // 2 + 1)) if j == 0 else None)
            def convolve(n):
                t = PE_CONV[n]
                pe.wait_ge(evac["V"], evacuated("V", s0 + 2 * t + 1))
                for d in range(TAPS):
                    c = n * TAPS + d
                    pe.wait_ge(diag, c + 1)
                    nc.tensor.matmul(ps[n][:, 0:NL], DG[:, c % NDG, :], UC[:, t, d:d + NL], start=d == 0,
                                     stop=d == TAPS - 1).then_inc(conv_p, 1)

            pe.wait_ge(evac["A"], evacuated("A", s0 + 15))
            pe.wait_ge(wb_in, 16 * 16)
            for j in range(8):
                t, g = j // 2, j % 2
                if g == 0:
                    pe.wait_ge(lconv, t + 1)
                if j >= 4:
                    pe.wait_ge(gact, j - 3)
                bank = ps[2 + (j % 4) // 2][:, 512 * (j % 2):512 * (j % 2) + 512]
                nc.tensor.matmul(bank, WB[:, g, t, :], XR[:, t, :], start=True, stop=True).then_inc(gpe, 1)
            for n in range(len(PE_CONV)):
                convolve(n)
            pe.wait_ge(gact, 8)
            pe.wait_ge(conv_k, 4)
            for t in range(4):
                last = nc.tensor.matmul(ps[2][:, 0:NL], onesm, CV[:, t, :], start=t == 0, stop=t == 3)
            last.then_inc(lnm, 1)
            for t in range(4):
                pe.wait_ge(lns, t + 1)
                last = nc.tensor.matmul(ps[3][:, 0:NL], onesm, TH[:, t, :], start=t == 0, stop=t == 3)
            last.then_inc(lnv, 1)
            s0 = 2 * SLOT0[2, "w_out2"]
            pe.wait_ge(ylru, 4)
            for j in range(8):
                s = s0 + j
                if j >= 2:
                    wait_half(s)
                product(s, MIX, NL, ready=(lambda k: pe.wait_ge(mix_lo, k + 1)) if j == 0 else None)
            spread_sum(6, NL)
            pe.wait_ge(r_in, 32)
            pe.wait_ge(lnr, 1)
            pe.wait_ge(h2, 16)
            for c in range(4):
                for k in range(KD):
                    last = nc.tensor.matmul(ps[3][:, c * 64:c * 64 + NR], H[:, k, c * P:(c + 1) * P], WR[:, k, :],
                                            start=k == 0, stop=k == KD - 1)
            last.then_inc(rl, 1)
            for c in range(3):
                if c < 2:
                    wait_half(2 * N_STREAM + c)
                for k in range(KD):
                    last = nc.tensor.transpose(ps[c][:, k * P:(k + 1) * P], H[:, k, c * P:(c + 1) * P], ident)
                last.then_inc(ht, 1)
            pe.wait_ge(htk_a, 1)
            pe.wait_ge(htk_v, 1)
            for k in range(KD):
                last = nc.tensor.transpose(ps[0][:, k * P:(k + 1) * P], H[:, k, 3 * P:4 * P], ident)
            last.then_inc(ht, 1)
            pe.wait_ge(r_mask, 1)
            for c in range(4):
                for b in range(c + 1):
                    nc.tensor.matmul(ps[3][:, c * 32:(c + 1) * 32], tri if b == c else ones1, SEL[:, b * 32:(b + 1) * 32],
                                     start=b == 0, stop=b == c)
            for b in range(4):
                last = nc.tensor.matmul(ps[3][:, 128:160], ones1, SEL[:, b * 32:(b + 1) * 32], start=b == 0, stop=b == 3)
            last.then_inc(r_pos, 1)

            pe.wait_ge(htk_a, 4)
            pe.wait_ge(htk_v, 4)
            pe.wait_ge(r_ok, 1)
            total = pe.value_load(total_i[0:1, 0:1], min_val=PAIRS, max_val=PAIRS * (NL // CAP))

            def gather(half):
                for k in range(4 * half, 4 * half + 4):
                    for c in range(4):
                        last = nc.tensor.matmul(ps[0][:, k * P:(k + 1) * P], htok(c, k), SEL[:, c * P:(c + 1) * P],
                                                start=c == 0, stop=c == 3)
                last.then_inc(m_xg, 1)

            def turn_selection():
                for c in range(4):
                    last = nc.tensor.transpose(ps[3][:, c * P:(c + 1) * P], SELG[:, c * P:(c + 1) * P], ident)
                last.then_inc(m_selt, 1)

            pe.wait_ge(m_sel, 1)
            gather(0)
            gather(1)
            turn_selection()
            with pe.Fori(0, total) as i:
                pe.wait_ge(m_xga, i + 1)
                pe.wait_ge(m_xgv, i + 1)
                for w13 in range(2):
                    for kk in range(2):
                        q = 4 * w13 + 2 * kk
                        pe.wait_ge(m_load[q], 16 * i + 16)
                        pe.wait_ge(m_load[q + 1], 16 * i + 16)
                        for k in range(4):
                            for x in range(2):
                                w = MR[:, q + x, k * 512:(k + 1) * 512]
                                last = nc.tensor.matmul(ps[1][CAP * x:CAP * x + CAP, 512 * w13:512 * w13 + 512],
                                                        XG[:, 4 * kk + k, x * CAP:(x + 1) * CAP], w,
                                                        start=kk == 0 and k == 0, stop=kk == 1 and k == 3)
                        last.then_inc(m_steps, 2)
                pe.wait_ge(m_sel, i + 2)
                pe.wait_ge(m_add, 8 * i + 1)
                gather(0)
                pe.wait_ge(m_g, i + 1)
                for k in range(4):
                    last = nc.tensor.transpose(ps[3][:, 512 + k * P:640 + k * P], GH[:, k * P:(k + 1) * P], ident)
                last.then_inc(m_gt, 1)
                pe.wait_ge(m_gk, i + 1)
                for kk in range(2):
                    q = 8 + 2 * kk
                    pe.wait_ge(m_load[q], 16 * i + 16)
                    pe.wait_ge(m_load[q + 1], 16 * i + 16)
                    for k in range(2):
                        for n in range(2):
                            for x in range(2):
                                w = MR[:, q + x, k * D + 512 * n:k * D + 512 * n + 512]
                                last = nc.tensor.matmul(ps[2][CAP * x:CAP * x + CAP, 512 * n:512 * n + 512],
                                                        GT[:, 2 * kk + k, x * CAP:(x + 1) * CAP], w,
                                                        start=kk == 0 and k == 0, stop=kk == 1 and k == 1)
                    last.then_inc(m_steps, 2)
                gather(1)
                pe.wait_ge(m_w, i + 1)
                pe.wait_ge(m_pick, i + 1)
                turn_selection()
                pe.wait_ge(m_ysv, i + 1)
                for m in range(KD):
                    if m < 2:
                        pe.wait_ge((m_xga, m_xgv)[m], i + 2)
                    if m >= 2:
                        pe.wait_ge(m_add, 8 * i + m)
                    for x in range(2):
                        last = nc.tensor.matmul(ps[0][:, 512 * (m % 2):512 * (m % 2) + 512],
                                                YP[x][:, m // 4, (m % 4) * P:(m % 4 + 1) * P], PICK, start=x == 0, stop=x == 1)
                    last.then_inc(m_sc, 1)

            pe.wait_ge(p_in, 32)
            pe.wait_ge(m_add, 8 * total + 1)
            for m in range(KD):
                if m >= 2:
                    pe.wait_ge(e_sq, m - 1)
                for k in range(2):
                    last = nc.tensor.matmul(ps[m % 2][:, 0:NL], WP[:, k, m * P:(m + 1) * P], PTT[:, k, :],
                                            start=k == 0, stop=k == 1)
                last.then_inc(e_pe, 1)
            spread_sum(7, NL)
            for m in range(KD):
                pe.wait_ge(e_sq, m + 1)
                last = nc.tensor.matmul(ps[3][:, 0:NL], onesm, EQ[:, m, :], start=m == 0, stop=m == KD - 1)
            last.then_inc(e_ms, 1)
            for m in range(KD):
                if m % 2 == 0:
                    pe.wait_ge(pg_in, 64)
                if m >= 2:
                    pe.wait_ge(pg_a, m - 1)
                w = MR[:, m // 2, :].rearrange("p (k n) -> p k n", n=256)
                for k in range(KD):
                    if m == 0:
                        pe.wait_ge(h2, 17 + k)
                    last = nc.tensor.matmul(ps[m % 2][:, 0:NL], w[:, k, (m % 2) * P:(m % 2 + 1) * P], H[:, k, 0:NL],
                                            start=k == 0, stop=k == KD - 1)
                last.then_inc(pg_pe, 1)
            spread_sum(8, NL)

        @block.scalar
        def _(act):
            act.dma_start(vec[:, :], vecs).then_inc(inputs, 16)
            act.dma_start(cst[:, :], consts).then_inc(inputs, 16)
            for k in range(KD):
                act.dma_start(X[:, k, 0:NL], xT[k * P:(k + 1) * P, :]).then_inc(x_loaded, 16)
                act.dma_start(X[:, k, NL:T], ctxT[k * P:(k + 1) * P, :]).then_inc(x_loaded, 16)
            act.wait_ge(inputs, 32)
            act.wait_ge(sc_zero, 1)
            act.activation(sc2[:, :, 0:2], vcol("c2", 0, 16).rearrange("p (k n) -> p k n", n=2), ACT.Silu)\
               .then_inc(silu_done, 1)

            def keep_mod(n):
                act.wait_ge(steps, 2 * n + 2)
                act.activation(mrow[:, :], ps[3][:, 512:768], ACT.Copy).then_inc(mod_kept, 1)


            def squares(n, nt, tiles=range(KD)):
                for m in tiles:
                    if n == 0:
                        act.wait_ge(x_loaded, 32 * (m + 1) if m == KD - 1 else 256)
                    elif n in (5, 8):
                        act.wait_ge(x_upd, (1 if n == 5 else 9) + m)
                    elif n == 6:
                        act.wait_ge(evac["V"], evacuated("V", 2 * SLOT0[2, "w_out2"] + m))
                    elif n != 7:
                        act.wait_ge(evac["V"], evacuated("V", updating_step(n, m)))
                    if m >= 2:
                        act.wait_ge(summed, 7 * n + m - 1)
                    act.activation(CGS[n][:, m % 2, 0:nt], X[:, m, 0:nt], ACT.Square).then_inc(squared, 1)

            def root(n, nt):
                act.wait_ge(ms_ready, n + 1)
                act.activation(rms[:, 0:nt // P], ps[2][:, 0:nt // P], ACT.Sqrt, bias=epsc[:, 0:1]).then_inc(rooted, 1)

            def upper_h(l, which, nt):
                n = 2 * l + which
                for k in range(KD):
                    act.wait_ge(normed, 8 * n + k + 1)
                    for kind, (a, b) in enumerate(((0, NL), (NL, nt))):
                        if a == b:
                            continue
                        dst = TM[:, k % 4, a:b] if k % 2 else HS[0][:, k, a:b]
                        last = act.activation(dst, TM[:, k % 4, a:b], ACT.Identity,
                                              bias=mod[:, 48 * l + 24 * which + k, kind:kind + 1])
                    if k % 2:
                        last.then_inc(h_sum, 1)
                        act.wait_ge(h_sum, 4 * n + k // 2 + 1)
                        last = act.activation(HS[0][:, k, 0:nt], TM[:, k % 4, 0:nt], ACT.Copy)
                    last.then_inc(h_hi, 1)

            def upper(s, per=0, i=0):
                if not is_split(s):
                    return
                act.wait_ge(loaded[(s // 2) % RING], 4 * per * i + 16 * (s // 4 + 1))
                act.wait_ge(steps, per * i + (s - 1))
                act.activation(part(0, s), raw_half(s), ACT.Copy).then_inc(hi_done, 1)

            act.wait_ge(small_ok, 1)
            squares(0, T)
            for l in range(LAYERS):
                ntq = T if l == 0 else NL
                if l == 0:
                    upper(2 * SLOT0[0, "gq"])
                    upper(2 * SLOT0[0, "gq"] + 1)
                root(2 * l, T)
                upper_h(l, 0, T)

                def step_done(s):
                    upper(s + 2)
                    act.wait_ge(steps, s + 1)

                def keep_head(t):
                    s = 2 * SLOT0[l, "gq"] + t
                    g = 5 * l + t
                    nt = ntq if t < 4 else T
                    step_done(s)
                    if g >= 2:
                        act.wait_ge(g_n, g - 1)
                    act.activation(RAWH[:, t % 2, 0:nt], ps[s % 2][:, 0:nt], ACT.Copy).then_inc(evac["A"], 1)
                    act.wait_ge(evac["A"], evacuated("A", s))
                    act.activation(SQH[:, t % 2, 0:nt], RAWH[:, t % 2, 0:nt], ACT.Square).then_inc(g_sq, 1)

                def root_head(t):
                    g = 5 * l + t
                    nt = ntq if t < 4 else T
                    act.wait_ge(g_ms, g + 1)
                    act.activation(SQH[:, t % 2, 0:nt], ps[2][:, 0:nt], ACT.Sqrt, bias=epsc[:, 0:1]).then_inc(g_rt, 1)

                def keep_v_features(j, s):
                    step_done(s)
                    if j == 0:
                        act.wait_ge(g_n, 5 * l + 4)
                    if j == 1:
                        act.wait_ge(g_n, 5 * l + 5)
                    if j >= 2:
                        act.wait_ge(v_t, 5 * l + j - 1)
                    act.activation(RAWH[:, (j + 1) % 2, 0:T], ps[s % 2][:, 0:T], ACT.Copy).then_inc(evac["A"], 1)

                def keep_v(j):
                    at = 512 if j == 0 else (j - 1) * P
                    act.wait_ge(v_t, 5 * l + j + 1)
                    act.activation(V[:, :, at:at + P], ps[2][:, 0:T].rearrange("p (c n) -> p c n", n=P), ACT.Copy)\
                       .then_inc(v_k, 1)

                for t in range(5):
                    keep_head(t)
                    if t:
                        root_head(t - 1)
                keep_v_features(0, 2 * SLOT0[l, "gkv"] + 1)
                root_head(4)
                s = 2 * SLOT0[l, "nak"]
                for j in range(4):
                    step_done(s + j)
                    act.activation(KNA[:, j, :], ps[(s + j) % 2][:, 0:T], ACT.Copy).then_inc(evac["A"], 1)
                    if j == 1:
                        keep_v(0)
                s = 2 * SLOT0[l, "naq"]
                for j in range(4):
                    step_done(s + j)
                    act.activation(QNA[:, j, 0:ntq], ps[(s + j) % 2][:, 0:ntq], ACT.Copy, scale=QSCALE)\
                       .then_inc(evac["A"], 1)
                s = 2 * SLOT0[l, "nav"]
                for j in range(4):
                    keep_v_features(j + 1, s + j)
                    if j:
                        keep_v(j)
                keep_v(4)

                units = attention_units(l)
                NU = len(units)
                u0 = U0[l]
                act.wait_ge(g_q, 5 * (l + 1))
                slot = SLOT0[l, "mod_rest"]
                per_pair = NU // 8

                def upper_q(i):
                    na, t, qb, _h = units[i]
                    src = (QNA if na else QG)[:, t, qb * P:(qb + 1) * P]
                    act.activation(q_parts[:, ((u0 + i) // 2) % 2, :], src, ACT.Copy).then_inc(q_hi, 1)

                upper_q(0)
                upper_q(2)
                act.wait_ge(steps, 2 * SLOT0[l, "mod_rest"])
                for t in range(5):
                    src = KNA[:, t, :] if t < 4 else KG[:, 0, :]
                    act.activation(KU[:, t, :], src, ACT.Copy).then_inc(k_hi, 1)
                for i in range(NU + 4):
                    if 2 <= i < NU + 2:
                        u = u0 + i - 2
                        if i >= 5:
                            act.wait_ge(s_pv, (u - 3) // 2 + 1)
                        if units[i - 2][2] < 4:
                            act.wait_ge(s_tr, 2 * u + 1)
                            act.activation(PT[:, u % 3, 0:512], ps[2][:, 0:512], ACT.Copy).then_inc(s_pta, 1)
                        else:
                            act.wait_ge(s_tr, 2 * u + 2)
                            act.activation(small[:, 3, 7:8], epsc[:, 0:1], ACT.Copy).then_inc(s_pta, 1)
                    if i < NU:
                        u = u0 + i
                        c0 = 0 if units[i][2] < 4 else 512
                        act.wait_ge(s_mx, u + 1)
                        if i >= 3:
                            act.wait_ge(s_tr, 2 * (u - 3) + 2)
                        act.activation(PB[:, u % 3, c0:T], ps[i % 2][:, c0:T], ACT.Exp, bias=small[:, 0, u % 8:u % 8 + 1],
                                       accum_out=small[:, 1, u % 8:u % 8 + 1]).then_inc(s_exp, 1)
                        if i % 2 and i + 3 < NU:
                            upper_q(i + 3)
                        if i % (per_pair // (3 if l == 0 else 2)) == 0:
                            keep_mod(slot)
                            slot += 1
                    if i >= 4 and i % 2 == 0:
                        na, t, qb, _h = units[i - 4]
                        w = (u0 + i - 4) // 2
                        act.wait_ge(s_pv, w + 1)
                        act.activation(Y[:, (0 if na else 4) + t, qb * P:(qb + 1) * P],
                                       ps[3][:, P * (w % 2):P * (w % 2) + P], ACT.Copy).then_inc(s_y, 1)

                s0 = 2 * SLOT0[l, "merge"]
                nt = ntq
                upper(s0)
                upper(s0 + 1)
                act.wait_ge(s_y, (u0 + NU) // 2)
                for k in range(KD):
                    act.activation(YS2[0][:, k, 0:nt], Y[:, k, 0:nt], ACT.Copy).then_inc(y_hi, 1)

                def gates(i):
                    for j in range(4):
                        for half in range(2):
                            s = s0 + 2 * j + half
                            upper(s + 2, 8, i)
                            if j % 2:
                                continue
                            act.wait_ge(steps, 8 * i + (s + 1))
                            if j:
                                act.wait_ge(evac["V"], ev("V", s - 2, 8, i))
                            elif not isinstance(i, int):
                                act.wait_ge(evac["V"], ev("V", s, 8, i))
                            act.activation(RAW[:, half, 0:nt], ps[half][:, 0:nt], ACT.Sigmoid).then_inc(evac["A"], 1)

                gates(0)
                with act.Fori(1, 4) as i:
                    gates(i)
                act.wait_ge(steps, 2 * SLOT0[l, "w_o"])
                for k in range(KD):
                    act.wait_ge(merged, 8 * l + k + 1)
                    act.activation(MS2[0][:, k, 0:nt], M[:, k, 0:nt], ACT.Copy).then_inc(y_hi, 1)

                for m in range(KD):
                    upper(2 * SLOT0[l, "w_o"] + m + 2)
                    squares(2 * l + 1, nt, [m])
                root(2 * l + 1, nt)
                upper_h(l, 1, nt)

                for hf in range(2):
                    s0 = 2 * SLOT0[l, f"ffn_in{hf}"]
                    done = (2 * l + hf) * KH

                    def hidden(j0, j1, i=0):
                        for j in range(j0, j1):
                            s = s0 + 2 * j
                            upper(s + 2, 4, i)
                            act.wait_ge(steps, 4 * i + (s + 1))
                            if j >= 2:
                                act.wait_ge(gs_lo, 2 * i + (done + j - 1))
                            act.activation(RAW[:, j % 2, 0:nt], ps[0][:, 0:nt], ACT.Silu).then_inc(evac["A"], 1)
                            upper(s + 3, 4, i)
                            act.wait_ge(evac["V"], ev("V", s + 1, 4, i))
                            if isinstance(i, int):
                                dst, src = GS[0][:, j, 0:nt], RAW[:, j % 2, 0:nt]
                            else:
                                dst, src = GS[0][:, ds(2 * i + j, 1), 0:nt], RAW[:, j % 2:j % 2 + 1, 0:nt]
                            act.activation(dst, src, ACT.Copy).then_inc(gs_hi, 1)

                    hidden(0, 3)
                    with act.Fori(0, (KH - 3) // 2) as i:
                        hidden(3, 5, i)
                    s0 = 2 * SLOT0[l, f"ffn_out{hf}"]
                    if hf == 0:
                        for j in range(16):
                            upper(s0 + j + 2)
                    else:
                        for j in range(16):
                            upper(s0 + j + 2)
                            if j % 4 >= 2:
                                squares(2 * l + 2, T if l == 0 else NL, [2 * (j // 4) + j % 2])
            root(4, NL)
            squares(5, NL)
            root(5, NL)
            for k in range(KD):
                act.wait_ge(h2, k + 1)
                act.activation(H2[0][:, k, :], H[:, k, 0:NL], ACT.Copy).then_inc(p_hi, 1)
            act.wait_ge(lam_a, 1)
            act.activation(lam8[:, 1, :], lam8[:, 0, :], ACT.Exp).then_inc(lam_e, 1)
            s0 = 2 * SLOT0[2, "w_in2"]
            for t in range(4):
                s = s0 + 2 * t
                upper(s + 2)
                act.wait_ge(steps, s + 1)
                if t >= 2:
                    act.wait_ge(evac["V"], evacuated("V", s - 3))
                act.activation(RAW2[:, t % 2, 0:NL], ps[0][:, 0:NL], ACT.Sigmoid).then_inc(evac["A"], 1)
                upper(s + 3)
            for t in range(4):
                s = s0 + 8 + t
                upper(s + 2)
                act.wait_ge(steps, s + 1)
                act.activation(XL[:, t, LTAPS - 1:LTAPS - 1 + NL], ps[s % 2][:, 0:NL], ACT.Copy).then_inc(evac["A"], 1)
            for t in range(4):
                s = s0 + 12 + t
                upper(s + 2)
                act.wait_ge(steps, s + 1)
                act.activation(GL[:, t, :], ps[s % 2][:, 0:NL], ACT.Gelu_apprx_tanh).then_inc(evac["A"], 1)
            for j in range(8):
                t, g = j // 2, j % 2
                act.wait_ge(gpe, j + 1)
                act.activation((LA, LU)[g][:, t, :], ps[2 + (j % 4) // 2][:, 512 * (j % 2):512 * (j % 2) + 512],
                               ACT.Sigmoid, bias=vcol(("b_r", "b_i")[g], t)).then_inc(gact, 1)
            act.wait_ge(r_lam, 1)
            for t in range(4):
                act.wait_ge(gact, 2 * t + 1)
                act.activation(TH[:, t, :], LA[:, t, :], ACT.Tanh, scale=lam8[:, 6, t:t + 1]).then_inc(lth, 1)
            for t in range(4):
                act.wait_ge(lth, t + 1)
                act.activation(LA[:, t, :], LA[:, t, :], ACT.Exp, scale=lam8[:, 7, t:t + 1]).then_inc(lexp, 1)
            for t in range(4):
                act.wait_ge(lm2, t + 1)
                act.activation(TH[:, t, :], TH[:, t, :], ACT.Sqrt).then_inc(lsq, 1)
            for n, t in enumerate(PE_CONV):
                act.wait_ge(conv_p, TAPS * (n + 1))
                act.activation(CV[:, t, :], ps[n][:, 0:NL], ACT.Identity, bias=vcol("conv_b", t)).then_inc(conv_k, 1)
            for t in range(4):
                act.wait_ge(lnc, t + 1)
                act.wait_ge(ylru, t + 1)
                act.activation(TH[:, t, :], CV[:, t, :], ACT.Square).then_inc(lns, 1)
            for t in range(4):
                act.activation(MIX[0][:, t, :], LH[:, t, :], ACT.Copy).then_inc(mix_hi, 1)
            act.wait_ge(lnv, 1)
            act.activation(RAW2[:, 0, 0:NL], ps[3][:, 0:NL], ACT.Sqrt, bias=epsc[:, 0:1], scale=2.0).then_inc(lnr, 1)
            for t in range(4):
                act.wait_ge(lnn, t + 1)
                act.activation(CV[:, t, :], CV[:, t, :], ACT.Silu, scale=vcol("ln_g", t), bias=vcol("ln_b", t))\
                   .then_inc(yconv, 1)
                act.wait_ge(yconv, t + 1)
                act.activation(MIX[0][:, 4 + t, :], CV[:, t, :], ACT.Copy).then_inc(mix_hi, 1)
            for m in range(KD):
                upper(2 * SLOT0[2, "w_out2"] + m + 2)
                squares(6, NL, [m])
            root(6, NL)

            for c in range(4):
                if c == 3:
                    for n in range(2):
                        act.wait_ge(re1, n + 1)
                        act.activation(rexp[n], rexp[n], ACT.Exp).then_inc(re2, 1)
                act.wait_ge(ht, c + 1)
                act.activation(htok_half(c, 0), ps[c % 3][:, 0:512].rearrange("p (a b) -> p a b", a=2), ACT.Copy)\
                   .then_inc(htk_a, 1)

            act.wait_ge(r_ok, 1)
            total = act.value_load(total_i[0:1, 0:1], min_val=PAIRS, max_val=PAIRS * (NL // CAP))

            def gathered(n):
                act.wait_ge(m_xg, 2 * n - 1)
                act.activation(scr[:, 0:512], ps[0][:, 0:512], ACT.Copy).then_inc(m_xga, 1)

            def slot_weights(n):
                act.wait_ge(m_selt, n)
                act.activation(SELT, ps[3][:, 0:512], ACT.Copy, accum_out=wslot[:, 0:1]).then_inc(m_w, 1)

            gathered(1)
            slot_weights(1)
            with act.Fori(0, total) as i:
                act.wait_ge(m_steps, 12 * i + 4)
                act.activation(SGM, ps[1][:, 0:512], ACT.Silu).then_inc(m_act, 1)
                gathered(i + 2)
                act.wait_ge(m_gt, i + 1)
                act.activation(scr[:, 3072:3584], ps[3][:, 512:1024], ACT.Copy).then_inc(m_gk, 1)
                act.wait_ge(m_w, i + 1)
                act.wait_ge(m_steps, 12 * i + 12)
                act.activation(YP[0], ps[2][:, :].rearrange("p (a b) -> p a b", a=2), ACT.Copy, scale=wslot[:, 0:1])\
                   .then_inc(m_ysa, 1)
                act.wait_ge(m_ysv, i + 1)
                slot_weights(i + 2)

            act.wait_ge(m_add, 8 * total + 1)
            for m in range(KD):
                squares(7, NL, [m])
                act.wait_ge(e_pe, m + 1)
                act.activation(EB[:, m, :], ps[m % 2][:, 0:NL], ACT.Copy).then_inc(e_k, 1)
                act.activation(EQ[:, m, :], ps[m % 2][:, 0:NL], ACT.Square).then_inc(e_sq, 1)
            root(7, NL)
            act.wait_ge(e_ms, 1)
            act.activation(RE, ps[3][:, 0:NL], ACT.Sqrt, bias=epsc[:, 0:1]).then_inc(e_rt, 1)
            for m in range(KD):
                act.wait_ge(pg_pe, m + 1)
                if m >= 2:
                    act.wait_ge(x_upd, 8 + m - 1)
                act.activation(PG[:, m % 2, :], ps[m % 2][:, 0:NL], ACT.Sigmoid).then_inc(pg_a, 1)
                if m:
                    squares(8, NL, [m - 1])
            squares(8, NL, [KD - 1])
            root(8, NL)

        @block.gpsimd
        def _(pool):
            def sum_squares(n, nt, tiles=range(KD - 1)):
                total, sq = NGS[n], CGS[n]
                for m in tiles:
                    if m == KD - 1:
                        continue
                    pool.wait_ge(squared, 8 * n + m + 1)
                    if m == 0:
                        nc.gpsimd.tensor_copy(total[:, 0, 0:nt], sq[:, 0, 0:nt]).then_inc(summed, 1)
                    else:
                        pool.wait_ge(summed, 7 * n + m)
                        nc.gpsimd.tensor_tensor(total[:, 0, 0:nt], total[:, 0, 0:nt], sq[:, m % 2, 0:nt], ALU.add)\
                            .then_inc(summed, 1)

            def lower(s, per=0, i=0):
                if not is_split(s):
                    return
                pool.wait_ge(hi_done, per * i + splits(s))
                nc.gpsimd.tensor_tensor(part(1, s), raw_half(s), part(0, s).bitcast(fp32), ALU.subtract)\
                    .then_inc(lo_done, 1)

            def lower_h(n, nt):
                for k in range(1, KD, 2):
                    pool.wait_ge(h_hi, 8 * n + k + 1)
                    nc.gpsimd.tensor_tensor(HS[1][:, k, 0:nt], TM[:, k % 4, 0:nt], HS[0][:, k, 0:nt].bitcast(fp32),
                                            ALU.subtract).then_inc(h_lop, 1)

            nc.gpsimd.memset(sc2[:, :, :], 0.0).then_inc(sc_zero, 1)
            nc.gpsimd.memset(epsc[:, :], EPS).then_inc(small_ok, 1)
            sum_squares(0, T)
            def head_cos(l, t):
                g = 5 * l + t
                pool.wait_ge(g_n, g + 1)
                if g >= 2:
                    pool.wait_ge(g_q, g - 1)
                if t == 4 or l == 0:
                    dst = QG[:, t, NL:T] if t < 4 else KG[:, 0, NL:T]
                    nc.gpsimd.tensor_copy(dst, NGH[:, t % 2, NL:T])
                nc.gpsimd.tensor_tensor(CGH[:, t % 2, 0:NL], NGH[:, t % 2, 0:NL], cosT, ALU.mult).then_inc(g_cos, 1)

            def load_bias(l, h):
                b = h % 4
                for half in range(2):
                    src = bass.AP(rows.tensor, ((l * 8 + h) * 15 + 1 - half) * GRID * 128 + 63,
                                  [[127, GRID], [GRID * 128, 14], [1, GRID]])
                    pool.dma_start(BIAS[half * GRID:(half + 1) * GRID, b, :].rearrange("p (i u) -> p i u", u=GRID),
                                   src).then_inc(bias_in[b], 16)

            def mask_bias(l, h):
                b = h % 4
                pool.wait_ge(bias_in[b], 32 * (2 * l + h // 4 + 1))
                t3 = BIAS[:, b, :].rearrange("p (i u) -> p i u", u=GRID)
                nc.gpsimd.tensor_tensor(t3, t3, namask[:, None, :].to_broadcast([P, 14, GRID]), ALU.add).then_inc(bias_ok, 1)

            for l in range(LAYERS):
                ntq = T if l == 0 else NL
                s0 = 2 * SLOT0[l, "gq"]
                if l == 0:
                    lower(s0)
                    lower(s0 + 1)
                lower_h(2 * l, T)
                if l == 0:
                    for ll in range(LAYERS):
                        src = bass.AP(rpb.tensor, ll * 120 * 128, [[128, 120], [0, GRID], [1, 128]])
                        dst = bass.AP(rows.tensor, ll * 120 * GRID * 128, [[GRID * 128, 120], [128, GRID], [1, 128]])
                        pool.dma_start(dst, src).then_inc(rows_in, 16)
                for j in range(18):
                    lower(s0 + j + 2)
                    if 1 <= j <= 5:
                        head_cos(l, j - 1)
                    if j == 8:
                        pool.wait_ge(g_q, 5 * (l + 1))
                        pool.wait_ge(rows_in, 16 * LAYERS)
                        for h in range(4):
                            load_bias(l, h)
                units = attention_units(l)
                per_head = len(units) // 8
                for h in range(8):
                    if h >= 4:
                        pool.wait_ge(s_mx, U0[l] + per_head * (h // 2 - 1))
                        load_bias(l, h)
                    mask_bias(l, h)
                s0 = 2 * SLOT0[l, "merge"]
                lower(s0)
                lower(s0 + 1)
                with pool.Fori(0, 4) as i:
                    for j in range(8):
                        lower(s0 + j + 2, 8, i)
                for m in range(KD):
                    sum_squares(2 * l + 1, ntq, [m])
                    lower(2 * SLOT0[l, "w_o"] + m + 2)
                lower_h(2 * l + 1, ntq)
                for hf in range(2):
                    s0 = 2 * SLOT0[l, f"ffn_in{hf}"]
                    with pool.Fori(0, KH // 2) as i:
                        for j in range(4):
                            lower(s0 + j + 2, 4, i)
                    for j in range(2 * KH - 2, 2 * KH):
                        lower(s0 + j + 2)
                    s0 = 2 * SLOT0[l, f"ffn_out{hf}"]
                    if hf == 0:
                        for j in range(16):
                            lower(s0 + j + 2)
                    else:
                        for j in range(16):
                            if j < 14:
                                lower(s0 + j + 2)
                            if j % 4 >= 2:
                                sum_squares(2 * l + 2, T if l == 0 else NL, [2 * (j // 4) + j % 2])
                            if j >= 14:
                                lower(s0 + j + 2)
            sum_squares(5, NL)
            for k in range(1, KD, 2):
                pool.wait_ge(p_hi, k + 1)
                nc.gpsimd.tensor_tensor(H2[1][:, k, :], H[:, k, 0:NL], H2[0][:, k, :].bitcast(fp32), ALU.subtract)\
                    .then_inc(p_lop, 1)
            pool.wait_ge(x_upd, 8)
            nc.gpsimd.memset(UC[:, :, 0:TAPS - 1], 0.0).then_inc(zeroed, 1)
            nc.gpsimd.memset(XL[:, :, 0:LTAPS - 1], 0.0).then_inc(zeroed, 1)
            nc.gpsimd.memset(WB, 0.0).then_inc(wb_zero, 1)
            pool.wait_ge(wb_zero, 1)

            def diagonal(c):
                t, d = PE_CONV[c // TAPS], c % TAPS
                if c >= NDG:
                    pool.wait_ge(conv_p, c - NDG + 1)
                nc.gpsimd.tensor_scalar(DG[:, c % NDG, :], ident, vcol("conv_w", 4 * d + t), None, ALU.mult)\
                    .then_inc(diag, 1)

            for j in range(16):
                lower(2 * SLOT0[2, "w_in2"] + j + 2)
                if j < NDG:
                    diagonal(j)
                g, h = j // 8, j % 8
                lo = (h % 2) * HD
                pool.dma_start(WB[lo:lo + HD, g, h // 2, lo:lo + HD], lru_w[g, h]).then_inc(wb_in, 16)
            pool.dma_start(WR[:, :, :].rearrange("p k n -> p (k n)"), router).then_inc(r_in, 16)
            pool.dma_start(rb[:, :], router_b).then_inc(r_in, 16)
            for c in range(NDG, TAPS * len(PE_CONV)):
                diagonal(c)
            for m in range(KD):
                sum_squares(6, NL, [m])
                lower(2 * SLOT0[2, "w_out2"] + m + 2)
            for n in (7, 8):
                sum_squares(n, NL)

        @block.vector
        def _(dve):
            def rstd(n, nt):
                dve.wait_ge(rooted, n + 1)
                nc.vector.reciprocal(rms[:, 0:nt // P], rms[:, 0:nt // P]).then_inc(rstd_ok, 1)
                dve.wait_ge(rstd_ok, 2 * n + 1)
                c = nt // P
                nc.vector.tensor_tensor(NGS[n][:, 1, 0:nt].rearrange("p (c n) -> p c n", n=P),
                                        ident[:, None, :].to_broadcast([P, c, P]),
                                        rms[:, 0:c, None].to_broadcast([P, c, P]), ALU.mult).then_inc(rstd_ok, 1)
                dve.wait_ge(spread, n + 1)

            def times_rstd(n, nt):
                l, which = n // 2, n % 2
                rstd(n, nt)
                dve.wait_ge(mod_ready, n + 1)

                def kinds():
                    return [(kind, a, b) for kind, (a, b) in enumerate(((0, NL), (NL, nt))) if a < b]

                def lower_h(k):
                    dve.wait_ge(h_hi, 8 * n + k + 1)
                    for kind, a, b in kinds():
                        last = nc.vector.scalar_tensor_tensor(out=HS[1][:, k, a:b], in0=TM[:, k % 4, a:b],
                                                              scalar=mod[:, 48 * l + 24 * which + k, kind:kind + 1],
                                                              in1=HS[0][:, k, a:b].bitcast(fp32), op0=ALU.add,
                                                              op1=ALU.subtract)
                    last.then_inc(h_lov, 1)

                for k in range(KD):
                    if k >= 4:
                        dve.wait_ge((h_lov, h_lop)[k % 2], 4 * n + (k - 4) // 2 + 1)
                    for kind, a, b in kinds():
                        last = nc.vector.scalar_tensor_tensor(out=TM[:, k % 4, a:b], in0=X[:, k, a:b],
                                                              scalar=amod[:, n, k, kind:kind + 1],
                                                              in1=ps[2][:, a:b], op0=ALU.mult, op1=ALU.mult)
                    last.then_inc(normed, 1)
                    if k % 2:
                        lower_h(k - 1)

            modc = [0]

            def mod_add(l, m0, m1, last=True):
                for kind in range(2):
                    nc.vector.tensor_tensor(mod[:, 48 * l + m0:48 * l + m1, kind],
                                            ps[3][:, 768 + 96 * l + 2 * m0 + kind:768 + 96 * l + 2 * m1:2],
                                            vcol(f"b_mod{l}", m0, m1 - m0), ALU.add).then_inc(mod_sum, 1)
                modc[0] += 2
                dve.wait_ge(mod_sum, modc[0])

            def mod_gain(l, which):
                for kind in range(2):
                    a = 48 * l + 24 * which + 8
                    ins = nc.vector.scalar_tensor_tensor(out=amod[:, 2 * l + which, :, kind], in0=mod[:, a:a + 8, kind],
                                                         scalar=1.0, in1=vcol(f"norm{which + 1}{l}", 0, 8),
                                                         op0=ALU.add, op1=ALU.mult)
                    ins.then_inc(mod_ready, 1) if kind else None

            dve.wait_ge(inputs, 32)
            for l in range(LAYERS):
                nc.vector.tensor_scalar(qg8[:, l:l + 1], vcol(f"q_gain{l}"), QSCALE, None, ALU.mult).then_inc(small_q, 1)
            for n in range(8):
                dve.wait_ge(steps, 2 * n + 2)
                nc.vector.tensor_copy(mrow[:, :], ps[3][:, 512:768]).then_inc(mod_kept, 1)
            dve.wait_ge(mod_turned, 8)
            mod_add(0, 0, 16)
            mod_gain(0, 0)
            for l in range(LAYERS):
                ntq = T if l == 0 else NL
                times_rstd(2 * l, T)
                dve.wait_ge(small_q, LAYERS)

                def norm_head(t):
                    g = 5 * l + t
                    nt = ntq if t < 4 else T
                    dve.wait_ge(g_rt, g + 1)
                    nc.vector.reciprocal(SQH[:, t % 2, 0:nt], SQH[:, t % 2, 0:nt]).then_inc(g_rr, 1)
                    dve.wait_ge(g_rr, g + 1)
                    if g >= 2:
                        dve.wait_ge(g_cos, g - 1)
                        dve.wait_ge(g_rot, g - 1)
                    gain = qg8[:, l:l + 1] if t < 4 else vcol(f"k_gain{l}")
                    nc.vector.scalar_tensor_tensor(out=NGH[:, t % 2, 0:nt], in0=RAWH[:, t % 2, 0:nt], scalar=gain,
                                                   in1=SQH[:, t % 2, 0:nt], op0=ALU.mult, op1=ALU.mult).then_inc(g_n, 1)

                def rope_head(t):
                    g = 5 * l + t
                    dve.wait_ge(g_rot, g + 1)
                    dst = QG[:, t, 0:NL] if t < 4 else KG[:, 0, 0:NL]
                    nc.vector.tensor_tensor(dst, ps[3][:, 0:NL], sinT, ALU.mult).then_inc(g_sin, 1)
                    dve.wait_ge(g_sin, g + 1)
                    dve.wait_ge(g_cos, g + 1)
                    nc.vector.tensor_tensor(dst, dst, CGH[:, t % 2, 0:NL], ALU.add).then_inc(g_q, 1)

                norm_head(0)
                for t in range(1, 5):
                    norm_head(t)
                    rope_head(t - 1)
                rope_head(4)

                units = attention_units(l)
                NU = len(units)
                u0 = U0[l]
                def lower_q(i):
                    na, t, qb, _h = units[i]
                    w = (u0 + i) // 2
                    dve.wait_ge(q_hi, w + 1)
                    nc.vector.tensor_tensor(q_parts[:, 2 + w % 2, :], (QNA if na else QG)[:, t, qb * P:(qb + 1) * P],
                                            q_parts[:, w % 2, :].bitcast(fp32), ALU.subtract).then_inc(q_lo, 1)

                lower_q(0)
                lower_q(2)
                for t in range(5):
                    dve.wait_ge(k_hi, 5 * l + t + 1)
                    nc.vector.tensor_tensor(KL[t], KNA[:, t, :] if t < 4 else KG[:, 0, :], KU[:, t, :].bitcast(fp32),
                                            ALU.subtract).then_inc(k_lo, 1)
                bias_units = [i for i, (na, _, qb, _) in enumerate(units) if na and qb < 4]
                for i in range(NU + 4):
                    if i < NU:
                        na, t, qb, half = units[i]
                        u = u0 + i
                        c = u % 8
                        dve.wait_ge(s_sc, u + 1)
                        if na and qb < 4:
                            h = 2 * t + half
                            dve.wait_ge(bias_ok, 8 * l + h + 1)
                            at = (6 - 2 * qb) * GRID
                            nc.vector.tensor_tensor(ps[i % 2][:, 0:512], ps[i % 2][:, 0:512],
                                                    BIAS[:, h % 4, at:at + 512], ALU.add).then_inc(s_m1, 1)
                            dve.wait_ge(s_m1, 32 * l + bias_units.index(i) + 1)
                        c0 = 0 if qb < 4 else 512
                        nc.vector.tensor_reduce(small[:, 0, c:c + 1], ps[i % 2][:, c0:T], AX.X, ALU.max, negate=True)\
                            .then_inc(s_mx, 1)
                    if 1 <= i < NU + 1:
                        u = u0 + i - 1
                        c = u % 8
                        dve.wait_ge(s_exp, u + 1)
                        nc.vector.reciprocal(small[:, 2, c:c + 1], small[:, 1, c:c + 1]).then_inc(s_ri, 1)
                        dve.wait_ge(s_ri, u + 1)
                        if i >= 3:
                            dve.wait_ge(s_tr, 2 * (u - 2) + 2)
                        nc.vector.tensor_scalar(inv[:, u % 2, :], ident, small[:, 2, c:c + 1], None, ALU.mult)\
                            .then_inc(s_dg, 1)
                        if i >= 2 and i % 2 == 0 and i + 2 < NU:
                            lower_q(i + 2)
                    if 2 <= i < NU + 2:
                        u = u0 + i - 2
                        dve.wait_ge(s_tr, 2 * u + 2)
                        if i >= 5:
                            dve.wait_ge(s_pv, (u - 3) // 2 + 1)
                        nc.vector.tensor_copy(PT[:, u % 3, 512:T], ps[2][:, 512:T]).then_inc(s_ptb, 1)

                dve.wait_ge(mod_turned, 32 if l == 0 else 48)
                mod_add(l, 16, 48)
                mod_gain(l, 1)
                if l == 0:
                    mod_add(1, 0, 16)
                    mod_gain(1, 0)

                s0 = 2 * SLOT0[l, "merge"]
                nt = ntq

                def lower_y(parts, src, first):
                    for k in range(KD):
                        dve.wait_ge(y_hi, first + k + 1)
                        nc.vector.tensor_tensor(parts[1][:, k, 0:nt], src[:, k, 0:nt], parts[0][:, k, 0:nt].bitcast(fp32),
                                                ALU.subtract).then_inc(y_lo, 1)

                lower_y(YS2, Y, 16 * l)

                def products(i):
                    for j in (1, 3):
                        for half in range(2):
                            s = s0 + 2 * j + half
                            dve.wait_ge(steps, 8 * i + (s + 1))
                            dve.wait_ge(evac["A"], ev("A", s, 8, i))
                            if isinstance(i, int):
                                tile, src, gate = M[:, 2 * i + half, 0:nt], ps[half][:, 0:nt], RAW[:, half, 0:nt]
                                mine = SQ[:, half, 0:nt]
                            else:
                                tile, src = M[:, ds(2 * i + half, 1), 0:nt], ps[half][:, None, 0:nt]
                                gate, mine = RAW[:, half:half + 1, 0:nt], SQ[:, half:half + 1, 0:nt]
                            nc.vector.tensor_tensor(tile if j == 1 else mine, src, gate, ALU.mult).then_inc(evac["V"], 1)
                            if j == 3:
                                dve.wait_ge(evac["V"], ev("V", s, 8, i))
                                nc.vector.tensor_tensor(tile, tile, mine, ALU.add).then_inc(merged, 1)

                products(0)
                with dve.Fori(1, 4) as i:
                    products(i)
                lower_y(MS2, M, 16 * l + 8)

                def update(s, g0, m):
                    dve.wait_ge(steps, s + 1)
                    for kind, (a, b) in enumerate(((0, NL), (NL, nt))):
                        if a == b:
                            continue
                        gate = mod[:, 48 * l + g0 + m, kind:kind + 1]
                        last = nc.vector.scalar_tensor_tensor(out=X[:, m, a:b], in0=ps[s % 2][:, a:b], scalar=gate,
                                                              in1=X[:, m, a:b], op0=ALU.mult, op1=ALU.add)
                    last.then_inc(evac["V"], 1)

                for m in range(8):
                    update(2 * SLOT0[l, "w_o"] + m, 16, m)
                times_rstd(2 * l + 1, nt)

                for hf in range(2):
                    s0 = 2 * SLOT0[l, f"ffn_in{hf}"]
                    done = (2 * l + hf) * KH

                    def hidden(j0, j1, i=0):
                        for j in range(j0, j1):
                            s = s0 + 2 * j + 1
                            dve.wait_ge(steps, 4 * i + (s + 1))
                            dve.wait_ge(evac["A"], ev("A", s, 4, i))
                            g = RAW[:, j % 2, 0:nt]
                            nc.vector.tensor_tensor(g, ps[1][:, 0:nt], g, ALU.mult).then_inc(evac["V"], 1)
                            dve.wait_ge(gs_hi, 2 * i + (done + j + 1))
                            if isinstance(i, int):
                                dst, hi = GS[1][:, j, 0:nt], GS[0][:, j, 0:nt]
                            else:
                                dst, hi = GS[1][:, ds(2 * i + j, 1), 0:nt], GS[0][:, ds(2 * i + j, 1), 0:nt]
                                g = RAW[:, j % 2:j % 2 + 1, 0:nt]
                            nc.vector.tensor_tensor(dst, g, hi.bitcast(fp32), ALU.subtract).then_inc(gs_lo, 1)

                    hidden(0, 3)
                    with dve.Fori(0, (KH - 3) // 2) as i:
                        hidden(3, 5, i)
                    s0 = 2 * SLOT0[l, f"ffn_out{hf}"]
                    for j in range(4):
                        for half in range(2):
                            update(s0 + 4 * j + 2 + half, 40, 2 * j + half)
            rstd(4, NL)
            for k in range(KD):
                nc.vector.scalar_tensor_tensor(out=X[:, k, 0:NL], in0=X[:, k, 0:NL], scalar=vcol("final_norm", k),
                                               in1=ps[2][:, 0:NL], op0=ALU.mult, op1=ALU.mult).then_inc(x_upd, 1)

            links = [0]

            def link(ins):
                links[0] += 1
                ins.then_inc(chain, 1)
                dve.wait_ge(chain, links[0])

            def plain_norm(n, name):
                rstd(n, NL)
                for k in range(KD):
                    nc.vector.scalar_tensor_tensor(out=H[:, k, 0:NL], in0=X[:, k, 0:NL], scalar=vcol(name, k),
                                                   in1=ps[2][:, 0:NL], op0=ALU.mult, op1=ALU.mult).then_inc(h2, 1)

            lam = vcol("lam", 0, 4)
            L = lambda i: lam8[:, i, :]
            nc.vector.scalar_tensor_tensor(out=L(0), in0=lam, scalar=-1.0, in1=lam, op0=ALU.mult, op1=ALU.min)\
                .then_inc(lam_a, 1)
            plain_norm(5, "g_mix")
            for k in range(0, KD, 2):
                dve.wait_ge(p_hi, k + 1)
                nc.vector.tensor_tensor(H2[1][:, k, :], H[:, k, 0:NL], H2[0][:, k, :].bitcast(fp32), ALU.subtract)\
                    .then_inc(p_lov, 1)
            dve.wait_ge(lam_e, 1)
            link(nc.vector.tensor_scalar(L(2), L(1), 2.0, None, ALU.add))
            link(nc.vector.reciprocal(L(3), L(2)))
            link(nc.vector.tensor_tensor(L(2), L(1), L(3), ALU.mult))
            link(nc.vector.tensor_tensor(L(3), L(2), L(2), ALU.mult))
            link(nc.vector.tensor_scalar(L(4), L(3), 1.0 / 17, None, ALU.mult))
            for odd in range(15, 1, -2):
                link(nc.vector.scalar_tensor_tensor(out=L(4), in0=L(4), scalar=1.0 / odd, in1=L(3), op0=ALU.add, op1=ALU.mult))
            link(nc.vector.scalar_tensor_tensor(out=L(4), in0=L(4), scalar=1.0, in1=L(2), op0=ALU.add, op1=ALU.mult))
            link(nc.vector.tensor_scalar(L(5), lam, -1.0, 0.0, ALU.mult, ALU.max))
            link(nc.vector.scalar_tensor_tensor(out=L(5), in0=L(4), scalar=2.0, in1=L(5), op0=ALU.mult, op1=ALU.add))
            link(nc.vector.tensor_scalar(L(6), L(5), 8.0, None, ALU.mult))
            nc.vector.tensor_scalar(L(7), L(5), -8.0, None, ALU.mult).then_inc(r_lam, 1)

            s0 = 2 * SLOT0[2, "w_in2"]
            dve.wait_ge(zeroed, 2)
            for t in range(4):
                s = s0 + 2 * t + 1
                dve.wait_ge(steps, s + 1)
                dve.wait_ge(evac["A"], evacuated("A", s))
                nc.vector.tensor_tensor(UC[:, t, TAPS - 1:TAPS - 1 + NL], ps[1][:, 0:NL], RAW2[:, t % 2, 0:NL], ALU.mult)\
                    .then_inc(evac["V"], 1)
            dve.wait_ge(evac["V"], evacuated("V", s0 + 7))
            mine = [t for t in range(4) if t not in PE_CONV]
            def recurrence_inputs():
                dve.wait_ge(lconv, 4)
                dve.wait_ge(gact, 8)
                for t in range(4):
                    dve.wait_ge(lexp, t + 1)
                    link(nc.vector.tensor_tensor(LH[:, t, :], LA[:, t, :], LA[:, t, :], ALU.mult))
                    nc.vector.scalar_tensor_tensor(out=TH[:, t, :], in0=LH[:, t, :], scalar=1.0, in1=TH[:, t, :],
                                                   op0=ALU.add, op1=ALU.mult).then_inc(lm2, 1)
                    link(nc.vector.tensor_tensor(LU[:, t, :], LU[:, t, :], XR[:, t, :], ALU.mult))

            for d in range(TAPS):
                if d == RECURRENCE_AT:
                    recurrence_inputs()
                for n, t in enumerate(mine):
                    src, w = UC[:, t, d:d + NL], vcol("conv_w", 4 * d + t)
                    if d == 0:
                        ins = nc.vector.tensor_scalar(CV[:, t, :], src, w, vcol("conv_b", t), ALU.mult, ALU.add)
                    else:
                        dve.wait_ge(conv_t, len(mine) * (d - 1) + n + 1)
                        ins = nc.vector.scalar_tensor_tensor(out=CV[:, t, :], in0=src, scalar=w, in1=CV[:, t, :],
                                                             op0=ALU.mult, op1=ALU.add)
                    ins.then_inc(conv_t, 1) if d < TAPS - 1 else ins.then_inc(conv_k, 1)
                if d == SHORT_AT:
                    dve.wait_ge(evac["A"], evacuated("A", s0 + 11))
                    for t in range(4):
                        link(nc.vector.tensor_scalar(XR[:, t, :], XL[:, t, 0:NL], vcol("lru_w", t), vcol("lru_b", t),
                                                     ALU.mult, ALU.add))
                        for e in range(1, LTAPS):
                            ins = nc.vector.scalar_tensor_tensor(out=XR[:, t, :], in0=XL[:, t, e:e + NL],
                                                                 scalar=vcol("lru_w", 4 * e + t), in1=XR[:, t, :],
                                                                 op0=ALU.mult, op1=ALU.add)
                            link(ins) if e < LTAPS - 1 else ins.then_inc(lconv, 1)
            for t in range(4):
                dve.wait_ge(lsq, t + 1)
                link(nc.vector.tensor_tensor(LU[:, t, :], LU[:, t, :], TH[:, t, :], ALU.mult))
                link(nc.vector.tensor_tensor_scan(LH[:, t, :], LA[:, t, :], LU[:, t, :], 0.0, ALU.mult, ALU.add))
                nc.vector.tensor_tensor(LH[:, t, :], LH[:, t, :], GL[:, t, :], ALU.mult).then_inc(ylru, 1)
            dve.wait_ge(lnm, 1)
            for t in range(4):
                nc.vector.scalar_tensor_tensor(out=CV[:, t, :], in0=ps[2][:, 0:NL], scalar=-2.0, in1=CV[:, t, :],
                                               op0=ALU.mult, op1=ALU.add).then_inc(lnc, 1)

            def lower_mix(t, src):
                dve.wait_ge(mix_hi, t + 1)
                nc.vector.tensor_tensor(MIX[1][:, t, :], src, MIX[0][:, t, :].bitcast(fp32), ALU.subtract)\
                    .then_inc(mix_lo, 1)

            for t in range(4):
                lower_mix(t, LH[:, t, :])
            dve.wait_ge(lnr, 1)
            link(nc.vector.reciprocal(RAW2[:, 0, 0:NL], RAW2[:, 0, 0:NL]))
            for t in range(4):
                dve.wait_ge(lns, t + 1)
                nc.vector.tensor_tensor(CV[:, t, :], CV[:, t, :], RAW2[:, 0, 0:NL], ALU.mult).then_inc(lnn, 1)
            for t in range(4):
                lower_mix(4 + t, CV[:, t, :])
            for m in range(KD):
                s = 2 * SLOT0[2, "w_out2"] + m
                dve.wait_ge(steps, s + 1)
                nc.vector.tensor_tensor(X[:, m, 0:NL], ps[s % 2][:, 0:NL], X[:, m, 0:NL], ALU.add).then_inc(evac["V"], 1)
            plain_norm(6, "g_ffn")

            def r3(ap, n):
                return ap.rearrange("p (c n) -> p c n", n=n)

            def over(ap, n):
                return ap[:, :, None].to_broadcast([P, ap.shape[1], n])

            eidx = cst[:, CST["eidx"]:CST["eidx"] + NE]
            LG, EM, EQU = rtile(0, 4, NR), rtile(144, 4, NE), rtile(272, 4, NE)
            CAND, OH1, OH2 = rtile(400, 4, NE), rtile(528, 4, NE), rtile(656, 4, NE)
            g4 = rtile(784, 4, NG4)
            GEQ, GCAND, GHOT, GSH = (rtile(800 + 16 * i, 4, NG4) for i in range(4))
            col4 = [scr[:, 880 + 4 * i:884 + 4 * i] for i in range(8)]
            gmax, gbest, gsum, m1, b1, m2, dif, den = col4

            def hottest(hot, vals, eq, cand, top, best, n):
                link(nc.vector.tensor_reduce(top, vals, AX.X, ALU.max))
                link(nc.vector.tensor_tensor(eq, vals, over(top, n), ALU.is_equal))
                idx = eidx[:, 0:n][:, None, :].to_broadcast([P, 4, n])
                link(nc.vector.scalar_tensor_tensor(out=cand, in0=eq, scalar=100.0, in1=idx, op0=ALU.mult,
                                                    op1=ALU.subtract))
                link(nc.vector.tensor_reduce(best, cand, AX.X, ALU.max))
                link(nc.vector.tensor_tensor(hot, cand, over(best, n), ALU.is_equal))

            dve.wait_ge(rl, 1)
            dve.wait_ge(r_in, 32)
            link(nc.vector.tensor_tensor(LG, r3(ps[3][:, 0:256], 64)[:, :, 0:NR],
                                         rb[:, None, :].to_broadcast([P, 4, NR]), ALU.add))
            link(nc.vector.tensor_copy(g4, LG[:, :, 0:NG4]))
            hottest(GHOT, g4, GEQ, GCAND, gmax, gbest, NG4)
            nc.vector.tensor_tensor(GSH, g4, over(gmax, NG4), ALU.subtract).then_inc(re1, 1)
            link(nc.vector.tensor_scalar(GEQ, GHOT, 1e30, -1e30, ALU.mult, ALU.add))
            for g in range(NG4):
                link(nc.vector.tensor_tensor(EM[:, :, 8 * g:8 * g + 8], LG[:, :, NG4 + 8 * g:NG4 + 8 * g + 8],
                                             GEQ[:, :, g:g + 1].to_broadcast([P, 4, 8]), ALU.add))
            hottest(OH1, EM, EQU, CAND, m1, b1, NE)
            link(nc.vector.scalar_tensor_tensor(out=EM, in0=OH1, scalar=-3e30, in1=EM, op0=ALU.mult, op1=ALU.add))
            hottest(OH2, EM, EQU, CAND, m2, b1, NE)
            mask = r3(SEL[:, 0:128], NE)
            nc.vector.tensor_tensor(mask, OH1, OH2, ALU.add).then_inc(r_mask, 1)
            nc.vector.tensor_tensor(dif, m2, m1, ALU.subtract).then_inc(re1, 1)
            for c in range(4):
                dve.wait_ge(ht, c + 1)
                nc.vector.tensor_copy(htok_half(c, 1), ps[c % 3][:, 512:1024].rearrange("p (a b) -> p a b", a=2))\
                    .then_inc(htk_v, 1)

            dve.wait_ge(re2, 2)
            link(nc.vector.tensor_reduce(gsum, GSH, AX.X, ALU.add))
            link(nc.vector.tensor_scalar(den, dif, 1.0, None, ALU.add))
            link(nc.vector.tensor_tensor(gsum, gsum, den, ALU.mult))
            link(nc.vector.reciprocal(m1, gsum))
            link(nc.vector.tensor_tensor(m2, m1, dif, ALU.mult))
            link(nc.vector.tensor_tensor(OH1, OH1, over(m1, NE), ALU.mult))
            link(nc.vector.tensor_tensor(OH2, OH2, over(m2, NE), ALU.mult))
            link(nc.vector.tensor_tensor(gate[:, :, :], OH1, OH2, ALU.add))
            dve.wait_ge(r_pos, 1)
            link(nc.vector.scalar_tensor_tensor(out=pos[:, :, :], in0=r3(ps[3][:, 0:128], NE), scalar=1.0, in1=mask,
                                                op0=ALU.add, op1=ALU.mult))
            link(nc.vector.tensor_scalar(pos[:, :, :], pos[:, :, :], -1.0, None, ALU.add))
            cnt = scr[:, 912:944]
            link(nc.vector.tensor_copy(cnt, ps[3][:, 128:160]))
            link(nc.vector.tensor_reduce(gmax[:, 0:1], cnt, AX.X, ALU.max))
            passes = scr[:, 944:952]
            link(nc.vector.tensor_scalar(passes, cst[:, CST["iota"]:CST["iota"] + 8], float(CAP), None, ALU.mult))
            link(nc.vector.tensor_tensor(passes, passes, gmax[:, 0:1].to_broadcast([P, 8]), ALU.is_lt))
            link(nc.vector.tensor_reduce(gmax[:, 1:2], passes, AX.X, ALU.add))
            link(nc.vector.tensor_scalar(gmax[:, 2:3], gmax[:, 1:2], float(PAIRS), None, ALU.mult))
            nc.vector.tensor_copy(total_i[:, :], gmax[:, 2:3]).then_inc(r_ok, 1)

            dve.wait_ge(r_ok, 1)
            total = dve.value_load(total_i[0:1, 0:1], min_val=PAIRS, max_val=PAIRS * (NL // CAP))
            iota = cst[:, CST["iota"]:CST["iota"] + CAP]
            sel4 = SEL.rearrange("p (c x n) -> p c x n", c=4, x=2)
            selg4 = SELG.rearrange("p (c x n) -> p c x n", c=4, x=2)
            shape4 = [P, 4, 2, CAP]

            def select(j, first=False):
                two = pos[:, :, ds(2 * j, 2)] if not first else pos[:, :, 0:2]
                wts = gate[:, :, ds(2 * j, 2)] if not first else gate[:, :, 0:2]
                nc.vector.tensor_tensor(sel4, iota[:, None, None, :].to_broadcast(shape4),
                                        two[:, :, :, None].to_broadcast(shape4), ALU.is_equal).then_inc(m_eq, 1)
                return two, wts

            def picks(n):
                dve.wait_ge(m_w, n)
                nc.vector.tensor_scalar(PICK, SELT, 0.0, None, ALU.is_gt).then_inc(m_pick, 1)

            def gathered(n):
                dve.wait_ge(m_xg, 2 * n)
                nc.vector.tensor_copy(scr[:, 512:1024], ps[0][:, 512:1024]).then_inc(m_xgv, 1)

            two, wts = select(0, True)
            dve.wait_ge(m_eq, 1)
            nc.vector.tensor_tensor(selg4, sel4, wts[:, :, :, None].to_broadcast(shape4), ALU.mult).then_inc(m_sel, 1)
            nc.vector.tensor_scalar(two, two, -float(CAP), None, ALU.add).then_inc(m_add, 1)
            def select_next(n):
                dve.wait_ge(m_selt, n)
                two, wts = select(n % PAIRS)
                dve.wait_ge(m_eq, n + 1)
                nc.vector.tensor_tensor(selg4, sel4, wts[:, :, :, None].to_broadcast(shape4), ALU.mult).then_inc(m_sel, 1)
                nc.vector.tensor_scalar(two, two, -float(CAP), None, ALU.add).then_inc(m_dec, 1)

            gathered(1)
            picks(1)
            select_next(1)
            with dve.Fori(0, total) as i:
                dve.wait_ge(m_act, i + 1)
                dve.wait_ge(m_steps, 12 * i + 8)
                nc.vector.tensor_tensor(GH, ps[1][:, 512:1024], SGM, ALU.mult).then_inc(m_g, 1)
                dve.wait_ge(m_ysa, i + 1)
                nc.vector.scalar_tensor_tensor(out=YP[1], in0=ps[2][:, :].rearrange("p (a b) -> p a b", a=2),
                                               scalar=wslot[:, 0:1], in1=YP[0].bitcast(fp32), op0=ALU.mult,
                                               op1=ALU.subtract).then_inc(m_ysv, 1)
                gathered(i + 2)
                for m in range(KD):
                    dve.wait_ge(m_sc, 8 * i + (m + 1))
                    nc.vector.tensor_tensor(X[:, m, 0:NL], ps[0][:, 512 * (m % 2):512 * (m % 2) + 512], X[:, m, 0:NL],
                                            ALU.add).then_inc(m_add, 1)
                picks(i + 2)
                select_next(i + 2)

            dve.wait_ge(m_add, 8 * total + 1)
            plain_norm(7, "g_ple")
            dve.wait_ge(e_rt, 1)
            link(nc.vector.reciprocal(RE, RE))
            dve.wait_ge(e_k, 8)
            for m in range(KD):
                nc.vector.scalar_tensor_tensor(out=EB[:, m, :], in0=EB[:, m, :], scalar=vcol("g_proj", m), in1=RE,
                                               op0=ALU.mult, op1=ALU.mult).then_inc(e_ok, 1)
            for m in range(KD):
                dve.wait_ge(pg_a, m + 1)
                dve.wait_ge(e_ok, m + 1)
                link(nc.vector.tensor_tensor(PG[:, m % 2, :], PG[:, m % 2, :], EB[:, m, :], ALU.mult))
                nc.vector.tensor_tensor(X[:, m, 0:NL], X[:, m, 0:NL], PG[:, m % 2, :], ALU.add).then_inc(x_upd, 1)
            rstd(8, NL)
            for k in range(KD):
                nc.vector.scalar_tensor_tensor(out=X[:, k, 0:NL], in0=X[:, k, 0:NL], scalar=vcol("g_final", k),
                                               in1=ps[2][:, 0:NL], op0=ALU.mult, op1=ALU.mult).then_inc(x_upd, 1)


def slots(w):
    k, n = w.shape
    return w.reshape(k // P, P, n // 256, 256).transpose(2, 1, 0, 3).reshape(n // 256, P, -1)


def lay_out(x):
    f = np.float32
    z = np.zeros((N_STREAM, P, SLOT), f)

    def put(l, name, blocks):
        n = SLOT0[l, name]
        for b in blocks:
            z[n:n + b.shape[0], :, :b.shape[2]] = b
            n += b.shape[0]

    for l in range(LAYERS):
        wm, w = x["w_mod"][l], x["w_in"][l]
        if l == 0:
            put(0, "mod_head", [slots(wm[:, :2048])])
            put(0, "mod_rest", [slots(wm[:, 2048:]), slots(x["w_mod"][1][:, :2048])])
        else:
            put(1, "mod_rest", [slots(wm[:, 2048:])])
        naq, nak, nav, gq, gk, gv, ga, gb = np.split(w, np.cumsum([512, 512, 512, 512, 128, 128, 1024]), axis=1)
        order = [h for t in range(4) for h in (t, t + 4)]
        gq = gq.reshape(D, 8, HD)[:, order].reshape(D, 512)
        put(l, "gq", [slots(gq)])
        put(l, "gkv", [slots(np.concatenate([gk, gv], axis=1))])
        put(l, "nak", [slots(nak)])
        put(l, "naq", [slots(naq)])
        put(l, "nav", [slots(nav)])
        ga, gb, pa = slots(ga), slots(gb), slots(x["w_pa"][l])
        pb = slots(x["w_pb"][l].reshape(8, HD, D)[order].reshape(512, D))
        put(l, "merge", [b[j:j + 1] for j in range(4) for b in (ga, pa, gb, pb)])
        put(l, "w_o", [slots(x["w_o"][l])])
        wf = x["w_ffn_in"][l].reshape(D, 2, KF, P).transpose(0, 2, 1, 3).reshape(D, KF * 256)
        wo = x["w_ffn_out"][l].reshape(2, KH * P, D)
        for hf in range(2):
            put(l, f"ffn_in{hf}", [slots(wf)[hf * KH:(hf + 1) * KH]])
            put(l, f"ffn_out{hf}", [slots(rows[:, 256 * j:256 * j + 256]) for j in range(4)
                                    for rows in np.split(wo[hf], [FFQ[0] * P])])

    v = np.zeros((P, NV), f)

    def col(name, a):
        a = np.asarray(a).reshape(-1, P).T
        v[:, VEC[name]:VEC[name] + a.shape[1]] = a

    v[:, VEC["c2"]:VEC["c2"] + 16:2] = x["c"].reshape(KD, P).T
    v[:, VEC["c2"] + 1:VEC["c2"] + 16:2] = x["c_ctx"].reshape(KD, P).T
    for l in range(LAYERS):
        for name in ("norm1", "norm2", "b_mod"):
            col(f"{name}{l}", x[name][l])
        for name in ("q_gain", "k_gain"):
            col(f"{name}{l}", np.tile(x[name][l], 2))
    col("final_norm", x["final_norm"])

    for name, src in (("g_mix", "g_mix"), ("conv_b", "conv_dw_b"), ("ln_g", "conv_ln_g"), ("ln_b", "conv_ln_b"),
                      ("conv_w", "conv_dw_w"), ("lru_w", "lru_conv_w"), ("lru_b", "lru_conv_b"), ("b_r", "lru_b_r"),
                      ("b_i", "lru_b_i"), ("lam", "lru_lambda"), ("g_ffn", "g_ffn"), ("g_ple", "g_ple"),
                      ("g_proj", "g_ple_proj")):
        col(name, x[src + "_2"][0])
    col("g_final", x["g_final_2"])

    w = x["w_in_2"][0].reshape(D, 4, 4, P)
    put(2, "w_in2", [slots(np.stack([w[:, 1], w[:, 0]], axis=2).reshape(D, D)), slots(w[:, 2:].reshape(D, D))])
    put(2, "w_out2", [slots(np.roll(x["w_out_2"][0], D // 2, axis=0))])

    def chunks(w, rows, per):
        w = w.reshape(PAIRS, 2, rows // P // per, per, P, -1).transpose(0, 2, 1, 4, 3, 5)
        return w.reshape(PAIRS, -1, P, SLOT)

    experts = np.concatenate([chunks(x["w1_2"][0], D, 4), chunks(x["w3_2"][0], D, 4), chunks(x["w2_2"][0], D // 2, 2)],
                             axis=1)
    router = np.concatenate([x["w_group_2"][0], x["w_expert_2"][0]], axis=1)
    router = router.reshape(KD, P, NR).transpose(1, 0, 2).reshape(P, KD * NR)
    router_b = np.concatenate([x["b_group_2"][0], x["b_expert_2"][0]])[None].repeat(P, axis=0)

    def by_rows(a):
        return a.reshape(-1, P, a.shape[-1]).transpose(1, 0, 2).reshape(P, -1)

    pad = np.zeros((LAYERS, 8, 15, 128), f)
    pad[..., 48:79] = x["na_rpb"]
    return {"stream": z, "vecs": v, "consts": constants(), "xT": np.ascontiguousarray(x["x"][0].T),
            "ctxT": np.ascontiguousarray(x["ctx"][0].T), "rpb": pad, "experts": experts,
            "router": router, "router_b": router_b, "lru_w": np.concatenate([x["lru_w_r_2"], x["lru_w_i_2"]]),
            "w_ple": by_rows(x["w_ple_2"][0]), "pT": by_rows(x["p_2"][0, 0].T), "w_gate": slots(x["w_ple_gate_2"][0])}


def constants():
    f = np.float32
    c = np.zeros((P, NCST), f)
    i = np.arange(P)
    c[:, 0:128] = np.eye(P)
    c[:, 128:256] = 1.0 / D
    c[:, 256:384] = (i[:, None] // HD == i[None, :] // HD) / HD
    c[i[1::2], 384 + i[0::2]] = -1
    c[i[0::2], 384 + i[1::2]] = 1
    t = np.arange(NL)
    half = HD // 2
    inv = (f(10000.0) ** (-np.arange(0, half, 2, dtype=f) / f(half))).astype(f)
    ang = np.concatenate([(t // GRID).astype(f)[:, None] * inv, (t % GRID).astype(f)[:, None] * inv], axis=1)
    pair = (i % HD) // 2
    c[:, CST["cos"]:CST["cos"] + NL] = np.cos(ang).T[pair]
    c[:, CST["sin"]:CST["sin"] + NL] = np.sin(ang).T[pair]
    w = i % GRID
    u = np.arange(GRID)
    start = np.clip(w - 8, 0, GRID - 16)[:, None]
    c[:, CST["namask"]:CST["namask"] + GRID] = np.where((u >= start) & (u < start + 16), 0, -1e30)
    c[:, CST["iota"]:CST["iota"] + HD] = u
    c[:, CST["one"]:CST["one"] + P] = 1
    c[:, CST["eidx"]:CST["eidx"] + NR] = np.arange(NR)
    for j in range(2):
        c[j::32, CST["fold"] + j] = 1
    c[:, CST["tri"]:CST["tri"] + P] = i[:, None] < i[None, :]
    return c


def kernel(**inputs):
    import concourse.bacc as bacc
    from concourse.bass_utils import run_bass_kernel_spmd

    nc = bacc.Bacc("TRN2", target_bir_lowering=False, num_devices=1)
    arrays = lay_out({k: np.asarray(a) for k, a in inputs.items()})
    fp32 = mybir.dt.float32
    aps = {n: nc.dram_tensor(n, a.shape, fp32, kind="ExternalInput").ap() for n, a in arrays.items()}
    outT = nc.dram_tensor("outT", (D, NL), fp32, kind="ExternalOutput").ap()
    build(nc, out=outT, **aps)
    r = run_bass_kernel_spmd(nc, [arrays], core_ids=[0])
    return np.ascontiguousarray(r.results[0]["outT"].T)[None]
```
